# Optimizing a Trainium2 kernel written in Bass

```python
import math
import jax
import jax.numpy as jnp
from jax import lax
import numpy as np

D_MODEL = 2048
BATCH = 1
SEQ = 512
DEPTH = 2
DEC_BATCH = 8
DEC_SEQ = 1
PAST_LEN = 2048
PAGE_SIZE = 128

HEAD_DIM = 128
H_A = D_MODEL // (2 * HEAD_DIM)
G_A = 2
R_A = H_A // G_A
CMP_BLOCK = 32
CMP_HID = 256
SEL_BLOCK = 64
N_SEL = 16
WINDOW = 512
H_B = D_MODEL // (2 * HEAD_DIM)
G_B = 2
R_B = H_B // G_B
H_IDX = 16
D_IDX = 128
TOPK_MAX = 256
D_CONV = D_MODEL
CONV_W = 3
N_BUCKETS = 32
REL_MAX_DIST = 1024
Q_BLOCK = 128
RMS_EPS = 1e-6
NEG = -1e30
SEL_FORCE = 1e4
N_ATT = (DEPTH + 1) // 2
N_CONV = DEPTH // 2
ATT_SPLIT = (H_A * HEAD_DIM,) + (G_A * HEAD_DIM,) * 6 + (3 * H_A, H_A * HEAD_DIM, H_B * HEAD_DIM, G_B * HEAD_DIM, G_B * HEAD_DIM, H_IDX * D_IDX, H_IDX, D_IDX, H_B * HEAD_DIM)
P_ATT = sum(ATT_SPLIT)
D_ATT_OUT = (H_A + H_B) * HEAD_DIM

kernel_name = 'hybrid_nsa_dsa_shortconv_decoder_step'

def rms_norm(x, g):
    x32 = x.astype(jnp.float32)
    y = x32 * lax.rsqrt(jnp.mean(x32 * x32, axis=-1, keepdims=True) + RMS_EPS)
    return (y * g.astype(jnp.float32)).astype(x.dtype)

def modulate(x, g, shift, scale):
    return rms_norm(x, g) * (1 + scale[:, None, :]) + shift[:, None, :]

def rel_bucket(n):
    n = jnp.maximum(n, 0)
    max_exact = N_BUCKETS // 2
    nf = jnp.maximum(n, max_exact).astype(jnp.float32)
    large = max_exact + (jnp.log(nf / max_exact) / math.log(REL_MAX_DIST / max_exact) * (N_BUCKETS - max_exact)).astype(jnp.int32)
    large = jnp.minimum(large, N_BUCKETS - 1)
    return jnp.where(n < max_exact, n, large)

def masked_softmax(logits, mask):
    logits = jnp.where(mask, logits, NEG)
    m = jnp.max(logits, axis=-1, keepdims=True)
    p = jnp.where(mask, jnp.exp(logits - m), 0.0)
    return p / jnp.maximum(jnp.sum(p, axis=-1, keepdims=True), 1e-30)

def dense_attention(q, t, k, v, s, tbl, window):
    logits = jnp.einsum('bqgrd,bngd->bqgrn', q, k, preferred_element_type=jnp.float32) * (q.shape[-1] ** -0.5)
    n = t[:, None] - s[None, :]
    bias = jnp.transpose(tbl[rel_bucket(n)], (0, 2, 3, 1))[None]
    mask = n >= 0
    if window is not None:
        mask = mask & (n <= window) & (s >= 0)[None, :]
    p = masked_softmax(logits + bias, mask[None, :, None, None, :])
    out = jnp.einsum('bqgrn,bngd->bqgrd', p.astype(v.dtype), v)
    return out, p

def gathered_attention(q, t, kg, vg, s, tbl):
    logits = jnp.einsum('bqgrd,bqgnd->bqgrn', q, kg, preferred_element_type=jnp.float32) * (q.shape[-1] ** -0.5)
    n = t[None, :, None, None] - s
    g_idx = jnp.arange(tbl.shape[1])[None, None, :, None]
    bias = jnp.transpose(tbl, (1, 0, 2))[g_idx, rel_bucket(n)]
    p = masked_softmax(logits + jnp.moveaxis(bias, -1, 3), (n >= 0)[:, :, :, None, :])
    return jnp.einsum('bqgrn,bqgnd->bqgrd', p.astype(vg.dtype), vg)

def compress(kr, pe, w1, w2, nb):
    b, _, g, d = kr.shape
    blk = kr[:, :nb * CMP_BLOCK].reshape(b, nb, CMP_BLOCK, g, d) + pe[None, None, :, None, :]
    blk = jnp.transpose(blk, (0, 1, 3, 2, 4)).reshape(b, nb, g, CMP_BLOCK * d)
    return jax.nn.silu(blk @ w1) @ w2

def nsa_select(p_cmp, t, n_sel_blocks, n_select):
    ratio = SEL_BLOCK // CMP_BLOCK
    p = jnp.sum(p_cmp, axis=3)
    b, q, g, nb = p.shape
    p = jnp.pad(p, ((0, 0), (0, 0), (0, 0), (0, n_sel_blocks * ratio - nb)))
    p = p.reshape(b, q, g, n_sel_blocks, ratio).sum(-1)
    j = jnp.arange(n_sel_blocks)[None, :]
    cur = (t // SEL_BLOCK)[:, None]
    forced = ((j == 0) | (j == cur) | (j == cur - 1)).astype(jnp.float32)
    score = jnp.where((j <= cur)[None, :, None, :], p + SEL_FORCE * forced[None, :, None, :], NEG)
    return lax.top_k(score, n_select)[1]

def dsa_select(qi, wi, kidx, t, topk):
    dots = jnp.einsum('bqhd,bld->bqhl', qi, kidx, preferred_element_type=jnp.float32) * (D_IDX ** -0.5)
    score = jnp.einsum('bqh,bqhl->bql', wi.astype(jnp.float32), jax.nn.relu(dots))
    s = jnp.arange(kidx.shape[1])
    score = jnp.where(s[None, None, :] <= t[None, :, None], score, NEG)
    return lax.top_k(score, topk)[1]

def gather_pages(pool, page_table):
    bd, npg = page_table.shape
    return pool[page_table].reshape((bd, npg * pool.shape[1]) + pool.shape[2:])

def gather_rows(pool, page_table, new, s, g):
    ps = pool.shape[1]
    past = page_table.shape[1] * ps
    bd = s.shape[0]
    b_idx = jnp.arange(bd).reshape((bd,) + (1,) * (s.ndim - 1))
    sp = jnp.clip(s, 0, past - 1)
    page = page_table[b_idx, sp // ps]
    from_pool = pool[page, sp % ps, g]
    sn = jnp.clip(s - past, 0, new.shape[1] - 1)
    from_new = new[b_idx, sn, g]
    return jnp.where((s >= past)[..., None], from_new, from_pool)

def att_project(h, w_in):
    b, t, _ = h.shape
    proj = h @ w_in
    parts = []
    start = 0
    for size in ATT_SPLIT:
        parts.append(proj[..., start:start + size])
        start += size
    qa, kc, vc, ks, vs, kw, vw, ga, za, qb, kb, vb, qi, wi, ki, zb = parts
    qa = qa.reshape(b, t, G_A, R_A, HEAD_DIM)
    kc, vc, ks, vs, kw, vw = [a.reshape(b, t, G_A, HEAD_DIM) for a in (kc, vc, ks, vs, kw, vw)]
    ga = jax.nn.sigmoid(ga).reshape(b, t, G_A, R_A, 3)
    qb = qb.reshape(b, t, G_B, R_B, HEAD_DIM)
    kb = kb.reshape(b, t, G_B, HEAD_DIM)
    vb = vb.reshape(b, t, G_B, HEAD_DIM)
    qi = qi.reshape(b, t, H_IDX, D_IDX)
    wi = wi * (H_IDX ** -0.5)
    return qa, kc, vc, ks, vs, kw, vw, ga, za, qb, kb, vb, qi, wi, ki, zb

def split_bias(rel_bias):
    return (rel_bias[:, :H_A].reshape(N_BUCKETS, G_A, R_A), rel_bias[:, H_A:].reshape(N_BUCKETS, G_B, R_B))

def att_merge(ga, za, zb, o_cmp, o_slc, o_win, o_b, w_out):
    b, t = za.shape[:2]
    o_a = ga[..., 0:1] * o_cmp + ga[..., 1:2] * o_slc + ga[..., 2:3] * o_win
    o_a = o_a.reshape(b, t, -1) * jax.nn.silu(za)
    o_b = o_b.reshape(b, t, -1) * jax.nn.silu(zb)
    return jnp.concatenate([o_a, o_b], axis=-1) @ w_out

def att_prompt(h, w_in, w_out, cmpw, rel_bias):
    b, t_len, _ = h.shape
    qa, kc, vc, ks, vs, kw, vw, ga, za, qb, kb, vb, qi, wi, ki, zb = att_project(h, w_in)
    tbl_a, tbl_b = split_bias(rel_bias)
    t = jnp.arange(t_len)
    nb = t_len // CMP_BLOCK
    k_cmp = compress(kc, cmpw[0], cmpw[1], cmpw[2], nb)
    v_cmp = compress(vc, cmpw[3], cmpw[4], cmpw[5], nb)
    o_cmp, p_cmp = dense_attention(qa, t, k_cmp, v_cmp, jnp.arange(nb) * CMP_BLOCK + CMP_BLOCK - 1, tbl_a, None)
    n_sel_blocks = -(-t_len // SEL_BLOCK)
    sel = nsa_select(p_cmp, t, n_sel_blocks, min(N_SEL, n_sel_blocks))
    topk = min(TOPK_MAX, t_len // 4)
    kw_pad = jnp.concatenate([jnp.zeros((b, WINDOW, G_A, HEAD_DIM), kw.dtype), kw], axis=1)
    vw_pad = jnp.concatenate([jnp.zeros((b, WINDOW, G_A, HEAD_DIM), vw.dtype), vw], axis=1)
    n_chunks = t_len // Q_BLOCK
    b_a = jnp.arange(b)[:, None, None, None]
    g_a = jnp.arange(G_A)[None, None, :, None]
    b_b = jnp.arange(b)[:, None, None]

    def to_chunks(a):
        return jnp.moveaxis(a.reshape((b, n_chunks, Q_BLOCK) + a.shape[2:]), 1, 0)

    def from_chunks(a):
        return jnp.moveaxis(a, 0, 1).reshape((b, t_len) + a.shape[3:])

    def block(xs):
        ci, qa_c, sel_c, qb_c, qi_c, wi_c = xs
        t_c = ci * Q_BLOCK + jnp.arange(Q_BLOCK)
        s = (sel_c[..., None] * SEL_BLOCK + jnp.arange(SEL_BLOCK)).reshape(b, Q_BLOCK, G_A, -1)
        sc = jnp.minimum(s, t_len - 1)
        o_slc = gathered_attention(qa_c, t_c, ks[b_a, sc, g_a], vs[b_a, sc, g_a], s, tbl_a)
        s_w = ci * Q_BLOCK - WINDOW + jnp.arange(WINDOW + Q_BLOCK)
        k_w = lax.dynamic_slice_in_dim(kw_pad, ci * Q_BLOCK, WINDOW + Q_BLOCK, axis=1)
        v_w = lax.dynamic_slice_in_dim(vw_pad, ci * Q_BLOCK, WINDOW + Q_BLOCK, axis=1)
        o_win, _ = dense_attention(qa_c, t_c, k_w, v_w, s_w, tbl_a, WINDOW)
        idx = dsa_select(qi_c, wi_c, ki, t_c, topk)
        s_b = jnp.broadcast_to(idx[:, :, None, :], (b, Q_BLOCK, G_B, topk))
        o_b = gathered_attention(qb_c, t_c, jnp.swapaxes(kb[b_b, idx], 2, 3), jnp.swapaxes(vb[b_b, idx], 2, 3), s_b, tbl_b)
        return o_slc, o_win, o_b

    o_slc, o_win, o_b = lax.map(block, (jnp.arange(n_chunks), to_chunks(qa), to_chunks(sel), to_chunks(qb), to_chunks(qi), to_chunks(wi)))
    out = att_merge(ga, za, zb, o_cmp, from_chunks(o_slc), from_chunks(o_win), from_chunks(o_b), w_out)
    n_win = min(WINDOW, t_len)
    return out, (kc, vc, ks, vs, kw[:, t_len - n_win:], vw[:, t_len - n_win:], kb, vb, ki)

def att_sample(h, c_cmp_k, c_cmp_v, c_slc_k, c_slc_v, s_win_k, s_win_v, c_dsa_k, c_dsa_v, c_idx_k, page_table, w_in, w_out, cmpw, rel_bias):
    bd, tn, _ = h.shape
    qa, kc, vc, ks, vs, kw, vw, ga, za, qb, kb, vb, qi, wi, ki, zb = att_project(h, w_in)
    tbl_a, tbl_b = split_bias(rel_bias)
    past = page_table.shape[1] * c_cmp_k.shape[1]
    l_tot = past + tn
    t = past + jnp.arange(tn)
    kc_all = jnp.concatenate([gather_pages(c_cmp_k, page_table), kc], axis=1)
    vc_all = jnp.concatenate([gather_pages(c_cmp_v, page_table), vc], axis=1)
    nb = l_tot // CMP_BLOCK
    k_cmp = compress(kc_all, cmpw[0], cmpw[1], cmpw[2], nb)
    v_cmp = compress(vc_all, cmpw[3], cmpw[4], cmpw[5], nb)
    o_cmp, p_cmp = dense_attention(qa, t, k_cmp, v_cmp, jnp.arange(nb) * CMP_BLOCK + CMP_BLOCK - 1, tbl_a, None)
    n_sel_blocks = -(-l_tot // SEL_BLOCK)
    sel = nsa_select(p_cmp, t, n_sel_blocks, min(N_SEL, n_sel_blocks))
    s = (sel[..., None] * SEL_BLOCK + jnp.arange(SEL_BLOCK)).reshape(bd, tn, G_A, -1)
    g_a = jnp.arange(G_A)[None, None, :, None]
    o_slc = gathered_attention(qa, t, gather_rows(c_slc_k, page_table, ks, s, g_a), gather_rows(c_slc_v, page_table, vs, s, g_a), s, tbl_a)
    wb = s_win_k.shape[1]
    k_w = jnp.concatenate([s_win_k, kw], axis=1)
    v_w = jnp.concatenate([s_win_v, vw], axis=1)
    s_w = past - wb + jnp.arange(wb + tn)
    o_win, _ = dense_attention(qa, t, k_w, v_w, s_w, tbl_a, WINDOW)
    ki_all = jnp.concatenate([gather_pages(c_idx_k, page_table), ki], axis=1)
    topk = min(TOPK_MAX, l_tot // 4)
    idx = dsa_select(qi, wi, ki_all, t, topk)
    g_b = jnp.arange(G_B)
    k_b = jnp.swapaxes(gather_rows(c_dsa_k, page_table, kb, idx[..., None], g_b), 2, 3)
    v_b = jnp.swapaxes(gather_rows(c_dsa_v, page_table, vb, idx[..., None], g_b), 2, 3)
    s_b = jnp.broadcast_to(idx[:, :, None, :], (bd, tn, G_B, topk))
    o_b = gathered_attention(qb, t, k_b, v_b, s_b, tbl_b)
    out = att_merge(ga, za, zb, o_cmp, o_slc, o_win, o_b, w_out)
    return out, (kc, vc, ks, vs, k_w[:, tn:], v_w[:, tn:], kb, vb, ki)

def conv_mixer(h, state, w_in, conv_w, conv_b, w_out):
    hh, bg, cg, z = jnp.split(h @ w_in, 4, axis=-1)
    u = cg * hh
    u_pad = jnp.concatenate([state.astype(u.dtype), u], axis=1)
    t = u.shape[1]
    y = conv_b + conv_w[0] * u_pad[:, 0:t]
    for k in range(1, CONV_W):
        y = y + conv_w[k] * u_pad[:, k:k + t]
    out = (jax.nn.silu(z) * bg * y) @ w_out
    return out, u_pad[:, t:]

def setup_inputs(seed: int = 0) -> dict:
    key = jax.random.key(seed)
    ks = jax.random.split(key, 40)
    n_pages = PAST_LEN // PAGE_SIZE
    n_used = DEC_BATCH * n_pages
    n_pool = n_used + n_used // 4
    win_buf = min(WINDOW, PAST_LEN)

    def nrm(k, shape, scale=1.0):
        return scale * jax.random.normal(k, shape, jnp.float32)

    page_table = jax.random.permutation(ks[0], n_pool)[:n_used].reshape(DEC_BATCH, n_pages).astype(jnp.int32)
    return {
        'x_prompt': nrm(ks[1], (BATCH, SEQ, D_MODEL)),
        'x_sample': nrm(ks[2], (DEC_BATCH, DEC_SEQ, D_MODEL)),
        'cache_nsa_cmp_k': nrm(ks[3], (N_ATT, n_pool, PAGE_SIZE, G_A, HEAD_DIM)),
        'cache_nsa_cmp_v': nrm(ks[4], (N_ATT, n_pool, PAGE_SIZE, G_A, HEAD_DIM)),
        'cache_nsa_slc_k': nrm(ks[5], (N_ATT, n_pool, PAGE_SIZE, G_A, HEAD_DIM)),
        'cache_nsa_slc_v': nrm(ks[6], (N_ATT, n_pool, PAGE_SIZE, G_A, HEAD_DIM)),
        'state_nsa_win_k': nrm(ks[7], (N_ATT, DEC_BATCH, win_buf, G_A, HEAD_DIM)),
        'state_nsa_win_v': nrm(ks[8], (N_ATT, DEC_BATCH, win_buf, G_A, HEAD_DIM)),
        'cache_dsa_k': nrm(ks[9], (N_ATT, n_pool, PAGE_SIZE, G_B, HEAD_DIM)),
        'cache_dsa_v': nrm(ks[10], (N_ATT, n_pool, PAGE_SIZE, G_B, HEAD_DIM)),
        'cache_dsa_idx_k': nrm(ks[11], (N_ATT, n_pool, PAGE_SIZE, D_IDX)),
        'state_conv': nrm(ks[12], (N_CONV, DEC_BATCH, CONV_W - 1, D_CONV)),
        'page_table': page_table,
        'c_prompt': nrm(ks[13], (BATCH, D_MODEL)),
        'c_sample': nrm(ks[14], (DEC_BATCH, D_MODEL)),
        'w_ada': nrm(ks[15], (DEPTH, D_MODEL, 3 * D_MODEL), 0.5 * D_MODEL ** -0.5),
        'b_ada': nrm(ks[16], (DEPTH, 3 * D_MODEL), 0.02),
        'norm_g': 1.0 + nrm(ks[17], (DEPTH, D_MODEL), 0.05),
        'rel_bias': nrm(ks[18], (N_BUCKETS, H_A + H_B), 0.5),
        'w_in_att': nrm(ks[19], (N_ATT, D_MODEL, P_ATT), D_MODEL ** -0.5),
        'w_out_att': nrm(ks[20], (N_ATT, D_ATT_OUT, D_MODEL), D_ATT_OUT ** -0.5),
        'cmp_pe_k': nrm(ks[21], (N_ATT, CMP_BLOCK, HEAD_DIM), 0.1),
        'cmp_w1_k': nrm(ks[22], (N_ATT, CMP_BLOCK * HEAD_DIM, CMP_HID), (CMP_BLOCK * HEAD_DIM) ** -0.5),
        'cmp_w2_k': nrm(ks[23], (N_ATT, CMP_HID, HEAD_DIM), CMP_HID ** -0.5),
        'cmp_pe_v': nrm(ks[24], (N_ATT, CMP_BLOCK, HEAD_DIM), 0.1),
        'cmp_w1_v': nrm(ks[25], (N_ATT, CMP_BLOCK * HEAD_DIM, CMP_HID), (CMP_BLOCK * HEAD_DIM) ** -0.5),
        'cmp_w2_v': nrm(ks[26], (N_ATT, CMP_HID, HEAD_DIM), CMP_HID ** -0.5),
        'w_in_conv': nrm(ks[27], (N_CONV, D_MODEL, 4 * D_CONV), D_MODEL ** -0.5),
        'conv_w': nrm(ks[28], (N_CONV, CONV_W, D_CONV), CONV_W ** -0.5),
        'conv_b': nrm(ks[29], (N_CONV, D_CONV), 0.02),
        'w_out_conv': nrm(ks[30], (N_CONV, D_CONV, D_MODEL), D_CONV ** -0.5),
        'final_norm_g': 1.0 + nrm(ks[31], (D_MODEL,), 0.05),
    }

def reference(x_prompt, x_sample, cache_nsa_cmp_k, cache_nsa_cmp_v, cache_nsa_slc_k, cache_nsa_slc_v, state_nsa_win_k, state_nsa_win_v, cache_dsa_k, cache_dsa_v, cache_dsa_idx_k, state_conv, page_table, c_prompt, c_sample, w_ada, b_ada, norm_g, rel_bias, w_in_att, w_out_att, cmp_pe_k, cmp_w1_k, cmp_w2_k, cmp_pe_v, cmp_w1_v, cmp_w2_v, w_in_conv, conv_w, conv_b, w_out_conv, final_norm_g):
    yp, ys = x_prompt, x_sample
    att_p, att_s, conv_p, conv_s = [], [], [], []
    for layer in range(DEPTH):
        i = layer // 2
        sh_p, sc_p, gt_p = jnp.split(c_prompt @ w_ada[layer] + b_ada[layer], 3, axis=-1)
        sh_s, sc_s, gt_s = jnp.split(c_sample @ w_ada[layer] + b_ada[layer], 3, axis=-1)
        hp = modulate(yp, norm_g[layer], sh_p, sc_p)
        hs = modulate(ys, norm_g[layer], sh_s, sc_s)
        if layer % 2 == 0:
            cmpw = (cmp_pe_k[i], cmp_w1_k[i], cmp_w2_k[i], cmp_pe_v[i], cmp_w1_v[i], cmp_w2_v[i])
            op, st = att_prompt(hp, w_in_att[i], w_out_att[i], cmpw, rel_bias)
            att_p.append(st)
            osm, st = att_sample(hs, cache_nsa_cmp_k[i], cache_nsa_cmp_v[i], cache_nsa_slc_k[i], cache_nsa_slc_v[i], state_nsa_win_k[i], state_nsa_win_v[i], cache_dsa_k[i], cache_dsa_v[i], cache_dsa_idx_k[i], page_table, w_in_att[i], w_out_att[i], cmpw, rel_bias)
            att_s.append(st)
        else:
            op, st = conv_mixer(hp, jnp.zeros((hp.shape[0], CONV_W - 1, D_CONV), hp.dtype), w_in_conv[i], conv_w[i], conv_b[i], w_out_conv[i])
            conv_p.append(st)
            osm, st = conv_mixer(hs, state_conv[i], w_in_conv[i], conv_w[i], conv_b[i], w_out_conv[i])
            conv_s.append(st)
        yp = yp + gt_p[:, None, :] * op
        ys = ys + gt_s[:, None, :] * osm
    y_prompt = rms_norm(yp, final_norm_g)
    y_sample = rms_norm(ys, final_norm_g)
    cmp_k_p, cmp_v_p, slc_k_p, slc_v_p, win_k_p, win_v_p, dsa_k_p, dsa_v_p, idx_k_p = [jnp.stack(z) for z in zip(*att_p)]
    cmp_k_s, cmp_v_s, slc_k_s, slc_v_s, win_k_s, win_v_s, dsa_k_s, dsa_v_s, idx_k_s = [jnp.stack(z) for z in zip(*att_s)]
    conv_new_p = jnp.stack(conv_p)
    conv_new_s = jnp.stack(conv_s)
    return (y_prompt, y_sample, cmp_k_p, cmp_k_s, cmp_v_p, cmp_v_s, slc_k_p, slc_k_s, slc_v_p, slc_v_s, win_k_p, win_k_s, win_v_p, win_v_s, dsa_k_p, dsa_k_s, dsa_v_p, dsa_v_s, idx_k_p, idx_k_s, conv_new_p, conv_new_s)


_drawn_inputs = setup_inputs


def setup_inputs(seed=0):
    import zlib

    import numpy as np

    out = dict(_drawn_inputs(seed))
    spreads = {}
    factors = {'cache_nsa_cmp_k': 4.538,
     'cache_nsa_cmp_v': 3.415,
     'cache_nsa_slc_k': 5.37,
     'cache_nsa_slc_v': 4.661,
     'cmp_pe_k': 8.0,
     'cmp_pe_v': 4.664,
     'conv_b': 6.837}
    for name, (base, spread) in spreads.items():
        noise = np.random.default_rng([zlib.crc32(name.encode()), seed]).standard_normal(out[name].shape)
        drawn = base * np.exp(spread * noise) if base else spread * noise
        out[name] = jnp.asarray(drawn.astype(out[name].dtype))
    for name, factor in factors.items():
        out[name] = (out[name] * factor).astype(out[name].dtype)
    return out
```

```python
from contextlib import ExitStack, contextmanager

import concourse.bass as bass
from concourse import mybir

F32 = mybir.dt.float32
F32R = mybir.dt.float32r
I32 = mybir.dt.int32
ALU = mybir.AluOpType
ACT = mybir.ActivationFunctionType
AX = mybir.AxisListType.X

P = 128
D = 2048
KT = D // P
T = 512
TT = T // P
NS = 8
TC = T + NS
HC = TC // 2
C9 = 1 + NS
G = 2
NH = 8
NI = 16
PAST = 2048
PG = 16
NPOOL = 160
WIN = 512
CB = 32
NCB = PAST // CB
CH = 256
TOPK_P = 128
TOPK_S = 256
NEG = -1e30
TAKEN = -3e38
SCALE = P ** -0.5
EPS = 1e-6

RUNS = [(0, 0, 20), (20, 2584, 36), (56, 7208, 9)]
QA, KC, VC, KS, VS, KW, VW, ZA, QB, KB, VB, QI, KI, ZB, GW = 0, 8, 10, 12, 14, 16, 18, 20, 28, 36, 38, 40, 56, 57, 65
NTILES = 66
GA_COL, WI_COL = 2560, 7192
NGA, NGW = 24, 40
WI_ROW = P - NI

C_ID, C_BD8, C_R16, C_BD16, C_END = 0, 128, 136, 152, 160
C_E8 = C_END + 64
C_RT = C_END
C_ALL = C_E8 + 64
O_P, O_S, O_C, O_ALL = 0, 512, 512 + 2049, 512 + 2049 + 64

BREV = 640


class Kernel:

    def __init__(self, nc, ctx, ins, outs):
        self.nc, self.ctx, self.i, self.o = nc, ctx, ins, outs
        self.stages, self.stage_sems = 0, []
        self.psum = ctx.enter_context(nc.psum_tensor("psum", [P, 8, 512], F32))

    def sb(self, name, shape, dt=F32, ctx=None):
        return (ctx or self.ctx).enter_context(self.nc.sbuf_tensor(name, shape, dt))

    def sem(self, name):
        handle = self.nc.alloc_semaphore(name=f"{name}_{self.stages}")
        if self.stages:
            self.stage_sems.append(handle)
        return handle

    @contextmanager
    def stage(self):
        self.stages += 1
        self.stage_sems = []
        yield
        numbers = sorted(s.num for s in self.stage_sems)
        while numbers:
            n = next((i for i in range(1, len(numbers)) if numbers[i] != numbers[0] + i), len(numbers))
            self.nc.gpsimd.sem_clear(range(numbers[0], numbers[0] + n))
            numbers = numbers[n:]
        for s in self.stage_sems:
            self.nc.release_semaphore(s)
        self.nc.all_engine_barrier()

    def split_buffers(self, tag, ctx):
        self.hh, self.hl = (self.sb(f"{n}{tag}", [P, KT, TC], F32R, ctx) for n in ("h_high", "h_low"))
        self.wh, self.wl = (self.sb(f"{n}{tag}", [P, 2, KT * P], F32R, ctx) for n in ("w_high", "w_low"))

    def dram(self, name, shape):
        return self.nc.dram_tensor(name, shape, F32, kind="Internal").ap()


def stage_load(k):
    nc, ps = k.nc, k.psum
    loaded, table_in = k.sem("ld_loaded"), k.sem("ld_table")
    turned, kept = k.sem("ld_turned"), k.sem("ld_kept")
    bias_mm, bias_row, bias_out, diag_in = k.sem("ld_bias_mm"), k.sem("ld_bias_row"), [k.sem("ld_bias_out0"), k.sem("ld_bias_out1")], None
    with ExitStack() as ctx:
        xn = k.sb("xn", [P, TT, D], ctx=ctx)
        xs = k.sb("xs", [NS, D], ctx=ctx)
        cn = k.sb("cn", [C9, D], ctx=ctx)
        ba = k.sb("ba", [96, P], ctx=ctx)
        vecs = k.sb("vecs", [112, P], ctx=ctx)
        rows = k.sb("bias_rows", [P, 2, BREV], ctx=ctx)
        with nc.Block() as block:

            @block.sync
            def _(sp):
                sp.dma_start(k.const[:, :], k.i["const"]).then_inc(loaded, 16)
                sp.dma_start(k.pages[:, :], k.i["page_table"].rearrange("(o s) p -> o (s p)", o=1)).then_inc(loaded, 16)
                sp.dma_start(xs[:, :], k.i["x_sample"][:, 0, :]).then_inc(loaded, 16)
                sp.dma_start(cn[0:1, :], k.i["c_prompt"]).then_inc(loaded, 16)
                sp.dma_start(cn[1:C9, :], k.i["c_sample"]).then_inc(loaded, 16)
                sp.dma_start(ba[:, :], k.i["b_ada"].rearrange("l (a p) -> (l a) p", p=P)).then_inc(loaded, 16)
                sp.dma_start(vecs[0:32, :], k.i["norm_g"].rearrange("l (a p) -> (l a) p", p=P)).then_inc(loaded, 16)
                sp.dma_start(vecs[32:48, :], k.i["final_norm_g"].rearrange("(a p) -> a p", p=P)).then_inc(loaded, 16)
                sp.dma_start(vecs[48:96, :], k.i["conv_w"].rearrange("o w (a p) -> (o w a) p", p=P)).then_inc(loaded, 16)
                sp.dma_start(vecs[96:112, :], k.i["conv_b"].rearrange("o (a p) -> (o a) p", p=P)).then_inc(loaded, 16)
                sp.dma_start(xn[:, :, :], k.i["x_prompt"][0].rearrange("(i p) d -> p i d", p=P)).then_inc(loaded, 16)
                for h in range(2 * NH):
                    sp.wait_ge(bias_row, 2 * h + 2)
                    sp.dma_start(bass.AP(k.bias_skew.tensor, h * P * (BREV + 1), [[BREV + 1, P], [1, BREV]]), rows[:, h % 2, :]).then_inc(bias_out[h % 2], 16)

            @block.tensor
            def _(pe):
                pe.sem_inc(k.w_free, 4)
                pe.wait_ge(loaded, 11 * 16)
                n = 0
                for kt in range(KT):
                    if kt >= 4:
                        pe.wait_ge(kept, kt - 3)
                    for i in range(TT):
                        mm = pe.transpose(ps[:, kt % 4, i * P:(i + 1) * P], xn[:, i, kt * P:(kt + 1) * P], k.ident)
                    mm.then_inc(turned, 1)
                for kt in range(KT):
                    mm = pe.transpose(ps[:, 4, kt * NS:(kt + 1) * NS], xs[:, kt * P:(kt + 1) * P], k.ident[0:NS, 0:NS])
                mm.then_inc(turned, 1)
                for kt in range(KT):
                    mm = pe.transpose(ps[:, 5, kt * C9:(kt + 1) * C9], cn[:, kt * P:(kt + 1) * P], k.ident[0:C9, 0:C9])
                mm.then_inc(turned, 1)
                pe.transpose(ps[:, 6, 0:96], ba[:, :], k.ident[0:96, 0:96])
                pe.transpose(ps[:, 6, 96:208], vecs[:, :], k.ident[0:112, 0:112]).then_inc(turned, 1)
                pe.wait_ge(table_in, 32)
                pe.wait_ge(kept, KT + 3)
                for h in range(2 * NH):
                    if h >= 2:
                        pe.wait_ge(bias_row, 2 * h - 2)
                    pe.matmul(ps[:, 6 + h % 2, :], k.table[:, h:h + 1].broadcast_to([32, P]), k.hot[:, O_P:O_P + T], start=True, stop=True).then_inc(bias_mm, 1)

            @block.scalar
            def _(act):
                act.dma_start(k.table[:, :], k.i["rel_bias"]).then_inc(table_in, 16)
                act.dma_start(k.hot[:, :], k.i["hot"]).then_inc(table_in, 16)
                act.wait_ge(turned, KT + 1)
                nc.scalar.activation(k.xT[:, :, T:TC], ps[:, 4, 0:KT * NS].rearrange("p (k s) -> p k s", s=NS), ACT.Copy).then_inc(k.s_small, 1)
                act.wait_ge(turned, KT + 2)
                nc.scalar.activation(k.cT[:, :, :], ps[:, 5, 0:KT * C9].rearrange("p (k s) -> p k s", s=C9), ACT.Copy).then_inc(k.s_small, 1)
                act.wait_ge(turned, KT + 3)
                nc.scalar.activation(k.vT[:, :], ps[:, 6, 0:208], ACT.Copy).then_inc(k.s_small, 1)

            @block.gpsimd
            def _(pool):
                pool.memset(k.onesb[:, :], 1.0).then_inc(k.s_ones, 1)
                pool.wait_ge(k.s_ones, 1)

            @block.vector
            def _(dve):
                dve.memset(rows[:, 0, T:BREV], NEG).then_inc(bias_row, 1)
                dve.memset(rows[:, 1, T:BREV], NEG).then_inc(k.s_misc, 1)
                for kt in range(KT):
                    dve.wait_ge(turned, kt + 1)
                    dve.tensor_copy(k.xT[:, kt, 0:T], ps[:, kt % 4, :]).then_inc(kept, 1)
                dve.wait_ge(k.s_small, 3)
                dve.wait_ge(k.s_misc, 1)
                dve.nop().then_inc(kept, 3)
                for h in range(2 * NH):
                    dve.wait_ge(bias_mm, h + 1)
                    if h >= 2:
                        dve.wait_ge(bias_out[h % 2], 16 * (h // 2))
                    dve.tensor_copy(rows[:, h % 2, 0:T], ps[:, 6 + h % 2, :]).then_inc(bias_row, 1 if h == 0 else 2)
                for b in range(2):
                    dve.wait_ge(bias_out[b], 16 * NH)


def stage_ada(k, layer):
    nc, ps = k.nc, k.psum
    rows_kept, turned, kept = (k.sem(f"ada_{n}") for n in ("rows_kept", "turned", "kept"))
    r = k.ring
    with ExitStack() as ctx:
        rows = k.sb(f"ada_rows{layer}", [C9, 2, 512], ctx=ctx)
        with nc.Block() as block:

            @block.sync
            def _(sp):
                with sp.Fori(0, 12) as j:
                    for s in range(4):
                        sp.wait_ge(k.w_free, j * 4 + (r + s + 1))
                        src = k.i["w_ada"][layer, s * 512:(s + 1) * 512, bass.ds(j * 512, 512)]
                        sp.dma_start(k.w[:, (r + s) % 4, :].rearrange("p (a n) -> p a n", n=512), src.rearrange("(a p) n -> p a n", p=P)).then_inc(k.w_in[(r + s) % 4], 16)

            @block.tensor
            def _(pe):
                pe.sem_inc(kept, 2)
                with pe.Fori(0, 6) as j:
                    for c in range(2):
                        for q in range(4):
                            n = r + c * 4 + q
                            pe.wait_ge(k.w_in[n % 4], j * 32 + 16 * (n // 4 + 1))
                            for a in range(4):
                                mm = pe.matmul(ps[0:C9, c, :], k.cT[:, q * 4 + a, :], k.w[:, n % 4, a * 512:(a + 1) * 512], start=(q + a == 0), stop=(q + a == 6))
                            mm.then_inc(k.w_free, 1)
                        pe.wait_ge(rows_kept, j * 2 + (c + 1))
                        pe.wait_ge(kept, j * 2 + (c + 1))
                        settle(k, pe)
                        for f in range(4):
                            mm = pe.transpose(ps[:, 2 + c, f * C9:(f + 1) * C9], rows[:, c, f * P:(f + 1) * P], k.ident[0:C9, 0:C9])
                        mm.then_inc(turned, 1)

            @block.scalar
            def _(act):
                with act.Fori(0, 6) as j:
                    for c in range(2):
                        act.wait_ge(k.w_free, j * 8 + (r + 4 + 4 * (c + 1)))
                        nc.scalar.activation(rows[:, c, :], ps[0:C9, c, :], ACT.Copy).then_inc(rows_kept, 1)

            @block.vector
            def _(dve):
                with dve.Fori(0, 6) as j:
                    for c in range(2):
                        dve.wait_ge(turned, j * 2 + (c + 1))
                        dve.tensor_tensor(k.adaT[:, bass.ds(j * 8 + c * 4, 4), :], ps[:, 2 + c, 0:4 * C9].rearrange("p (f c) -> p f c", c=C9),
                                          k.vT[:, bass.ds(j * 8 + (layer * 48 + c * 4), 4)].unsqueeze(2).broadcast_to([P, 4, C9]), ALU.add).then_inc(kept, 1)
                dve.wait_ge(kept, 14)
    k.ring += 48


def stage_norm(k, layer):
    nc, ps = k.nc, k.psum
    sq_done, sum_mm, step, root, scaled, high, fin = (k.sem(f"nm_{n}") for n in ("square", "sum", "step", "root", "scaled", "high", "fin"))
    with ExitStack() as ctx:
        sq = k.sb(f"nm_sq{layer}", [P, 2, TC], ctx=ctx)
        v = k.sb(f"nm_v{layer}", [P, TC], ctx=ctx)
        t = k.sb(f"nm_t{layer}", [P, TC], ctx=ctx)
        rs = k.sb(f"nm_r{layer}", [P, TC], ctx=ctx)
        ab = k.sb(f"nm_ab{layer}", [P, KT, C9], ctx=ctx)
        hs = k.sb(f"nm_hs{layer}", [P, KT, NS], ctx=ctx)
        hp = k.sb(f"nm_hp{layer}", [P, 4, T], ctx=ctx)
        with nc.Block() as block:

            @block.scalar
            def _(act):
                with act.Fori(0, KT // 2) as j:
                    for b in range(2):
                        act.wait_ge(sum_mm, j * 2 + (b + 1))
                        nc.scalar.activation(sq[:, b, :], k.xT[:, bass.ds(j * 2 + b, 1), :].rearrange("p o c -> p (o c)"), ACT.Square).then_inc(sq_done, 1)
                act.wait_ge(step, 1)
                nc.scalar.activation(rs[:, :], v[:, :], ACT.Sqrt).then_inc(root, 1)
                if layer == 2:
                    return
                for kt in range(KT):
                    act.wait_ge(scaled, kt + 1)
                    nc.scalar.activation(k.hh[:, kt, 0:T], hp[:, kt % 4, :], ACT.Identity, bias=k.adaT[:, kt, 0:1]).then_inc(high, 1)
                act.wait_ge(scaled, KT + 1)
                nc.scalar.activation(k.hh[:, :, T:TC], hs[:, :, :], ACT.Copy).then_inc(high, 1)

            @block.tensor
            def _(pe):
                pe.sem_inc(sum_mm, 2)
                for kt in range(KT):
                    pe.wait_ge(sq_done, kt + 1)
                    for hf in range(2):
                        mm = pe.matmul(ps[:, hf, 0:HC], k.ones, sq[:, kt % 2, hf * HC:(hf + 1) * HC], start=(kt == 0), stop=(kt == KT - 1))
                    mm.then_inc(sum_mm, 1)

            @block.vector
            def _(dve):
                n = 0

                def then(ins):
                    nonlocal n
                    n += 1
                    ins.then_inc(step, 1)
                    return n

                dve.wait_ge(sum_mm, KT + 2)
                for hf in range(2):
                    ins = dve.tensor_scalar(v[:, hf * HC:(hf + 1) * HC], ps[:, hf, 0:HC], 1.0 / D, EPS, ALU.mult, ALU.add)
                then(ins)
                if layer < 2:
                    dve.scalar_tensor_tensor(out=ab[:, :, :], in0=k.adaT[:, KT:2 * KT, :], scalar=1.0,
                                             in1=k.vT[:, 96 + layer * KT:96 + (layer + 1) * KT].unsqueeze(2).broadcast_to([P, KT, C9]), op0=ALU.add, op1=ALU.mult)
                dve.wait_ge(root, 1)
                dve.wait_ge(step, then(dve.reciprocal(t[:, :], rs[:, :])))
                dve.wait_ge(step, then(dve.tensor_tensor(rs[:, :], t[:, :], t[:, :], ALU.mult)))
                dve.wait_ge(step, then(dve.tensor_tensor(rs[:, :], rs[:, :], v[:, :], ALU.mult)))
                dve.wait_ge(step, then(dve.tensor_scalar(rs[:, :], rs[:, :], -0.5, 1.5, ALU.mult, ALU.add)))
                dve.wait_ge(step, then(dve.tensor_tensor(rs[:, :], rs[:, :], t[:, :], ALU.mult)))
                if layer == 2:
                    for kt in range(KT):
                        dve.scalar_tensor_tensor(out=k.hT[:, kt, :], in0=k.xT[:, kt, :], scalar=k.vT[:, 128 + kt:129 + kt], in1=rs[:, :], op0=ALU.mult, op1=ALU.mult).then_inc(fin, 1)
                    dve.wait_ge(fin, KT)
                    return

                def scale(kt):
                    dve.scalar_tensor_tensor(out=hp[:, kt % 4, :], in0=k.xT[:, kt, 0:T], scalar=ab[:, kt, 0:1], in1=rs[:, 0:T], op0=ALU.mult, op1=ALU.mult).then_inc(scaled, 1)

                def low(kt):
                    dve.wait_ge(high, kt + 1)
                    dve.scalar_tensor_tensor(out=k.hl[:, kt, 0:T], in0=hp[:, kt % 4, :], scalar=k.adaT[:, kt, 0:1], in1=k.hh[:, kt, 0:T].bitcast(F32), op0=ALU.add, op1=ALU.subtract).then_inc(fin, 1)

                for kt in range(KT + 2):
                    if kt < KT:
                        if kt >= 4:
                            dve.wait_ge(fin, kt - 3)
                        scale(kt)
                    if kt >= 2:
                        low(kt - 2)
                dve.wait_ge(step, then(dve.tensor_tensor(hs[:, :, :], k.xT[:, :, T:TC], rs[:, T:TC].unsqueeze(1).broadcast_to([P, KT, NS]), ALU.mult)))
                dve.wait_ge(step, then(dve.tensor_tensor(hs[:, :, :], hs[:, :, :], ab[:, :, 1:C9], ALU.mult)))
                dve.tensor_tensor(hs[:, :, :], hs[:, :, :], k.adaT[:, 0:KT, 1:C9], ALU.add).then_inc(scaled, 1)
                dve.wait_ge(high, KT + 1)
                dve.tensor_tensor(k.hl[:, :, T:TC], hs[:, :, :], k.hh[:, :, T:TC].bitcast(F32), ALU.subtract).then_inc(fin, 1)
                dve.wait_ge(fin, KT + 1)


class Split:

    def __init__(self, k):
        self.k, self.r = k, k.ring
        self.high, self.used = k.sem("sp_high"), k.sem("sp_used")

    def hi(self, act, s, j4):
        k, n = self.k, self.r + s
        act.wait_ge(k.w_in[n % 4], j4 * 4 + 16 * (n // 4 + 1))
        act.wait_ge(self.used, j4 + (s + 1))
        act.activation(k.wh[:, s % 2, :], k.w[:, n % 4, :], ACT.Copy).then_inc(self.high, 1)

    def lo(self, dve, s, j4):
        k, n = self.k, self.r + s
        dve.wait_ge(self.high, j4 + (s + 1))
        dve.tensor_tensor(k.wl[:, s % 2, :], k.w[:, n % 4, :], k.wh[:, s % 2, :].bitcast(F32), ALU.subtract).then_inc(k.w_free, 1)

    def matmuls(self, pe, s, j4, banks):
        k, n = self.k, self.r + s
        pe.wait_ge(k.w_free, j4 + (n + 5))
        wh, wl = (t[:, s % 2, :].rearrange("p (a n) -> p a n", n=P) for t in (k.wh, k.wl))
        for kt in range(KT):
            for m, (w, x) in enumerate(((wh, k.hh), (wh, k.hl), (wl, k.hh))):
                for hf in range(2):
                    mm = pe.matmul(k.psum[:, banks + hf, 0:HC], w[:, kt, :], x[:, kt, hf * HC:(hf + 1) * HC], start=(kt == 0 and m == 0), stop=(kt == KT - 1 and m == 2))
        mm.then_inc(self.used, 1)


def stage_project(k):
    nc, ps = k.nc, k.psum
    kept_a, kept_v = k.sem("pj_kept_a"), k.sem("pj_kept_v")
    stored = k.stored
    gate_w_in = k.sem("pj_gate_w_in")
    r = k.ring
    sp_ = Split(k)
    rounds = NTILES // 4 - 1
    with ExitStack() as ctx:
        out = k.sb("pj_out", [P, 4, TC], ctx=ctx)
        with nc.Block() as block:

            @block.sync
            def _(sp):

                def load(n, slot, col):
                    sp.wait_ge(k.w_free, n + 1)
                    sp.dma_start(k.w[:, slot, :].rearrange("p (a n) -> p a n", n=P), k.i["w_in_att"][0, :, col].rearrange("(a p) n -> p a n", p=P)).then_inc(k.w_in[slot], 16)

                for first, col, count in RUNS:
                    with sp.Fori(0, count // 4) as j:
                        for s in range(4):
                            load(j * 4 + (r + first + s), (r + first + s) % 4, bass.ds(j * 512 + (col + s * P), P))
                n = r + NTILES - 2
                load(n, n % 4, slice(RUNS[2][1] + 8 * P, RUNS[2][1] + 9 * P))
                n += 1
                sp.wait_ge(k.w_free, n + 1)
                wg = k.w[:, n % 4, :].rearrange("p (a n) -> p a n", n=P)
                sp.dma_start(wg[:, :, 0:WI_ROW], k.i["w_in_att"][0, :, GA_COL:GA_COL + WI_ROW].rearrange("(a p) n -> p a n", p=P)).then_inc(k.w_in[n % 4], 16)
                sp.dma_start(wg[:, :, WI_ROW:P], k.i["w_in_att"][0, :, WI_COL:WI_COL + NI].rearrange("(a p) n -> p a n", p=P)).then_inc(gate_w_in, 16)

            @block.tensor
            def _(pe):
                pe.sem_inc(kept_a, 4)
                pe.sem_inc(kept_v, 4)
                pe.sem_inc(sp_.used, 2)

                def tile(s, j4):
                    pe.wait_ge(kept_a, j4 + (s + 1))
                    pe.wait_ge(kept_v, j4 + (s + 1))
                    sp_.matmuls(pe, s, j4, (s % 4) * 2)

                with pe.Fori(0, rounds) as j:
                    for s in range(4):
                        tile(s, j * 4)
                for s in range(4 * rounds, NTILES):
                    tile(s, 0)

            @block.scalar
            def _(act):

                def step(s, j4, first=False, last=False):
                    if not last:
                        sp_.hi(act, s + 1, j4)
                    act.wait_ge(sp_.used, j4 + (s + 3))
                    if not first:
                        act.wait_ge(stored[s % 4], j4 * 4 + 16 * (s // 4))
                    nc.scalar.activation(out[:, s % 4, 0:HC], ps[:, (s % 4) * 2, 0:HC], ACT.Copy).then_inc(kept_a, 1)

                sp_.hi(act, 0, 0)
                for s in range(4):
                    step(s, 0, first=True)
                with act.Fori(1, rounds) as j:
                    for s in range(4):
                        step(s, j * 4)
                for s in range(4 * rounds, NTILES):
                    if s + 1 == NTILES - 1:
                        act.wait_ge(gate_w_in, 16)
                    step(s, 0, last=(s == NTILES - 1))

            @block.vector
            def _(dve):

                def step(s, j4, first=False, last=False):
                    if not last:
                        sp_.lo(dve, s + 1, j4)
                    dve.wait_ge(sp_.used, j4 + (s + 3))
                    if not first:
                        dve.wait_ge(stored[s % 4], j4 * 4 + 16 * (s // 4))
                    dve.tensor_copy(out[:, s % 4, HC:TC], ps[:, (s % 4) * 2 + 1, 0:HC]).then_inc(kept_v, 1)

                sp_.lo(dve, 0, 0)
                for s in range(4):
                    step(s, 0, first=True)
                with dve.Fori(1, rounds) as j:
                    for s in range(4):
                        step(s, j * 4)
                for s in range(4 * rounds, NTILES):
                    step(s, 0, last=(s == NTILES - 1))

            @block.gpsimd
            def _(pool):

                def store(s, j4, tile):
                    pool.wait_ge(kept_a, j4 + (s + 5))
                    pool.wait_ge(kept_v, j4 + (s + 5))
                    pool.dma_start(tile, out[:, s % 4, :]).then_inc(stored[s % 4], 16)

                with pool.Fori(0, rounds) as j:
                    for s in range(4):
                        store(s, j * 4, k.proj[bass.ds(j * 4 + s, 1)].rearrange("o p c -> (o p) c"))
                for s in range(4 * rounds, NTILES):
                    store(s, 0, k.proj[s])
                for s in range(4):
                    pool.wait_ge(stored[s], 16 * len(range(s, NTILES, 4)))
    k.ring += NTILES


def stage_rows(k):
    nc, ps = k.nc, k.psum
    tile_in, turned, rows_kept, rows_out, moved = (k.sem(f"rw_{n}") for n in ("tile_in", "turned", "rows_kept", "rows_out", "moved"))
    pairs = [(KC, "cmp_k"), (VC, "cmp_v"), (KS, "slc_k"), (VS, "slc_v"), (KW, "win_k"), (VW, "win_v"), (KB, "dsa_k"), (VB, "dsa_v"), (KI, "idx_k")]
    with ExitStack() as ctx:
        src = k.sb("rw_src", [P, 2, 2, TC], ctx=ctx)
        rows = k.sb("rw_rows", [P, 2, TT, 256], ctx=ctx)
        rows_s = k.sb("rw_rows_s", [NS, 2, 256], ctx=ctx)
        with nc.Block() as block:

            @block.sync
            def _(sp):
                for n, (tile, name) in enumerate(pairs + [(GW, None)]):
                    if n >= 2:
                        sp.wait_ge(turned, n - 1)
                    if name == "idx_k":
                        sp.dma_start(src[:, n % 2, 0, :], k.proj[tile]).then_inc(tile_in, 16)
                    elif name:
                        sp.dma_start(src[:, n % 2, :, :], k.proj[tile:tile + 2].rearrange("g p c -> p g c")).then_inc(tile_in, 16)
                    else:
                        sp.dma_start(src[:, n % 2, 0, :], k.proj[tile]).then_inc(tile_in, 16)
                    sp.wait_ge(tile_in, 16 * (n + 1))
                for name in ("win_k", "win_v"):
                    sp.dma_start(k.o[name + "_s"][0, :, 0:WIN - 1], k.i["state_nsa_" + name][0, :, 1:WIN]).then_inc(moved, 16)
                sp.wait_ge(moved, 32)

            @block.tensor
            def _(pe):
                for n, (tile, name) in enumerate(pairs + [(GW, None)]):
                    pe.wait_ge(tile_in, 16 * (n + 1))
                    if n >= 2:
                        pe.wait_ge(rows_kept, 2 * (n - 1))
                    width, parts = P, 2 if name and name != "idx_k" else 1
                    for g in range(parts):
                        for i in range(TT):
                            at = i * 256 + g * P
                            pe.transpose(ps[:, 3 * (n % 2) + at // 512, at % 512:at % 512 + width], src[0:width, n % 2, g, i * P:(i + 1) * P], k.ident[0:width, 0:width])
                        mm = pe.transpose(ps[0:NS, 3 * (n % 2) + 2, g * P:g * P + width], src[0:width, n % 2, g, T:TC], k.ident[0:width, 0:width])
                    mm.then_inc(turned, 1)

            @block.vector
            def _(dve):
                for n, (tile, name) in enumerate(pairs + [(GW, None)]):
                    width = 256 if name and name != "idx_k" else P
                    dve.wait_ge(turned, n + 1)
                    if name:
                        if n >= 2:
                            dve.wait_ge(rows_out, 32 * (n - 1))
                        to, to_s = rows[:, n % 2, :, 0:width], rows_s[:, n % 2, 0:width]
                    b = 3 * (n % 2)
                    if not name:
                        for at, row, w in ((0, 0, NGA), (NGA, WI_ROW, NI)):
                            dve.tensor_copy(k.gw[:, :, at:at + w], ps[:, b:b + 2, :].rearrange("p b (i c) -> p (b i) c", c=256)[:, :, row:row + w])
                            dve.tensor_copy(k.gws[:, at:at + w], ps[0:NS, b + 2, row:row + w]).then_inc(rows_kept, 1)
                        continue
                    dve.tensor_copy(to, ps[:, b:b + 2, :].rearrange("p b (i c) -> p (b i) c", c=256)[:, :, 0:width]).then_inc(rows_kept, 1)
                    dve.tensor_copy(to_s, ps[0:NS, b + 2, 0:width]).then_inc(rows_kept, 1)
                dve.wait_ge(rows_kept, 2 * (len(pairs) + 1))

            @block.scalar
            def _(act):
                for n, (tile, name) in enumerate(pairs):
                    width = P if name == "idx_k" else 256
                    act.wait_ge(rows_kept, 2 * (n + 1))
                    flat = "a b (i p) g d -> p (a b i) (g d)" if width == 256 else "a b (i p) d -> p (a b i) d"
                    flat_s = "a b t g d -> (a b t) (g d)" if width == 256 else "a b t d -> (a b t) d"
                    act.dma_start(k.o[name + "_p"].rearrange(flat, p=P), rows[:, n % 2, :, 0:width]).then_inc(rows_out, 16)
                    out_s = k.o[name + "_s"]
                    if name[:3] == "win":
                        out_s = out_s[:, :, WIN - 1:WIN]
                    act.dma_start(out_s.rearrange(flat_s), rows_s[:, n % 2, 0:width]).then_inc(rows_out, 16)
                    act.wait_ge(rows_out, 32 * (n + 1))


def stage_sample_queries(k):
    nc = k.nc
    got, zero, step, out, back = (k.sem(f"sq_{n}") for n in ("got", "zero", "step", "out", "back"))
    with nc.Block() as block:

        @block.sync
        def _(sp):
            sp.dma_start(k.sT[:, :, :], k.proj[0:GW, :, T:TC].rearrange("t p s -> p t s")).then_inc(got, 16)
            sp.wait_ge(step, 2)
            sp.dma_start(k.gate_rows, k.gws[:, :]).then_inc(out, 16)
            sp.wait_ge(out, 16)
            sp.dma_start(k.ga_s[:, :], k.gate_rows[:, 0:NGA].rearrange("s (h b) -> s h b", b=3)).then_inc(back, 16)
            sp.dma_start(k.wi_s[:, :], k.gate_rows[:, NGA:NGW].unsqueeze(2)).then_inc(back, 16)
            sp.wait_ge(back, 32)

        @block.gpsimd
        def _(pool):
            pool.memset(k.qpa[:, :], 0.0)
            pool.memset(k.qpb[:, :], 0.0)
            pool.memset(k.qpi[:, :], 0.0).then_inc(zero, 1)
            pool.memset(k.zeros[:, :], 0.0).then_inc(zero, 1)
            pool.wait_ge(zero, 2)

        @block.vector
        def _(dve):
            dve.wait_ge(k.s_sig, 2)
            dve.tensor_scalar(k.gw[:, :, 0:NGA], k.gw[:, :, 0:NGA], 1.0, None, ALU.add)
            dve.tensor_scalar(k.gws[:, 0:NGA], k.gws[:, 0:NGA], 1.0, None, ALU.add).then_inc(k.s_sig, 1)
            dve.wait_ge(k.s_sig, 3)
            dve.reciprocal(k.gw[:, :, 0:NGA], k.gw[:, :, 0:NGA])
            dve.reciprocal(k.gws[:, 0:NGA], k.gws[:, 0:NGA]).then_inc(step, 1)
            dve.tensor_scalar(k.gw[:, :, NGA:NGW], k.gw[:, :, NGA:NGW], NI ** -0.5, None, ALU.mult)
            dve.tensor_scalar(k.gws[:, NGA:NGW], k.gws[:, NGA:NGW], NI ** -0.5, None, ALU.mult).then_inc(step, 1)
            dve.wait_ge(got, 16)
            dve.wait_ge(zero, 2)
            for pad, tile, scale in ((k.qpa, QA, SCALE), (k.qpb, QB, SCALE)):
                for h in range(NH):
                    at = (h // 4) * 64 + h
                    dve.tensor_scalar(pad[:, at:at + 136 * 7 + 1:136], k.sT[:, tile + h, :], scale, None, ALU.mult).then_inc(step, 1)
            for h in range(NI):
                dve.tensor_scalar(k.qpi[:, h:h + 144 * 7 + 1:144], k.sT[:, QI + h, :], SCALE, None, ALU.mult).then_inc(step, 1)
            dve.wait_ge(step, 2 + 2 * NH + NI)
            dve.wait_ge(back, 32)
            dve.tensor_scalar(k.wsel[:, :], k.const[:, C_BD16:C_BD16 + NS], k.wi_s[:, 0:1], None, ALU.mult).then_inc(step, 1)
            dve.wait_ge(step, 3 + 2 * NH + NI)

        @block.scalar
        def _(act):
            nc.scalar.activation(k.gw[:, :, 0:NGA], k.gw[:, :, 0:NGA], ACT.Exp, scale=-1.0).then_inc(k.s_sig, 1)
            nc.scalar.activation(k.gws[:, 0:NGA], k.gws[:, 0:NGA], ACT.Exp, scale=-1.0).then_inc(k.s_sig, 1)


def settle(k, eng):
    eng.sem_inc(k.settled[eng.engine], 1)


def off(i):
    return P * (i * (i + 1) // 2)


def stage_index_prompt(k):
    nc, ps = k.nc, k.psum
    q_in, mm_done, relu_done, added, step, chosen = [k.sem("ip_q_in0"), k.sem("ip_q_in1")], *(k.sem(f"ip_{n}") for n in ("mm", "relu", "added", "step", "chosen"))
    k_in = k.sem("ip_k_in")
    with ExitStack() as ctx:
        q = k.sb("ip_q", [P, 2, TC], ctx=ctx)
        ki = k.sb("ip_k", [P, TC], ctx=ctx)
        rl = k.sb("ip_relu", [P, 2, off(TT)], ctx=ctx)
        best = k.sb("ip_best", [P, 8], ctx=ctx)
        sc = k.mask
        with nc.Block() as block:

            @block.sync
            def _(sp):
                sp.dma_start(ki[:, :], k.proj[KI]).then_inc(k_in, 16)
                with sp.Fori(0, NI // 2) as j:
                    for b in range(2):
                        sp.wait_ge(mm_done, j * 2 + (b + 1))
                        sp.dma_start(q[:, b, :], k.proj[bass.ds(j * 2 + (QI + b), 1)].rearrange("o p c -> (o p) c")).then_inc(q_in[b], 16)

            @block.tensor
            def _(pe):
                pe.sem_inc(mm_done, 2)
                pe.sem_inc(relu_done, 2)
                pe.wait_ge(k_in, 16)
                with pe.Fori(0, NI // 2) as j:
                    for b in range(2):
                        pe.wait_ge(q_in[b], j * 16 + 16)
                        pe.wait_ge(relu_done, j * 2 + (b + 1))
                        for i in range(TT):
                            mm = pe.matmul(ps[:, 4 * b + i, 0:P * (i + 1)], q[:, b, i * P:(i + 1) * P], ki[:, 0:P * (i + 1)], start=True, stop=True)
                        mm.then_inc(mm_done, 1)

            @block.scalar
            def _(act):
                with act.Fori(0, NI // 2) as j:
                    for b in range(2):
                        act.wait_ge(mm_done, j * 2 + (b + 3))
                        act.wait_ge(added, j * 2 + (b + 1))
                        for i in range(TT):
                            ins = nc.scalar.activation(rl[:, b, off(i):off(i + 1)], ps[:, 4 * b + i, 0:P * (i + 1)], ACT.Relu, scale=SCALE)
                        ins.then_inc(relu_done, 1)

            @block.vector
            def _(dve):
                dve.memset(sc[:, :], 0.0).then_inc(added, 2)
                with dve.Fori(0, NI // 2) as j:
                    for b in range(2):
                        dve.wait_ge(relu_done, j * 2 + (b + 3))
                        dve.wait_ge(added, j * 2 + (b + 2))
                        for i in range(TT):
                            ins = dve.scalar_tensor_tensor(out=sc[:, off(i):off(i + 1)], in0=rl[:, b, off(i):off(i + 1)], scalar=k.gw[:, i, bass.ds(j * 2 + (NGA + b), 1)],
                                                           in1=sc[:, off(i):off(i + 1)], op0=ALU.mult, op1=ALU.add)
                        ins.then_inc(added, 1)
                dve.wait_ge(step, TT)
                n = TT
                for i in range(1, TT):
                    with dve.Fori(0, TOPK_P // 8) as j:
                        dve.wait_ge(step, j * 2 + n)
                        settle(k, dve)
                        dve.max(best[:, :], sc[:, off(i):off(i + 1)]).then_inc(step, 1)
                        dve.wait_ge(step, j * 2 + (n + 1))
                        settle(k, dve)
                        dve.match_replace(sc[:, off(i):off(i + 1)], best[:, :], sc[:, off(i):off(i + 1)], TAKEN).then_inc(step, 1)
                    n += 2 * (TOPK_P // 8)
                dve.wait_ge(step, n)
                dve.memset(sc[:, off(0):off(1)], 0.0).then_inc(step, 1)
                dve.tensor_scalar(sc[:, off(1):off(TT)], sc[:, off(1):off(TT)], TAKEN, NEG, ALU.not_equal, ALU.mult).then_inc(step, 1)
                dve.wait_ge(step, n + 2)

            @block.gpsimd
            def _(pool):
                pool.wait_ge(added, NI + 2)
                for i in range(TT):
                    d = sc[:, off(i + 1) - P:off(i + 1)]
                    pool.affine_select(out=d, in_=d, compare_op=ALU.is_ge, fill=NEG, base=0, pattern=[[-1, P]], channel_multiplier=1).then_inc(step, 1)


def load_pages(k, sp, name, dst, arrived, s, group_dims=True):
    for g in range(PG):
        page = sp.value_load(k.pages[0:1, bass.ds(s * PG + g, 1)], min_val=0, max_val=NPOOL - 1)
        src = k.i[name][0, bass.ds(page, 1)]
        src = src.rearrange("o p g d -> (o p) (g d)") if group_dims else src.rearrange("o p d -> (o p) d")
        sp.dma_start(dst[:, g, :], src).then_inc(arrived, 16)


def stage_index_sample(k):
    nc, ps = k.nc, k.psum
    arrived = [k.sem("is_arrived0"), k.sem("is_arrived1")]
    turned, kept_a, kept_v, used, qcopy, relu_done, summed, scored, step = (k.sem(f"is_{n}") for n in
        ("turned", "kept_a", "kept_v", "used", "qcopy", "relu", "summed", "scored", "step"))
    with ExitStack() as ctx:
        pg = k.sb("is_pages", [P, 2, PG, P], ctx=ctx)
        kt = k.sb("is_keys", [P, 2, PAST], ctx=ctx)
        qs = k.sb("is_q", [P, 2, P], ctx=ctx)
        rl = k.sb("is_relu", [P, PAST + 1], ctx=ctx)
        best = k.sb("is_best", [NS, 8], ctx=ctx)
        sc = k.mask_s
        with nc.Block() as block:

            @block.sync
            def _(sp):
                with sp.Fori(0, NS // 2) as j:
                    for b in range(2):
                        sp.wait_ge(turned, j * 8 + (4 * b + 4))
                        load_pages(k, sp, "cache_dsa_idx_k", pg[:, b], arrived[b], j * 2 + b, False)

            @block.tensor
            def _(pe):
                pe.sem_inc(turned, 8)
                pe.sem_inc(used, 2)
                pe.sem_inc(kept_a, 1)
                pe.sem_inc(kept_v, 1)
                for c in range(4):
                    pe.matmul(ps[:, c, :], k.zeros[:, :], k.xT[:, 0, 0:512], start=True, stop=True)
                for s in range(NS):
                    mm = pe.matmul(ps[:, 4, 0:1], k.qpi[:, s * P:(s + 1) * P], k.sT[:, KI, s:s + 1], start=(s == 0), stop=(s == NS - 1))
                mm.then_inc(summed, 1)
                with pe.Fori(0, NS // 2) as j:
                    for b in range(2):
                        pe.wait_ge(arrived[b], j * (16 * PG) + 16 * PG)
                        for c in range(4):
                            pe.wait_ge(kept_v if c % 2 else kept_a, j * 4 + (2 * b + c // 2 + 1))
                            for g in range(4):
                                mm = pe.transpose(ps[:, 5 + c % 2, g * P:(g + 1) * P], pg[:, b, c * 4 + g, :], k.ident)
                            mm.then_inc(turned, 1)
                        pe.wait_ge(qcopy, j * 2 + (b + 1))
                        for c in range(4):
                            pe.wait_ge(kept_v if c % 2 else kept_a, j * 4 + (2 * b + c // 2 + 2))
                            mm = pe.matmul(ps[:, c, :], qs[:, b, :], kt[:, b, c * 512:(c + 1) * 512], start=False, stop=True, skip_group_check=True)
                        mm.then_inc(used, 1)
                pe.wait_ge(relu_done, 5)
                for c in range(4):
                    mm = pe.matmul(ps[0:NS, c, :], k.wsel[:, :], rl[:, c * 512:(c + 1) * 512], start=True, stop=True)
                pe.matmul(ps[0:NS, 4, 0:1], k.wsel[:, :], rl[:, PAST:PAST + 1], start=True, stop=True).then_inc(scored, 1)

            @block.scalar
            def _(act):
                with act.Fori(0, NS // 2) as j:
                    for b in range(2):
                        act.wait_ge(used, j * 2 + (b + 1))
                        nc.scalar.activation(qs[:, b, :], k.qpi[:, bass.ds(j * 256 + b * P, P)], ACT.Copy).then_inc(qcopy, 1)
                        for c in (0, 2):
                            act.wait_ge(turned, j * 8 + (8 + 4 * b + c + 1))
                            nc.scalar.activation(kt[:, b, c * 512:(c + 1) * 512], ps[:, 5, :], ACT.Copy).then_inc(kept_a, 1)
                act.wait_ge(used, NS + 2)
                act.wait_ge(summed, 1)
                for c in range(4):
                    nc.scalar.activation(rl[:, c * 512:(c + 1) * 512], ps[:, c, :], ACT.Relu).then_inc(relu_done, 1)
                nc.scalar.activation(rl[:, PAST:PAST + 1], ps[:, 4, 0:1], ACT.Relu).then_inc(relu_done, 1)

            @block.vector
            def _(dve):
                with dve.Fori(0, NS // 2) as j:
                    for b in range(2):
                        dve.wait_ge(used, j * 2 + (b + 1))
                        for c in (1, 3):
                            dve.wait_ge(turned, j * 8 + (8 + 4 * b + c + 1))
                            dve.tensor_copy(kt[:, b, c * 512:(c + 1) * 512], ps[:, 6, :]).then_inc(kept_v, 1)
                dve.wait_ge(scored, 1)
                dve.tensor_copy(sc[:, 0:PAST], ps[0:NS, 0:4, :].rearrange("p b c -> p (b c)"))
                dve.tensor_copy(sc[:, PAST:PAST + 1], ps[0:NS, 4, 0:1]).then_inc(step, 2)
                with dve.Fori(0, TOPK_S // 8) as j:
                    dve.wait_ge(step, j * 2 + 2)
                    settle(k, dve)
                    dve.max(best[:, :], sc[:, :]).then_inc(step, 1)
                    dve.wait_ge(step, j * 2 + 3)
                    settle(k, dve)
                    dve.match_replace(sc[:, :], best[:, :], sc[:, :], TAKEN).then_inc(step, 1)
                dve.wait_ge(step, 2 + TOPK_S // 4)
                dve.tensor_scalar(sc[:, :], sc[:, :], TAKEN, NEG, ALU.not_equal, ALU.mult).then_inc(step, 1)
                dve.wait_ge(step, 3 + TOPK_S // 4)


def stage_compress(k, which):
    nc, ps = k.nc, k.psum
    names = ("cz_w", "cz_prompt", "cz_zero", "cz_pe", "cz_pe_mm", "cz_pe_kept", "cz_turned", "cz_kept_a", "cz_kept_v", "cz_hid", "cz_x", "cz_exp",
             "cz_act", "cz_step", "cz_hid_turned", "cz_hid_kept", "cz_out", "cz_done", "cz_arrived0", "cz_arrived1")
    sems = [k.sem(n) for n in names]
    w_got, prompt_in, zeroed, pe_turned, pe_mm, pe_kept, turned, kept_a, kept_v, hid, x_done, exp_done, act_done, step, hid_turned, hid_kept, out_mm, done, arr0, arr1 = sems
    arrived = [arr0, arr1]
    keys = which == "k"
    dst = k.kcmp if keys else k.vcmp
    with ExitStack() as ctx:
        w1 = k.sb("cz_w1" + which, [P, CB, CH], ctx=ctx)
        w2 = k.sb("cz_w2" + which, [P, 2, P], ctx=ctx)
        pe_n = k.sb("cz_pen" + which, [CB, P], ctx=ctx)
        pe_t = k.sb("cz_pet" + which, [P, CB], ctx=ctx)
        pe_b = k.sb("cz_peb" + which, [P, CH], ctx=ctx)
        pg = k.sb("cz_pg" + which, [P, 2, PG // 2, 256], ctx=ctx)
        xt = k.sb("cz_xt" + which, [P, 2, G, PAST], ctx=ctx)
        x = k.sb("cz_x" + which, [P, CH], ctx=ctx)
        e = k.sb("cz_e" + which, [P, CH], ctx=ctx)
        hc = k.sb("cz_hc" + which, [P, CH], ctx=ctx)
        with nc.Block() as block:

            @block.sync
            def _(sp):
                sp.dma_start(pe_n[:, :], k.i["cmp_pe_" + which][0]).then_inc(w_got, 16)
                sp.dma_start(w1[:, :, :], k.i["cmp_w1_" + which][0].rearrange("(l d) n -> d l n", d=P)).then_inc(w_got, 16)
                sp.dma_start(w2[:, :, :], k.i["cmp_w2_" + which][0].rearrange("(c d) n -> d c n", d=P)).then_inc(w_got, 16)
                sp.wait_ge(zeroed, 1)
                t = KC if keys else VC
                sp.dma_start(xt[:, 1, :, 0:T], k.proj[t:t + 2, :, 0:T].rearrange("g p c -> p g c")).then_inc(prompt_in, 16)
                with sp.Fori(0, NS) as s:
                    for hf in range(2):
                        sp.wait_ge(turned, s * 8 + (4 * hf + 4))
                        for g in range(PG // 2):
                            page = sp.value_load(k.pages[0:1, bass.ds(s * PG + (hf * (PG // 2) + g), 1)], min_val=0, max_val=NPOOL - 1)
                            sp.dma_start(pg[:, hf, g, :], k.i["cache_nsa_cmp_" + which][0, bass.ds(page, 1)].rearrange("o p g d -> (o p) (g d)")).then_inc(arrived[hf], 16)

            @block.tensor
            def _(pe):
                pe.sem_inc(turned, 8)
                pe.sem_inc(kept_a, 1)
                pe.sem_inc(kept_v, 1)
                pe.wait_ge(w_got, 48)
                pe.transpose(ps[:, 6, 0:CB], pe_n[:, :], k.ident[0:CB, 0:CB]).then_inc(pe_turned, 1)
                pe.wait_ge(pe_kept, 1)
                for l in range(CB):
                    mm = pe.matmul(ps[:, 2, 0:CH], pe_t[:, l:l + 1].broadcast_to([P, P]), w1[:, l, :], start=(l == 0), stop=(l == CB - 1))
                mm.then_inc(pe_mm, 1)

                def hidden(b):
                    for l in range(CB):
                        rows = xt[:, b, :, :].rearrange("p g (n l) -> p (g n) l", l=CB)[:, :, l]
                        mm = pe.matmul(ps[:, b, 0:CH], rows, w1[:, l, :], start=(l == 0), stop=(l == CB - 1))
                    mm.then_inc(hid, 1)

                def second(n):
                    pe.wait_ge(act_done, n)
                    for c in range(2):
                        mm = pe.transpose(ps[:, 6, c * P:(c + 1) * P], hc[:, c * P:(c + 1) * P], k.ident)
                    mm.then_inc(hid_turned, 1)
                    pe.wait_ge(hid_kept, n)
                    for c in range(2):
                        if keys:
                            mm = pe.matmul(ps[:, 7, 0:P], w2[:, c, :], k.hct[:, c * P:(c + 1) * P], start=(c == 0), stop=(c == 1))
                        else:
                            mm = pe.matmul(ps[:, 7, 0:P], k.hct[:, c * P:(c + 1) * P], w2[:, c, :], start=(c == 0), stop=(c == 1))
                    mm.then_inc(out_mm, 1)

                pe.wait_ge(prompt_in, 16)
                hidden(1)
                with pe.Fori(0, NS // 2) as j:
                    for b in range(2):
                        for hf in range(2):
                            pe.wait_ge(arrived[hf], j * (2 * 8 * 16) + 8 * 16 * (b + 1))
                            for c in range(4):
                                pe.wait_ge(kept_v if c % 2 else kept_a, j * 8 + (4 * b + 2 * hf + c // 2 + 1))
                                for g in range(G):
                                    for q in range(2):
                                        mm = pe.transpose(ps[:, 4 + c % 2, g * 256 + q * P:g * 256 + (q + 1) * P], pg[:, hf, 2 * c + q, g * P:(g + 1) * P], k.ident)
                                mm.then_inc(turned, 1)
                        second(j * 2 + (b + 1))
                        pe.wait_ge(kept_a, j * 8 + (4 * b + 5))
                        pe.wait_ge(kept_v, j * 8 + (4 * b + 5))
                        hidden(b)
                second(NS + 1)

            def turned_rows(eng, copy, n, b, j, par, kept):
                eng.wait_ge(hid, n)
                for hf in range(2):
                    for c in range(par, 4, 2):
                        eng.wait_ge(turned, j * 16 + (8 * b + 4 * hf + c + 9))
                        at = hf * 1024 + c * 256
                        copy(xt[:, b, :, at:at + 256], ps[:, 4 + par, :].rearrange("p (g q) -> p g q", g=G)).then_inc(kept, 1)

            @block.scalar
            def _(act):
                def copy(o, i):
                    return nc.scalar.activation(o, i, ACT.Copy)

                def unit(n):
                    act.wait_ge(x_done, n)
                    nc.scalar.activation(e[:, :], x[:, :], ACT.Exp, scale=-1.0).then_inc(exp_done, 1)

                def turned_hidden(n):
                    act.wait_ge(hid_turned, n)
                    copy(k.hct[:, :], ps[:, 6, 0:CH]).then_inc(hid_kept, 1)

                act.wait_ge(pe_turned, 1)
                copy(pe_t[:, :], ps[:, 6, 0:CB]).then_inc(pe_kept, 1)
                with act.Fori(0, NS // 2) as j:
                    for b in range(2):
                        unit(j * 2 + (b + 1))
                        turned_rows(act, copy, j * 2 + (b + 1) if b else j * 2 + 1, b, j, 0, kept_a)
                        turned_hidden(j * 2 + (b + 1))
                unit(NS + 1)
                turned_hidden(NS + 1)

            @block.vector
            def _(dve):
                def silu(n, b, base):
                    dve.wait_ge(hid, n)
                    dve.tensor_tensor(x[:, :], ps[:, b, 0:CH], pe_b[:, :], ALU.add).then_inc(x_done, 1)
                    dve.wait_ge(exp_done, n)
                    dve.tensor_scalar(e[:, :], e[:, :], 1.0, None, ALU.add).then_inc(step, 1)
                    dve.wait_ge(step, base + 1)
                    dve.reciprocal(e[:, :], e[:, :]).then_inc(step, 1)
                    dve.wait_ge(step, base + 2)
                    dve.tensor_tensor(hc[:, :], x[:, :], e[:, :], ALU.mult).then_inc(act_done, 1)

                def keep_out(n, to):
                    dve.wait_ge(out_mm, n)
                    dve.tensor_copy(to, ps[:, 7, 0:P]).then_inc(done, 1)

                dve.memset(xt[:, 1, :, :], 0.0).then_inc(zeroed, 1)
                dve.wait_ge(pe_mm, 1)
                dve.tensor_copy(pe_b[:, :], ps[:, 2, 0:CH]).then_inc(step, 1)
                dve.wait_ge(step, 1)
                with dve.Fori(0, NS // 2) as j:
                    for b in range(2):
                        silu(j * 2 + (b + 1), 1 - b, j * 4 + (2 * b + 1))
                        turned_rows(dve, dve.tensor_copy, j * 2 + (b + 1) if b else j * 2 + 1, b, j, 1, kept_v)
                        keep_out(j * 2 + (b + 1), dst[:, bass.ds(j * 2 + b, 1), :].rearrange("p o c -> p (o c)"))
                silu(NS + 1, 1, 2 * NS + 1)
                keep_out(NS + 1, dst[:, NS, :])
                dve.wait_ge(done, NS + 1)



def stage_compressed_sample(k):
    nc, ps = k.nc, k.psum
    mm_done, step, exp_done, grouped, out_mm, ct_kept = (k.sem(f"cs_{n}") for n in ("mm", "step", "exp", "grouped", "out", "ct_kept"))
    R = NS * NH
    with ExitStack() as ctx:
        p = k.sb("cs_p", [R, 2, NCB], ctx=ctx)
        pt = k.sb("cs_pt", [P, R], ctx=ctx)
        st = k.sb("cs_stat", [R, 4], ctx=ctx)
        best = k.sb("cs_best", [NS * G, 8], ctx=ctx)
        with nc.Block() as block:

            @block.tensor
            def _(pe):
                pe.wait_ge(step, 1)
                pe.matmul(ps[0:R, 0, 0:NCB], k.tabs[:, 0, :], k.hot[:, O_C:O_C + NCB], start=True, stop=False)
                for n in range(NS * G):
                    mm = pe.matmul(ps[0:R, 0, 0:NCB], k.qpa[:, n * R:(n + 1) * R], k.kcmp[:, n // G + 1, (n % G) * NCB:(n % G + 1) * NCB], start=False, stop=(n == NS * G - 1))
                mm.then_inc(mm_done, 1)
                pe.wait_ge(step, 5)
                pe.matmul(ps[0:NS * G, 1, 0:NCB], k.const[0:R, C_R16:C_R16 + NS * G], p[:, 0, :], start=True, stop=True).then_inc(grouped, 1)
                pe.wait_ge(step, 8)
                pe.transpose(ps[:, 2, 0:R], p[:, :, :].rearrange("r a n -> r (a n)"), k.ident[0:R, 0:R]).then_inc(out_mm, 1)
                pe.wait_ge(ct_kept, 1)
                for n in range(NS * G):
                    s, g = n // G, n % G
                    at = s * NH + g * 4
                    mm = pe.matmul(ps[:, 3 + g, at:at + 4], k.vcmp[g * NCB:(g + 1) * NCB, s + 1, :], pt[g * NCB:(g + 1) * NCB, at:at + 4], start=(s == 0), stop=True, skip_group_check=True)
                mm.then_inc(out_mm, 1)

            @block.scalar
            def _(act):
                act.wait_ge(step, 3)
                nc.scalar.activation(p[:, 0, :], ps[0:R, 0, 0:NCB], ACT.Exp, bias=st[:, 1:2], accum_out=st[:, 2:3]).then_inc(exp_done, 1)
                act.wait_ge(out_mm, 1)
                nc.scalar.activation(pt[:, :], ps[:, 2, 0:R], ACT.Copy).then_inc(ct_kept, 1)

            @block.vector
            def _(dve):
                for m in range(2):
                    ins = dve.tensor_copy(k.tabs[:, m, :].rearrange("p (s h) -> p s h", h=NH), k.table[:, m * NH:(m + 1) * NH].unsqueeze(1).broadcast_to([32, NS, NH]))
                ins.then_inc(step, 1)
                dve.wait_ge(mm_done, 1)
                dve.reduce_max(st[:, 0:1], ps[0:R, 0, 0:NCB], AX).then_inc(step, 1)
                dve.wait_ge(step, 2)
                dve.tensor_scalar(st[:, 1:2], st[:, 0:1], -1.0, None, ALU.mult).then_inc(step, 1)
                dve.wait_ge(exp_done, 1)
                dve.reciprocal(st[:, 3:4], st[:, 2:3]).then_inc(step, 1)
                dve.wait_ge(step, 4)
                dve.tensor_scalar(p[:, 0, :], p[:, 0, :], st[:, 3:4], None, ALU.mult).then_inc(step, 1)
                dve.memset(k.msel[:, :], 0.0).then_inc(step, 1)
                dve.wait_ge(grouped, 1)
                dve.wait_ge(step, 6)
                dve.tensor_reduce(k.msel[:, 0:NCB // 2], ps[0:NS * G, 1, 0:NCB].rearrange("p (n r) -> p n r", r=2), AX, ALU.add).then_inc(step, 1)
                dve.wait_ge(step, 7)
                dve.tensor_scalar(p[:, 0, :], p[:, 0, :], k.ga_s[:, 0:1], None, ALU.mult).then_inc(k.s_misc2, 1)
                dve.wait_ge(k.s_misc2, 1)
                dve.tensor_copy(p[:, 1, :], p[:, 0, :]).then_inc(step, 1)
                n = 8
                for c in (slice(0, 1), slice(31, 33)):
                    dve.tensor_scalar(k.msel[:, c], k.msel[:, c], 1e4, None, ALU.add).then_inc(step, 1)
                    n += 1
                for r in range(2):
                    dve.wait_ge(step, n)
                    settle(k, dve)
                    dve.max(best[:, :], k.msel[:, :]).then_inc(step, 1)
                    dve.wait_ge(step, n + 1)
                    settle(k, dve)
                    dve.match_replace(k.msel[:, :], best[:, :], k.msel[:, :], TAKEN).then_inc(step, 1)
                    n += 2
                dve.wait_ge(step, n)
                dve.tensor_scalar(k.msel[:, :], k.msel[:, :], TAKEN, NEG, ALU.not_equal, ALU.mult)
                dve.wait_ge(out_mm, 2)
                for g in range(G):
                    def cols(t):
                        return t.rearrange("p (s h) -> p s h", h=NH)[:, :, g * 4:(g + 1) * 4]
                    dve.tensor_copy(cols(k.oS[:, 0, :]), cols(ps[:, 3 + g, 0:R])).then_inc(step, 1)
                dve.wait_ge(step, n + 2)


def stage_attend_sample(k, kind):
    nc, ps = k.nc, k.psum
    mixer, npg, kname, vname, ktile, nkname, gate = {
        "slc": (0, PG, "cache_nsa_slc_k", "cache_nsa_slc_v", KS, "slc_v_s", 1),
        "win": (0, WIN // P, "state_nsa_win_k", "state_nsa_win_v", KW, "win_v_s", 2),
        "dsa": (1, PG, "cache_dsa_k", "cache_dsa_v", KB, "dsa_v_s", None)}[kind]
    names = ("arr0", "arr1", "varr0", "varr1", "vnew", "turned", "kept_a", "kept_v", "used", "qcopy", "mm", "step", "exp", "pt", "pt_kept_a", "pt_kept_v", "vused", "out")
    sems = [k.sem("at_" + n) for n in names]
    arr0, arr1, varr0, varr1, vnew_in, turned, kept_a, kept_v, used, qcopy, mm_done, step, exp_done, pt_mm, pt_kept_a, pt_kept_v, vused, out_mm = sems
    arrived, v_arrived = [arr0, arr1], [varr0, varr1]
    R = NS * NH
    qp = (k.qpa, k.qpb)[mixer]
    NK = npg * P
    hp = npg // 2
    tb = hp // 2
    kb = NK // 512
    hot0 = O_S + PAST - NK
    with ExitStack() as ctx:
        pg = k.sb("at_pg" + kind, [P, 2, hp, 256], ctx=ctx)
        kt = k.sb("at_kt" + kind, [P, 2, G, NK], ctx=ctx)
        qs = k.sb("at_q" + kind, [P, 2, G * R], ctx=ctx)
        p = k.sb("at_p" + kind, [R, NK + 1], ctx=ctx)
        pt = k.sb("at_pt" + kind, [P, npg, R], ctx=ctx)
        st = k.sb("at_st" + kind, [R, 8], ctx=ctx)
        pd = k.sb("at_pd" + kind, [R, NS], ctx=ctx)
        pn = k.sb("at_pn" + kind, [NS, R], ctx=ctx)
        vnew = k.sb("at_vn" + kind, [NS, 256], ctx=ctx)
        with nc.Block() as block:

            @block.sync
            def _(sp):
                if kind == "win":
                    sp.dma_start(vnew[:, :], k.o[nkname][0, :, WIN - 1].rearrange("s g d -> s (g d)")).then_inc(vnew_in, 16)
                else:
                    sp.dma_start(vnew[:, :], k.o[nkname][0, :, 0].rearrange("s g d -> s (g d)")).then_inc(vnew_in, 16)

                def half(s, hf, name, sem):
                    if kind == "win":
                        sp.dma_start(pg[:, hf, :, :], k.i[name][0, bass.ds(s, 1), hf * hp * P:(hf + 1) * hp * P].rearrange("o (n p) g d -> p (o n) (g d)", p=P)).then_inc(sem, 16)
                        return
                    for g in range(hp):
                        page = sp.value_load(k.pages[0:1, bass.ds(s * PG + (hf * hp + g), 1)], min_val=0, max_val=NPOOL - 1)
                        sp.dma_start(pg[:, hf, g, :], k.i[name][0, bass.ds(page, 1)].rearrange("o p g d -> (o p) (g d)")).then_inc(sem, 16)

                with sp.Fori(0, NS) as s:
                    for hf in range(2):
                        sp.wait_ge(turned, s * (2 * tb) + (hf * tb + tb))
                        half(s, hf, kname, arrived[hf])
                sp.wait_ge(turned, 2 * tb * (NS + 1))
                with sp.Fori(0, NS) as s:
                    for hf in range(2):
                        sp.wait_ge(vused, s * 2 + (hf + 1))
                        half(s, hf, vname, v_arrived[hf])

            per = 16 * (1 if kind == "win" else hp)

            @block.tensor
            def _(pe):
                pe.sem_inc(turned, 2 * tb)
                pe.sem_inc(used, 2)
                pe.sem_inc(kept_a, 1)
                pe.sem_inc(kept_v, 1)
                pe.sem_inc(vused, 2)
                for c in range(kb + 1):
                    o = ps[0:R, c, :] if c < kb else ps[0:R, 4, 0:1]
                    hot = k.hot[:, hot0 + c * 512:hot0 + (c + 1) * 512] if c < kb else k.hot[:, O_S + PAST:O_S + PAST + 1]
                    pe.matmul(o, k.tabs[:, mixer, :], hot, start=True, stop=True)
                    if kind == "slc":
                        sel = k.msel[:, c * 8:(c + 1) * 8].unsqueeze(2).broadcast_to([NS * G, 8, 64]) if c < kb else k.msel[:, 32:33]
                        pe.matmul(o, k.const[0:NS * G, C_RT:C_RT + R], sel, start=False, stop=True, skip_group_check=True)
                    if kind == "dsa":
                        sel = k.mask_s[:, c * 512:(c + 1) * 512] if c < kb else k.mask_s[:, PAST:PAST + 1]
                        pe.matmul(o, k.const[0:NS, C_E8:C_E8 + R], sel, start=False, stop=True, skip_group_check=True)
                for n in range(NS * G):
                    pe.matmul(ps[0:R, 4, 0:1], qp[:, n * R:(n + 1) * R], k.sT[:, ktile + n % G, n // G:n // G + 1], start=False, stop=True, skip_group_check=True)
                with pe.Fori(0, NS // 2) as j:
                    for b in range(2):
                        for hf in range(2):
                            pe.wait_ge(arrived[hf], j * (2 * per) + per * (b + 1))
                            for c in range(tb):
                                q = hf * tb + c
                                pe.wait_ge(kept_v if q % 2 else kept_a, j * (2 * tb) + (tb * b + q // 2 + 1))
                                for g in range(G):
                                    for a in range(2):
                                        mm = pe.transpose(ps[:, 5 + q % 2, g * 256 + a * P:g * 256 + (a + 1) * P], pg[:, hf, 2 * c + a, g * P:(g + 1) * P], k.ident)
                                mm.then_inc(turned, 1)
                        pe.wait_ge(qcopy, j * 2 + (b + 1))
                        pe.wait_ge(kept_a, j * (2 * tb) + (tb * b + tb + 1))
                        pe.wait_ge(kept_v, j * (2 * tb) + (tb * b + tb + 1))
                        for c in range(kb):
                            for g in range(G):
                                mm = pe.matmul(ps[0:R, c, :], qs[:, b, g * R:(g + 1) * R], kt[:, b, g, c * 512:(c + 1) * 512], start=False, stop=True, skip_group_check=True)
                        mm.then_inc(used, 1)
                pe.wait_ge(step, kb + 6)
                for a in range(npg):
                    mm = pe.transpose(ps[:, 5 + a // 8, (a % 8) * R:(a % 8 + 1) * R], p[:, a * P:(a + 1) * P], k.ident[0:R, 0:R])
                pe.transpose(ps[0:NS, 7, 0:R], pd[:, :], k.ident[0:R, 0:R]).then_inc(pt_mm, 1)
                pe.wait_ge(pt_kept_a, 2)
                pe.wait_ge(pt_kept_v, 1)
                pe.wait_ge(vnew_in, 16)
                for g in range(G):
                    o = ps[:, 0, 0:R].rearrange("p (s h) -> p s h", h=NH)[:, :, g * 4:(g + 1) * 4]
                    pe.matmul(o, vnew[:, g * P:(g + 1) * P], pn[:, :].rearrange("p (s h) -> p s h", h=NH)[:, :, g * 4:(g + 1) * 4], start=(g == 0), stop=True, skip_group_check=True)
                with pe.Fori(0, NS) as s:
                    for hf in range(2):
                        pe.wait_ge(v_arrived[hf], s * per + per)
                        for a in range(hp):
                            for g in range(G):
                                mm = pe.matmul(ps[:, 0, bass.ds(s * NH + g * 4, 4)], pg[:, hf, a, g * P:(g + 1) * P], pt[:, hf * hp + a, bass.ds(s * NH + g * 4, 4)], start=False, stop=True, skip_group_check=True)
                        mm.then_inc(vused, 1)

            def turned_keys(eng, copy, j, b, par, kept):
                for q in range(par, 2 * tb, 2):
                    eng.wait_ge(turned, j * (4 * tb) + (2 * tb * b + q + 2 * tb + 1))
                    copy(kt[:, b, :, q * 256:(q + 1) * 256], ps[:, 5 + par, :].rearrange("p (g q) -> p g q", g=G)).then_inc(kept, 1)

            @block.scalar
            def _(act):
                def copy(o, i):
                    return nc.scalar.activation(o, i, ACT.Copy)

                with act.Fori(0, NS // 2) as j:
                    for b in range(2):
                        act.wait_ge(used, j * 2 + (b + 1))
                        copy(qs[:, b, :], qp[:, bass.ds(j * (4 * R) + b * 2 * R, 2 * R)]).then_inc(qcopy, 1)
                        turned_keys(act, copy, j, b, 0, kept_a)
                act.wait_ge(step, kb + 3)
                nc.scalar.activation(p[:, :], p[:, :], ACT.Exp, bias=st[:, 6:7], accum_out=st[:, 7:8]).then_inc(exp_done, 1)
                act.wait_ge(pt_mm, 1)
                copy(pt[:, 0:min(npg, 8), :], ps[:, 5, 0:min(npg, 8) * R].rearrange("p (a r) -> p a r", r=R)).then_inc(pt_kept_a, 1)
                copy(pn[:, :], ps[0:NS, 7, 0:R]).then_inc(pt_kept_a, 1)

            @block.vector
            def _(dve):
                with dve.Fori(0, NS // 2) as j:
                    for b in range(2):
                        dve.wait_ge(used, j * 2 + (b + 1))
                        turned_keys(dve, dve.tensor_copy, j, b, 1, kept_v)
                dve.wait_ge(used, NS + 2)
                for c in range(kb):
                    dve.tensor_copy(p[:, c * 512:(c + 1) * 512], ps[0:R, c, :]).then_inc(step, 1)
                dve.tensor_copy(p[:, NK:NK + 1], ps[0:R, 4, 0:1]).then_inc(step, 1)
                dve.wait_ge(step, kb + 1)
                dve.reduce_max(st[:, 5:6], p[:, :], AX).then_inc(step, 1)
                dve.wait_ge(step, kb + 2)
                dve.tensor_scalar(st[:, 6:7], st[:, 5:6], -1.0, None, ALU.mult).then_inc(step, 1)
                dve.wait_ge(exp_done, 1)
                dve.reciprocal(st[:, 4:5], st[:, 7:8]).then_inc(step, 1)
                dve.wait_ge(step, kb + 4)
                if gate is None:
                    dve.tensor_scalar(p[:, :], p[:, :], st[:, 4:5], None, ALU.mult).then_inc(step, 1)
                else:
                    dve.tensor_scalar(p[:, :], p[:, :], st[:, 4:5], k.ga_s[:, gate:gate + 1], ALU.mult, ALU.mult).then_inc(step, 1)
                dve.wait_ge(step, kb + 5)
                dve.tensor_scalar(pd[:, :], k.const[0:R, C_BD8:C_BD8 + NS], p[:, NK:NK + 1], None, ALU.mult).then_inc(step, 1)
                dve.wait_ge(pt_mm, 1)
                if npg > 8:
                    dve.tensor_copy(pt[:, 8:16, :], ps[:, 6, :].rearrange("p (a r) -> p a r", r=R)).then_inc(pt_kept_v, 1)
                else:
                    dve.nop().then_inc(pt_kept_v, 1)
                dve.wait_ge(vused, 2 * NS + 2)
                if kind == "dsa":
                    dve.tensor_copy(k.oS[:, 1, :], ps[:, 0, 0:R]).then_inc(out_mm, 1)
                else:
                    dve.tensor_tensor(k.oS[:, 0, :], ps[:, 0, 0:R], k.oS[:, 0, :], ALU.add).then_inc(out_mm, 1)
                dve.wait_ge(out_mm, 1)


def stage_attend_prompt(k, mixer):
    nc, ps = k.nc, k.psum
    A = mixer == 0
    branches = [(KS, "slc_v_p"), (KW, "win_v_p")] if A else [(KB, "dsa_v_p")]
    NB = len(branches)
    HG = NH // G
    units = [(r, i, br) for r in range(HG) for i in range(TT) for br in range(NB)]
    U = len(units)
    UH = U // HG
    SL = 2 if A else 4
    names = ("in0", "in1", "in2", "in3", "scaled", "qk", "added", "neg", "exp", "recip", "prob", "turned", "kept", "pv", "head", "fin", "ez", "zstep",
             "cqk", "cstep", "csub", "cexp", "cprob", "cturned", "ckept", "cmask", "vc", "zrecip")
    sems = [k.sem("pa_" + n) for n in names]
    in0, in1, in2, in3, scaled, qk, added, neg, exped, recip, prob, turned, kept, pv, head, fin, ez, zstep, cqk, cstep, csub, cexp, cprob, cturned, ckept, cmask_set, vc_out, zrecip = sems
    arrived = [in0, in1, in2, in3]
    loads = 8 if A else 5
    tile0, ztile, ytile = (QA, ZA, 0) if A else (QB, ZB, NH)
    tag = "AB"[mixer]
    ring = 4
    with ExitStack() as ctx:
        hq = k.sb("pa_q" + tag, [P, SL, T], ctx=ctx)
        hz = k.sb("pa_z" + tag, [P, SL, TC], ctx=ctx)
        hk = k.sb("pa_k" + tag, [P, SL, NB, T], ctx=ctx)
        hv = k.sb("pa_v" + tag, [P, SL, NB, TT, P], ctx=ctx)
        ht = k.sb("pa_t" + tag, [P, SL, T], ctx=ctx)
        hvc = k.sb("pa_vc" + tag, [NCB // 4, 2, P], ctx=ctx)
        e = k.sb("pa_e" + tag, [P, SL, TC], ctx=ctx)
        sc = k.sb("pa_s" + tag, [P, ring, T], ctx=ctx)
        pt = k.sb("pa_pt" + tag, [P, ring, T], ctx=ctx)
        st = k.sb("pa_st" + tag, [P, ring, 4], ctx=ctx)
        lc = k.sb("pa_lc" + tag, [P, TT, 16], ctx=ctx)
        cm = k.sb("pa_cm" + tag, [P, TT, 16], ctx=ctx)
        cs = k.sb("pa_cs" + tag, [P, 4, TT], ctx=ctx)
        pc = k.sb("pa_pc" + tag, [16, T], ctx=ctx)
        yo = k.sb("pa_yo" + tag, [P, 2, TC], ctx=ctx)
        with nc.Block() as block:

            @block.sync
            def _(sp):
                if A:
                    for g in range(G):
                        sp.dma_start(k.vcmp_rows[g], k.vcmp[g * NCB:g * NCB + 16, 0, :]).then_inc(vc_out, 16)
                    sp.wait_ge(vc_out, 32)
                with sp.Fori(0, G) as g:
                    for r in range(HG):
                        b = r % SL
                        sp.wait_ge(fin, g * HG + (r + 1))

                        def load(dst, src):
                            sp.dma_start(dst, src).then_inc(arrived[b], 16)

                        load(hq[:, b, :], k.proj[bass.ds(g * HG + (tile0 + r), 1), :, 0:T].rearrange("o p c -> (o p) c"))
                        load(hz[:, b, :], k.proj[bass.ds(g * HG + (ztile + r), 1)].rearrange("o p c -> (o p) c"))
                        load(ht[:, b, :], bass.AP(k.bias_skew.tensor, g * (HG * P * (BREV + 1)) + ((mixer * NH + r) * P * (BREV + 1) + P - 1), [[BREV, P], [1, T]]))
                        for br, (kt, v) in enumerate(branches):
                            load(hk[:, b, br, :], k.proj[bass.ds(g + kt, 1), :, 0:T].rearrange("o p c -> (o p) c"))
                            load(hv[:, b, br], k.o[v][0, 0, :, bass.ds(g, 1)].rearrange("(i p) o d -> p i (o d)", p=P))
                        if A:
                            load(hvc[:, b, :], k.vcmp_rows[bass.ds(g, 1)].rearrange("o n d -> (o n) d"))

            @block.tensor
            def _(pe):
                pe.sem_inc(added, 2)
                pe.sem_inc(kept, 2)
                pe.sem_inc(fin, SL)
                if A:
                    pe.sem_inc(csub, 1)
                    pe.sem_inc(ckept, 1)
                with pe.Fori(0, G) as g:
                    for t in range(U + 3):
                        if t < U:
                            r, i, br = units[t]
                            if t % UH == 0:
                                pe.wait_ge(scaled, g * HG + (r + 1))
                                if A:
                                    pe.wait_ge(csub, g * HG + (r + 1))
                                    for ii in range(TT):
                                        mm = pe.matmul(ps[:, 6, ii * 16:(ii + 1) * 16], hq[:, r % SL, ii * P:(ii + 1) * P], k.kcmp[:, 0, bass.ds(g * NCB, 16)], start=True, stop=True)
                                    mm.then_inc(cqk, 1)
                            pe.wait_ge(added, g * U + (t + 1))
                            pe.matmul(ps[:, t % 2, 0:P * (i + 1)], hq[:, r % SL, i * P:(i + 1) * P], hk[:, r % SL, br, 0:P * (i + 1)], start=True, stop=True).then_inc(qk, 1)
                        if 2 <= t < U + 2:
                            v = t - 2
                            r, i, br = units[v]
                            if A and v % UH == 0:
                                pe.wait_ge(cprob, g * HG + (r + 1))
                                pe.wait_ge(ckept, g * HG + (r + 1))
                                for ii in range(TT):
                                    mm = pe.transpose(ps[0:16, 7, ii * P:(ii + 1) * P], lc[:, ii, :], k.ident)
                                mm.then_inc(cturned, 1)
                            pe.wait_ge(prob, g * U + (v + 1))
                            pe.wait_ge(kept, g * U + (v + 1))
                            for c in range(i + 1):
                                mm = pe.transpose(ps[:, 2 + v % 2, c * P:(c + 1) * P], sc[:, v % ring, c * P:(c + 1) * P], k.ident)
                            mm.then_inc(turned, 1)
                        if t >= 3:
                            v = t - 3
                            r, i, br = units[v]
                            o = 4 + r % 2
                            if v % UH == 0:
                                pe.wait_ge(fin, g * HG + (r + SL - 1))
                                if A:
                                    pe.wait_ge(ckept, g * HG + (r + 2))
                                    pe.matmul(ps[:, o, :], hvc[:, r % SL, :], pc[:, :], start=True, stop=True)
                            pe.wait_ge(kept, g * U + (v + 3))
                            for c in range(i + 1):
                                mm = pe.matmul(ps[:, o, i * P:(i + 1) * P], hv[:, r % SL, br, c, :], pt[:, v % ring, c * P:(c + 1) * P],
                                               start=(not A and v % UH == 0 and c == 0), stop=True, skip_group_check=True)
                            mm.then_inc(pv, 1)

            @block.scalar
            def _(act):

                def scale_q(g, r):
                    act.wait_ge(arrived[r % SL], g * (HG // SL * 16 * loads) + 16 * loads * (r // SL + 1))
                    nc.scalar.activation(hq[:, r % SL, :], hq[:, r % SL, :], ACT.Copy, scale=SCALE).then_inc(scaled, 1)
                    nc.scalar.activation(e[:, r % SL, :], hz[:, r % SL, :], ACT.Exp, scale=-1.0).then_inc(ez, 1)

                with act.Fori(0, G) as g:
                    scale_q(g, 0)
                    for t in range(U + 2):
                        if t < U:
                            r, i, br = units[t]
                            if t % UH == UH - 2 and r + 1 < HG:
                                act.wait_ge(fin, g * HG + (r + 2))
                                scale_q(g, r + 1)
                            act.wait_ge(neg, g * U + (t + 1))
                            n = P * (i + 1)
                            nc.scalar.activation(sc[:, t % ring, 0:n], sc[:, t % ring, 0:n], ACT.Exp, bias=st[:, t % ring, 1:2], accum_out=st[:, t % ring, 2:3]).then_inc(exped, 1)
                            if A and t % UH == 0:
                                act.wait_ge(csub, g * HG + (r + 2))
                                nc.scalar.activation(lc[:, :, :], lc[:, :, :], ACT.Exp).then_inc(cexp, 1)
                        if t >= 2:
                            v = t - 2
                            r, i, br = units[v]
                            if A and v % UH == 0:
                                act.wait_ge(cturned, g * HG + (r + 1))
                                nc.scalar.activation(pc[:, :], ps[0:16, 7, :], ACT.Copy).then_inc(ckept, 1)
                            act.wait_ge(turned, g * U + (v + 1))
                            if v >= ring:
                                act.wait_ge(pv, g * U + (v - ring + 1))
                            nc.scalar.activation(pt[:, v % ring, 0:P * (i + 1)], ps[:, 2 + v % 2, 0:P * (i + 1)], ACT.Copy).then_inc(kept, 1)

            @block.vector
            def _(dve):

                def logits(g, t):
                    r, i, br = units[t]
                    n = P * (i + 1)
                    s = sc[:, t % ring, 0:n]
                    dve.wait_ge(qk, g * U + (t + 1))
                    if t >= ring:
                        dve.wait_ge(turned, g * U + (t - ring + 1))
                    bias = ht[:, r % SL, T - n:T]
                    if A:
                        settle(k, dve)
                        dve.tensor_tensor_reduce(s, ps[:, t % 2, 0:n], bias, 1.0, TAKEN, ALU.add, ALU.max, st[:, t % ring, 0:1]).then_inc(added, 1)
                        dve.wait_ge(added, g * U + (t + 3))
                    else:
                        dve.tensor_tensor(s, ps[:, t % 2, 0:n], bias, ALU.add).then_inc(added, 1)
                        dve.wait_ge(added, g * U + (t + 3))
                        settle(k, dve)
                        dve.tensor_tensor_reduce(s, s, k.mask[:, off(i):off(i + 1)], 1.0, TAKEN, ALU.add, ALU.max, st[:, t % ring, 0:1]).then_inc(cstep, 1)
                        dve.wait_ge(cstep, g * U + (t + 1))
                    dve.tensor_scalar(st[:, t % ring, 1:2], st[:, t % ring, 0:1], -1.0, None, ALU.mult).then_inc(neg, 1)

                def probabilities(g, t):
                    r, i, br = units[t]
                    s = sc[:, t % ring, 0:P * (i + 1)]
                    dve.wait_ge(exped, g * U + (t + 1))
                    dve.reciprocal(st[:, t % ring, 3:4], st[:, t % ring, 2:3]).then_inc(recip, 1)
                    dve.wait_ge(recip, g * U + (t + 1))
                    if A:
                        gate = k.gw[:, i, bass.ds(g * (3 * HG) + (3 * r + 1 + br), 1)]
                        dve.tensor_scalar(s, s, st[:, t % ring, 3:4], gate, ALU.mult, ALU.mult).then_inc(prob, 1)
                    else:
                        dve.tensor_scalar(s, s, st[:, t % ring, 3:4], None, ALU.mult).then_inc(prob, 1)

                def recip_z(g, r):
                    dve.wait_ge(zstep, g * (2 * HG) + (2 * r + 1))
                    dve.reciprocal(e[:, r % SL, :], e[:, r % SL, :]).then_inc(zrecip, 1)

                CS = 11

                def compressed_logits(g, r):
                    at = g * (HG * CS) + r * CS
                    dve.wait_ge(cqk, g * HG + (r + 1))
                    dve.wait_ge(cstep, at + 1)
                    dve.memset(lc[:, :, :], NEG).then_inc(cstep, 1)
                    dve.wait_ge(cstep, at + 2)
                    for i in range(TT):
                        n = 4 * (i + 1)
                        u0 = T - P * (i + 1) + CB - 1
                        dve.tensor_tensor(lc[:, i, 0:n], ps[:, 6, i * 16:i * 16 + n], ht[:, r % SL, u0:u0 + CB * (n - 1) + 1:CB], ALU.add).then_inc(cstep, 1)
                    dve.wait_ge(cstep, at + 6)
                    dve.reduce_max(cs[:, 0, :], lc[:, :, :], AX).then_inc(cstep, 1)
                    dve.wait_ge(cstep, at + 7)
                    dve.tensor_tensor(lc[:, :, :], lc[:, :, :], cs[:, 0, :].unsqueeze(2).broadcast_to([P, TT, 16]), ALU.subtract).then_inc(csub, 1)

                def compressed_probabilities(g, r):
                    at = g * (HG * CS) + r * CS
                    dve.wait_ge(cexp, g * HG + (r + 1))
                    dve.tensor_tensor(lc[:, :, :], lc[:, :, :], cm[:, :, :], ALU.mult).then_inc(cstep, 1)
                    dve.wait_ge(cstep, at + 8)
                    dve.tensor_reduce(cs[:, 1, :], lc[:, :, :], AX, ALU.add).then_inc(cstep, 1)
                    dve.wait_ge(cstep, at + 9)
                    dve.tensor_scalar(cs[:, 2, :], cs[:, 1, :], 1e-30, None, ALU.max).then_inc(cstep, 1)
                    dve.wait_ge(cstep, at + 10)
                    dve.reciprocal(cs[:, 1, :], cs[:, 2, :]).then_inc(cstep, 1)
                    dve.wait_ge(cstep, at + 11)
                    dve.tensor_tensor(cs[:, 3, :], cs[:, 1, :], k.gw[:, :, bass.ds(g * (3 * HG) + 3 * r, 1)].rearrange("p i o -> p (i o)"), ALU.mult).then_inc(cstep, 1)
                    dve.wait_ge(cstep, at + 12)
                    dve.tensor_tensor(lc[:, :, :], lc[:, :, :], cs[:, 3, :].unsqueeze(2).broadcast_to([P, TT, 16]), ALU.mult).then_inc(cprob, 1)

                def finish(g, r):
                    h = g * HG + r
                    dve.wait_ge(pv, g * U + UH * (r + 1))
                    dve.wait_ge(zstep, g * (2 * HG) + (2 * r + 2))
                    dve.wait_ge(k.y_out[r % 2], g * (16 * HG // 2) + 16 * (ytile // 2 + r // 2))
                    y = yo[:, r % 2, :]
                    dve.tensor_tensor(y[:, 0:T], ps[:, 4 + r % 2, :], e[:, r % SL, 0:T], ALU.mult)
                    o = k.oS[:, mixer, :].rearrange("p (s h) -> p h s", h=NH)[:, bass.ds(h, 1), :].rearrange("p o s -> p (o s)")
                    dve.tensor_tensor(y[:, T:TC], o, e[:, r % SL, T:TC], ALU.mult).then_inc(fin, 1)

                if A:
                    dve.wait_ge(cmask_set, 2)
                    dve.nop().then_inc(cstep, 1)
                with dve.Fori(0, G) as g:
                    for t in range(U + 4):
                        if t < U:
                            r = units[t][0]
                            logits(g, t)
                            if t % UH == 0:
                                if A:
                                    if r:
                                        dve.wait_ge(cturned, g * HG + r)
                                    compressed_logits(g, r)
                        if 1 <= t < U + 1:
                            if A and (t - 1) % UH == 0:
                                compressed_probabilities(g, units[t - 1][0])
                            probabilities(g, t - 1)
                            if (t - 1) % UH == 0:
                                recip_z(g, units[t - 1][0])
                        if t >= UH + 3 and (t - 3) % UH == 0:
                            finish(g, (t - 3) // UH - 1)
                dve.wait_ge(fin, NH + SL)

            @block.gpsimd
            def _(pool):
                if A:
                    pool.memset(cm[:, :, :], 1.0).then_inc(cmask_set, 1)
                    pool.wait_ge(cmask_set, 1)
                    pool.affine_select(out=cm[:, :, :], in_=cm[:, :, :], compare_op=ALU.is_ge, fill=0.0, base=-(CB - 1), pattern=[[P, TT], [-CB, 16]], channel_multiplier=1).then_inc(cmask_set, 1)
                def store(g, r):
                    pool.wait_ge(fin, g * HG + (r + 1 + SL))
                    pool.dma_start(k.y_rows[bass.ds(g * HG + (ytile + r), 1)].rearrange("o p c -> (o p) c"), yo[:, r % 2, :]).then_inc(k.y_out[r % 2], 16)

                with pool.Fori(0, G) as g:
                    for r in range(HG):
                        z = e[:, r % SL, :]
                        pool.wait_ge(ez, g * HG + (r + 1))
                        settle(k, pool)
                        pool.tensor_scalar(z, z, 1.0, None, ALU.add).then_inc(zstep, 1)
                        pool.wait_ge(zrecip, g * HG + (r + 1))
                        pool.tensor_tensor(z, hz[:, r % SL, :], z, ALU.mult).then_inc(zstep, 1)
                        if r:
                            store(g, r - 1)
                    store(g, HG - 1)
                for b in range(2):
                    pool.wait_ge(k.y_out[b], 16 * (ytile + NH) // 2)


def stage_out(k, layer):
    nc, ps = k.nc, k.psum
    w_out = k.i["w_out_att" if layer == 0 else "w_out_conv"]
    freed, step, fin, y_high, y_low = (k.sem("ou_" + n) for n in ("freed", "step", "fin", "y_high", "y_low"))
    y_in = [k.sem(f"ou_y_in{b}") for b in range(4)]
    r = k.ring
    sp_ = Split(k)
    with ExitStack() as ctx:
        t = k.sb(f"ou_t{layer}", [P, 2, NS], ctx=ctx)
        y = k.sb(f"ou_y{layer}", [P, 4, TC], ctx=ctx)
        with nc.Block() as block:

            @block.sync
            def _(sp):
                for kt in range(KT):
                    if kt >= 4:
                        sp.wait_ge(y_low, kt - 3)
                    sp.dma_start(y[:, kt % 4, :], k.y_rows[kt]).then_inc(y_in[kt % 4], 16)
                    if kt == 3:
                        for s in range(2):
                            sp.wait_ge(k.w_free, r + s + 1)
                            sp.dma_start(k.w[:, (r + s) % 4, :].rearrange("p (a n) -> p a n", n=P), w_out[0, :, s * P:(s + 1) * P].rearrange("(a p) n -> p a n", p=P)).then_inc(k.w_in[(r + s) % 4], 16)

                def load(s, j4, col):
                    sp.wait_ge(k.w_free, j4 + (r + s + 1))
                    sp.dma_start(k.w[:, (r + s) % 4, :].rearrange("p (a n) -> p a n", n=P), w_out[0, :, col].rearrange("(a p) n -> p a n", p=P)).then_inc(k.w_in[(r + s) % 4], 16)

                for s in range(2, 4):
                    load(s, 0, slice(s * P, (s + 1) * P))
                with sp.Fori(1, 4) as j:
                    for s in range(4):
                        load(s, j * 4, bass.ds(j * 512 + s * P, P))

            @block.tensor
            def _(pe):
                pe.sem_inc(freed, 4)
                pe.sem_inc(sp_.used, 2)
                pe.wait_ge(y_low, KT)

                def tile(s, j4):
                    pe.wait_ge(freed, j4 + (s + 1))
                    sp_.matmuls(pe, s, j4, 2 * (s % 4))

                with pe.Fori(0, 4) as j:
                    for s in range(4):
                        tile(s, j * 4)

            @block.scalar
            def _(act):
                for kt in range(KT):
                    act.wait_ge(y_in[kt % 4], 16 * (kt // 4 + 1))
                    nc.scalar.activation(k.hh[:, kt, :], y[:, kt % 4, :], ACT.Copy).then_inc(y_high, 1)
                    if kt == KT - 2:
                        sp_.hi(act, 0, 0)
                with act.Fori(0, 3) as j:
                    for s in range(4):
                        sp_.hi(act, s + 1, j * 4)
                for s in range(12, 15):
                    sp_.hi(act, s + 1, 0)

            @block.vector
            def _(dve):
                for kt in range(KT):
                    dve.wait_ge(y_high, kt + 1)
                    dve.tensor_tensor(k.hl[:, kt, :], y[:, kt % 4, :], k.hh[:, kt, :].bitcast(F32), ALU.subtract).then_inc(y_low, 1)
                sp_.lo(dve, 0, 0)

                def tile(s, j4, last=False):
                    if not last:
                        sp_.lo(dve, s + 1, j4)
                    dve.wait_ge(sp_.used, j4 + (s + 3))
                    f = j4 + s
                    x = k.xT[:, bass.ds(f, 1), :].rearrange("p o c -> p (o c)")
                    ada = k.adaT[:, bass.ds(f + 2 * KT, 1), :].rearrange("p o c -> p (o c)")
                    b = 2 * (s % 4)
                    dve.tensor_tensor(t[:, s % 2, :], ps[:, b + 1, T - HC:HC], ada[:, 1:C9], ALU.mult).then_inc(step, 1)
                    dve.scalar_tensor_tensor(out=x[:, 0:HC], in0=ps[:, b, 0:HC], scalar=ada[:, 0:1], in1=x[:, 0:HC], op0=ALU.mult, op1=ALU.add)
                    dve.scalar_tensor_tensor(out=x[:, HC:T], in0=ps[:, b + 1, 0:T - HC], scalar=ada[:, 0:1], in1=x[:, HC:T], op0=ALU.mult, op1=ALU.add).then_inc(freed, 1)
                    dve.wait_ge(step, j4 + (s + 1))
                    dve.tensor_tensor(x[:, T:TC], t[:, s % 2, :], x[:, T:TC], ALU.add).then_inc(fin, 1)

                with dve.Fori(0, 3) as j:
                    for s in range(4):
                        tile(s, j * 4)
                for s in range(12, 16):
                    tile(s, 0, last=(s == 15))
                dve.wait_ge(fin, KT)
                dve.wait_ge(freed, KT + 4)
    k.ring += 16


def stage_conv(k):
    nc, ps = k.nc, k.psum
    state_in, turned, st_kept, zeroed, cu_turned, cu_kept, out = (k.sem("cv_" + n) for n in ("state_in", "turned", "st_kept", "zeroed", "cu_turned", "cu_kept", "out"))
    freed = [k.sem(f"cv_freed{s}") for s in range(4)]
    step, ydone, zstep = k.sem("cv_step"), k.sem("cv_y"), k.sem("cv_zstep")
    zrecip = k.sem("cv_zrecip")
    r = k.ring
    sp_ = Split(k)
    CW = 96 + 48
    CBI = 96 + 96
    with ExitStack() as ctx:
        sn = k.sb("cv_sn", [2 * NS, D], ctx=ctx)
        stT = k.sb("cv_st", [P, KT, 2 * NS], ctx=ctx)
        hh = k.sb("cv_hh", [P, TC], ctx=ctx)
        bg = k.sb("cv_bg", [P, TC], ctx=ctx)
        z = k.sb("cv_z", [P, TC], ctx=ctx)
        e = k.sb("cv_e", [P, TC], ctx=ctx)
        u = k.sb("cv_u", [P, 2 + TC], ctx=ctx)
        y = k.sb("cv_yb", [P, TC], ctx=ctx)
        yo = k.sb("cv_yo", [P, TC], ctx=ctx)
        cu = k.sb("cv_cu", [P, KT, 2 + NS], ctx=ctx)
        rows = sn[0:2 + NS, :]
        with nc.Block() as block:

            @block.sync
            def _(sp):
                with sp.Fori(0, KT) as j:
                    for s in range(4):
                        sp.wait_ge(k.w_free, j * 4 + (r + s + 1))
                        sp.dma_start(k.w[:, (r + s) % 4, :].rearrange("p (a n) -> p a n", n=P), k.i["w_in_conv"][0, :, bass.ds(j * P + s * D, P)].rearrange("(a p) n -> p a n", p=P)).then_inc(k.w_in[(r + s) % 4], 16)
                sp.wait_ge(cu_kept, 1)
                sp.dma_start(k.o["conv_p"][0, 0], rows[0:2, :]).then_inc(out, 16)
                sp.dma_start(k.o["conv_s"][0, :, 1], rows[2:2 + NS, :]).then_inc(out, 16)
                sp.wait_ge(out, 48)

            @block.gpsimd
            def _(pool):
                pool.memset(u[:, 0:2], 0.0).then_inc(zeroed, 1)
                pool.wait_ge(zeroed, 1)
                with pool.Fori(0, KT) as j:
                    pool.wait_ge(freed[3], j + 2)
                    settle(k, pool)
                    pool.tensor_scalar(e[:, :], e[:, :], 1.0, None, ALU.add).then_inc(zstep, 1)
                    pool.wait_ge(zrecip, j + 1)
                    pool.tensor_tensor(e[:, :], z[:, :], e[:, :], ALU.mult).then_inc(zstep, 1)
                    pool.wait_ge(ydone, j + 2)
                    pool.dma_start(k.y_rows[bass.ds(j, 1)].rearrange("o p c -> (o p) c"), yo[:, :]).then_inc(k.y_out[0], 16)
                pool.wait_ge(k.y_out[0], 16 * (NH + KT))

            @block.tensor
            def _(pe):
                for s in range(4):
                    pe.sem_inc(freed[s], 1)
                pe.sem_inc(sp_.used, 2)
                pe.wait_ge(state_in, 16)
                for kt in range(KT):
                    mm = pe.transpose(ps[:, 0, kt * 16:(kt + 1) * 16], sn[:, kt * P:(kt + 1) * P], k.ident[0:16, 0:16])
                mm.then_inc(turned, 1)
                pe.wait_ge(st_kept, 1)
                with pe.Fori(0, KT) as j:
                    for s in range(4):
                        pe.wait_ge(freed[s], j + 1)
                        sp_.matmuls(pe, s, j * 4, 2 * s)
                pe.wait_ge(ydone, KT + 1)
                for s in range(4):
                    pe.wait_ge(freed[s], KT + 1)
                for kt in range(KT):
                    mm = pe.transpose(ps[0:2 + NS, kt // 4, (kt % 4) * P:(kt % 4 + 1) * P], cu[:, kt, :], k.ident)
                mm.then_inc(cu_turned, 1)

            def halves(s):
                return ps[:, 2 * s:2 * s + 2, 0:HC]

            def two(t):
                return t.rearrange("p (a c) -> p a c", c=HC)

            @block.scalar
            def _(act):
                act.dma_start(sn[:, :], k.i["state_conv"][0].rearrange("s w d -> (s w) d")).then_inc(state_in, 16)
                act.dma_start(k.o["conv_s"][0, :, 0], k.i["state_conv"][0, :, 1]).then_inc(out, 16)
                act.wait_ge(turned, 1)
                nc.scalar.activation(stT[:, :, :], ps[:, 0, 0:KT * 16].rearrange("p (k w) -> p k w", w=16), ACT.Copy).then_inc(st_kept, 1)
                def channels(j, last=False):
                    sp_.hi(act, 1, j * 4)
                    act.wait_ge(ydone, j + 1)
                    act.wait_ge(sp_.used, j * 4 + 3)
                    nc.scalar.activation(two(hh[:, :]), halves(0), ACT.Copy).then_inc(freed[0], 1)
                    sp_.hi(act, 2, j * 4)
                    act.wait_ge(sp_.used, j * 4 + 4)
                    nc.scalar.activation(two(bg[:, :]), halves(1), ACT.Copy).then_inc(freed[1], 1)
                    sp_.hi(act, 3, j * 4)
                    if not last:
                        sp_.hi(act, 4, j * 4)
                    act.wait_ge(sp_.used, j * 4 + 6)
                    nc.scalar.activation(two(z[:, :]), halves(3), ACT.Copy)
                    nc.scalar.activation(two(e[:, :]), halves(3), ACT.Exp, scale=-1.0).then_inc(freed[3], 1)

                sp_.hi(act, 0, 0)
                with act.Fori(0, KT - 1) as j:
                    channels(j)
                channels(KT - 1, True)

            @block.vector
            def _(dve):
                dve.wait_ge(zeroed, 1)
                dve.wait_ge(st_kept, 1)
                dve.nop().then_inc(ydone, 1)
                N = 8

                def channels(j, last=False, first=False):

                    def vec(col, base=0):
                        return k.vT[:, bass.ds(j + base + col, 1)]

                    def tap(w):
                        return vec(CW + w * KT)

                    for s in range(1, 4):
                        sp_.lo(dve, s, j * 4)
                    if not last:
                        sp_.lo(dve, 4, j * 4)
                    us = u[:, 2 + T:2 + TC]
                    st0 = stT[:, bass.ds(j, 1), :].rearrange("p o (s w) -> p (o s) w", w=2)
                    dve.wait_ge(freed[0], j + 2)
                    dve.wait_ge(sp_.used, j * 4 + 5)
                    dve.tensor_tensor(two(u[:, 2:2 + TC]), halves(2), two(hh[:, :]), ALU.mult).then_inc(freed[2], 1)
                    dve.wait_ge(freed[2], j + 2)
                    dve.tensor_copy(cu[:, bass.ds(j, 1), 0:2].rearrange("p o c -> p (o c)"), u[:, T:T + 2]).then_inc(step, 1)
                    dve.tensor_copy(cu[:, bass.ds(j, 1), 2:2 + NS].rearrange("p o c -> p (o c)"), us).then_inc(step, 1)
                    dve.tensor_scalar(y[:, 0:T], u[:, 0:T], tap(0), vec(CBI), ALU.mult, ALU.add).then_inc(step, 1)
                    dve.tensor_scalar(y[:, T:TC], st0[:, :, 0], tap(0), vec(CBI), ALU.mult, ALU.add).then_inc(step, 1)
                    dve.wait_ge(step, j * N + 4)
                    dve.scalar_tensor_tensor(out=y[:, 0:T], in0=u[:, 1:1 + T], scalar=tap(1), in1=y[:, 0:T], op0=ALU.mult, op1=ALU.add).then_inc(step, 1)
                    dve.scalar_tensor_tensor(out=y[:, T:TC], in0=st0[:, :, 1], scalar=tap(1), in1=y[:, T:TC], op0=ALU.mult, op1=ALU.add).then_inc(step, 1)
                    dve.wait_ge(step, j * N + 6)
                    dve.scalar_tensor_tensor(out=y[:, :], in0=u[:, 2:2 + TC], scalar=tap(2), in1=y[:, :], op0=ALU.mult, op1=ALU.add).then_inc(step, 1)
                    dve.wait_ge(zstep, j * 2 + 1)
                    dve.reciprocal(e[:, :], e[:, :]).then_inc(zrecip, 1)
                    dve.wait_ge(zstep, j * 2 + 2)
                    dve.wait_ge(freed[1], j + 2)
                    dve.tensor_tensor(e[:, :], e[:, :], bg[:, :], ALU.mult).then_inc(step, 1)
                    dve.wait_ge(step, j * N + 8)
                    if not first:
                        dve.wait_ge(k.y_out[0], j * 16 + 16 * NH)
                    dve.tensor_tensor(yo[:, :], e[:, :], y[:, :], ALU.mult).then_inc(ydone, 1)
                sp_.lo(dve, 0, 0)
                channels(0, first=True)
                with dve.Fori(1, KT - 1) as j:
                    channels(j)
                channels(KT - 1, last=True)
                dve.wait_ge(cu_turned, 1)
                dve.tensor_copy(rows[:, :], ps[0:2 + NS, 0:4, :].rearrange("p b c -> p (b c)")).then_inc(cu_kept, 1)
    k.ring += 64


def stage_final(k):
    nc, ps = k.nc, k.psum
    turned, kept_a, kept_v, out = (k.sem("fi_" + n) for n in ("turned", "kept_a", "kept_v", "out"))
    with ExitStack() as ctx:
        rows = k.sb("fi_rows", [P, TT + 1, D], ctx=ctx)
        with nc.Block() as block:

            @block.tensor
            def _(pe):
                for i in range(TT + 1):
                    w = P if i < TT else NS
                    if i >= 2:
                        pe.wait_ge(kept_a, i - 1)
                        pe.wait_ge(kept_v, i - 1)
                    for kt in range(KT):
                        mm = pe.transpose(ps[0:w, 4 * (i % 2) + kt // 4, (kt % 4) * P:(kt % 4 + 1) * P], k.hT[:, kt, i * P:i * P + w], k.ident)
                    mm.then_inc(turned, 1)

            @block.scalar
            def _(act):
                for i in range(TT + 1):
                    w = P if i < TT else NS
                    act.wait_ge(turned, i + 1)
                    nc.scalar.activation(rows[0:w, i, 0:1024].rearrange("p (b c) -> p b c", c=512), ps[0:w, 4 * (i % 2):4 * (i % 2) + 2, :], ACT.Copy).then_inc(kept_a, 1)

            @block.vector
            def _(dve):
                for i in range(TT + 1):
                    w = P if i < TT else NS
                    dve.wait_ge(turned, i + 1)
                    dve.tensor_copy(rows[0:w, i, 1024:2048].rearrange("p (b c) -> p b c", c=512), ps[0:w, 4 * (i % 2) + 2:4 * (i % 2) + 4, :]).then_inc(kept_v, 1)

            @block.sync
            def _(sp):
                for i in range(TT + 1):
                    sp.wait_ge(kept_a, i + 1)
                    sp.wait_ge(kept_v, i + 1)
                    if i < TT:
                        sp.dma_start(k.o["y_p"][0, i * P:(i + 1) * P, :], rows[:, i, :]).then_inc(out, 16)
                    else:
                        sp.dma_start(k.o["y_s"][:, 0, :], rows[0:NS, i, :]).then_inc(out, 16)
                sp.wait_ge(out, 16 * (TT + 1))


def build(nc, ins, outs):
    with ExitStack() as ctx:
        k = Kernel(nc, ctx, ins, outs)
        k.const = k.sb("const", [P, C_ALL])
        k.ident = k.const[:, C_ID:C_ID + P]
        k.onesb = k.sb("ones", [P, P])
        k.ones = k.onesb[:, :]
        k.xT = k.sb("xT", [P, KT, TC])
        k.cT = k.sb("cT", [P, KT, C9])
        k.vT = k.sb("vT", [P, 208])
        k.adaT = k.sb("adaT", [P, 48, C9])
        k.w = k.sb("w", [P, 4, 2048])
        k.bias_skew = k.dram("bias_skew", [2 * NH * P * (BREV + 1)])
        k.vcmp_rows = k.dram("vcmp_rows", [G, 16, P])
        k.proj = k.dram("proj", [NTILES, P, TC])
        k.y_rows = k.dram("y_rows", [KT, P, TC])
        k.gate_rows = k.dram("gate_rows", [NS, NGW])
        k.w_free = k.sem("w_free")
        k.y_out = [k.sem(f"y_out{b}") for b in range(2)]
        k.w_in = [k.sem(f"w_in{s}") for s in range(4)]
        k.stored = [k.sem(f"pj_stored{s}") for s in range(4)]
        k.s_small, k.s_misc, k.s_misc2, k.s_ones, k.s_sig = (k.sem(n) for n in ("small", "misc", "misc2", "ones_set", "sigmoid"))
        k.settled = {e.engine: k.sem(f"settled_{n}") for n, e in (("pe", nc.tensor), ("dve", nc.vector), ("pool", nc.gpsimd))}
        k.ring = 0
        with ExitStack() as layer0:
            k.pages = k.sb("pages", [1, P], I32, ctx=layer0)
            k.table = k.sb("table", [32, 2 * NH], ctx=layer0)
            k.hot = k.sb("hot", [32, O_ALL], ctx=layer0)
            k.gw = k.sb("gw", [P, TT, NGW], ctx=layer0)
            k.gws = k.sb("gws", [NS, NGW], ctx=layer0)
            with k.stage():
                stage_load(k)
            with k.stage():
                stage_ada(k, 0)
            with ExitStack() as projecting:
                k.split_buffers("0", projecting)
                with k.stage():
                    stage_norm(k, 0)
                with k.stage():
                    stage_project(k)
            with k.stage():
                stage_rows(k)
            k.sT = k.sb("sT", [P, GW, NS], ctx=layer0)
            k.qpa, k.qpb = k.sb("qpa", [P, NS * G * 64], ctx=layer0), k.sb("qpb", [P, NS * G * 64], ctx=layer0)
            k.ga_s, k.wi_s = k.sb("ga_s", [NS * NH, 3], ctx=layer0), k.sb("wi_s", [P, 1], ctx=layer0)
            k.wsel = k.sb("wsel", [P, NS], ctx=layer0)
            k.mask = k.sb("mask", [P, off(TT)], ctx=layer0)
            k.oS = k.sb("oS", [P, 2, NS * NH], ctx=layer0)
            k.kcmp, k.vcmp = k.sb("kcmp", [P, NS + 1, P], ctx=layer0), k.sb("vcmp", [P, NS + 1, P], ctx=layer0)
            with ExitStack() as sample:
                k.mask_s = k.sb("mask_s", [NS, PAST + 1], ctx=sample)
                with ExitStack() as indexing:
                    k.qpi = k.sb("qpi", [P, NS * P], ctx=indexing)
                    k.zeros = k.sb("zeros", [P, P], ctx=indexing)
                    with k.stage():
                        stage_sample_queries(k)
                    with k.stage():
                        stage_index_prompt(k)
                    with k.stage():
                        stage_index_sample(k)
                k.hct = k.sb("hct", [P, CH], ctx=sample)
                k.msel = k.sb("msel", [NS * G, 33], ctx=sample)
                k.tabs = k.sb("tabs", [32, 2, NS * NH], ctx=sample)
                with k.stage():
                    stage_compress(k, "k")
                with k.stage():
                    stage_compress(k, "v")
                with k.stage():
                    stage_compressed_sample(k)
                with k.stage():
                    stage_attend_sample(k, "slc")
                with k.stage():
                    stage_attend_sample(k, "win")
                with k.stage():
                    stage_attend_sample(k, "dsa")
            with k.stage():
                stage_attend_prompt(k, 0)
            with k.stage():
                stage_attend_prompt(k, 1)
        with ExitStack() as closing:
            k.split_buffers("1", closing)
            with k.stage():
                stage_out(k, 0)
            with k.stage():
                stage_ada(k, 1)
            with k.stage():
                stage_norm(k, 1)
            with k.stage():
                stage_conv(k)
            with k.stage():
                stage_out(k, 1)
        k.hT = k.sb("hT", [P, KT, TC])
        with k.stage():
            stage_norm(k, 2)
        with k.stage():
            stage_final(k)


OUTS = [("y_p", (1, T, D)), ("y_s", (NS, 1, D))]
for _n in ("cmp_k", "cmp_v", "slc_k", "slc_v", "win_k", "win_v", "dsa_k", "dsa_v"):
    OUTS += [(_n + "_p", (1, 1, T, G, P)), (_n + "_s", (1, NS, WIN if _n[:3] == "win" else 1, G, P))]
OUTS += [("idx_k_p", (1, 1, T, P)), ("idx_k_s", (1, NS, 1, P)), ("conv_p", (1, 1, 2, D)), ("conv_s", (1, NS, 2, D))]


def shape_constants():
    import numpy as np
    c = np.zeros((P, C_ALL), np.float32)
    c[:, C_ID:C_ID + P] = np.eye(P)
    for row in range(NS * NH):
        c[row, C_BD8 + row // NH] = 1
        c[row, C_R16 + row // 4] = 1
        c[row // 4, C_RT + row] = 1
        c[row // NH, C_E8 + row] = 1
    for row in range(P):
        c[row, C_BD16 + row // NI] = 1

    def bucket(n):
        far = 16 + (np.log(np.maximum(n, 16).astype(np.float32) / np.float32(16)) / np.float32(4.1588830833596715) * np.float32(16)).astype(np.int32)
        return np.where(n < 16, n, np.minimum(far, 31))

    hot = np.zeros((32, O_ALL), np.float32)
    hot[bucket(T - 1 - np.arange(T)), O_P + np.arange(T)] = 1
    hot[bucket(PAST - np.arange(PAST + 1)), O_S + np.arange(PAST + 1)] = 1
    hot[bucket(PAST - (CB * np.arange(NCB) + CB - 1)), O_C + np.arange(NCB)] = 1
    return {"const": c, "hot": hot}


def kernel(**inputs):
    import numpy as _np
    import concourse.bacc as _bacc
    from concourse.bass_utils import run_bass_kernel_spmd as _run

    nc = _bacc.Bacc("TRN2", target_bir_lowering=False, num_devices=1)
    arrays, ins, outs = {}, {}, {}
    for name, a in list(inputs.items()) + list(shape_constants().items()):
        a = _np.ascontiguousarray(a)
        arrays[f"in_{name}"] = a
        ins[name] = nc.dram_tensor(f"in_{name}", a.shape, mybir.dt.from_np(a.dtype), kind="ExternalInput").ap()
    for name, shape in OUTS:
        outs[name] = nc.dram_tensor(f"out_{name}", shape, F32, kind="ExternalOutput").ap()
    build(nc, ins, outs)
    r = _run(nc, [arrays], core_ids=[0])
    return tuple(r.results[0][f"out_{name}"] for name, _ in OUTS)
```

```python
from contextlib import ExitStack, contextmanager

import concourse.bass as bass
from concourse import mybir

F32 = mybir.dt.float32
F32R = mybir.dt.float32r
I32 = mybir.dt.int32
ALU = mybir.AluOpType
ACT = mybir.ActivationFunctionType
AX = mybir.AxisListType.X

P = 128
D = 2048
KT = D // P
T = 512
TT = T // P
NS = 8
TC = T + NS
HC = TC // 2
C9 = 1 + NS
G = 2
NH = 8
NI = 16
PAST = 2048
PG = 16
NPOOL = 160
WIN = 512
CB = 32
NCB = PAST // CB
CH = 256
TOPK_P = 128
TOPK_S = 256
NEG = -1e30
TAKEN = -3e38
SCALE = P ** -0.5
EPS = 1e-6

RUNS = [(0, 0, 20), (20, 2584, 36), (56, 7208, 9)]
QA, KC, VC, KS, VS, KW, VW, ZA, QB, KB, VB, QI, KI, ZB, GW = 0, 8, 10, 12, 14, 16, 18, 20, 28, 36, 38, 40, 56, 57, 65
NTILES = 66
GA_COL, WI_COL = 2560, 7192
NGA, NGW = 24, 40
WI_ROW = P - NI

C_ID, C_BD8, C_R16, C_BD16, C_END = 0, 128, 136, 152, 160
C_E8 = C_END + 64
C_RT = C_END
C_ALL = C_E8 + 64
O_P, O_S, O_C, O_ALL = 0, 512, 512 + 2049, 512 + 2049 + 64

BREV = 640


class Kernel:

    def __init__(self, nc, ctx, ins, outs):
        self.nc, self.ctx, self.i, self.o = nc, ctx, ins, outs
        self.stages, self.stage_sems = 0, []
        self.psum = ctx.enter_context(nc.psum_tensor("psum", [P, 8, 512], F32))

    def sb(self, name, shape, dt=F32, ctx=None):
        return (ctx or self.ctx).enter_context(self.nc.sbuf_tensor(name, shape, dt))

    def sem(self, name):
        handle = self.nc.alloc_semaphore(name=f"{name}_{self.stages}")
        if self.stages:
            self.stage_sems.append(handle)
        return handle

    @contextmanager
    def stage(self):
        self.stages += 1
        self.stage_sems = []
        yield
        numbers = sorted(s.num for s in self.stage_sems)
        while numbers:
            n = next((i for i in range(1, len(numbers)) if numbers[i] != numbers[0] + i), len(numbers))
            self.nc.gpsimd.sem_clear(range(numbers[0], numbers[0] + n))
            numbers = numbers[n:]
        for s in self.stage_sems:
            self.nc.release_semaphore(s)
        self.nc.all_engine_barrier()

    def split_buffers(self, tag, ctx):
        self.hh, self.hl = (self.sb(f"{n}{tag}", [P, KT, TC], F32R, ctx) for n in ("h_high", "h_low"))
        self.wh, self.wl = (self.sb(f"{n}{tag}", [P, 2, KT * P], F32R, ctx) for n in ("w_high", "w_low"))

    def dram(self, name, shape):
        return self.nc.dram_tensor(name, shape, F32, kind="Internal").ap()


def stage_load(k):
    nc, ps = k.nc, k.psum
    loaded, table_in = k.sem("ld_loaded"), k.sem("ld_table")
    turned, kept = k.sem("ld_turned"), k.sem("ld_kept")
    bias_mm, bias_row, bias_out = k.sem("ld_bias_mm"), k.sem("ld_bias_row"), [k.sem("ld_bias_out0"), k.sem("ld_bias_out1")]
    with ExitStack() as ctx:
        xn = k.sb("xn", [P, TT, D], ctx=ctx)
        xs = k.sb("xs", [NS, D], ctx=ctx)
        cn = k.sb("cn", [C9, D], ctx=ctx)
        ba = k.sb("ba", [96, P], ctx=ctx)
        vecs = k.sb("vecs", [112, P], ctx=ctx)
        rows = k.sb("bias_rows", [P, 2, BREV], ctx=ctx)
        with nc.Block() as block:

            @block.sync
            def _(sp):
                sp.dma_start(k.const[:, :], k.i["const"]).then_inc(loaded, 16)
                sp.dma_start(k.pages[:, :], k.i["page_table"].rearrange("(o s) p -> o (s p)", o=1)).then_inc(loaded, 16)
                sp.dma_start(xs[:, :], k.i["x_sample"][:, 0, :]).then_inc(loaded, 16)
                sp.dma_start(cn[0:1, :], k.i["c_prompt"]).then_inc(loaded, 16)
                sp.dma_start(cn[1:C9, :], k.i["c_sample"]).then_inc(loaded, 16)
                sp.dma_start(ba[:, :], k.i["b_ada"].rearrange("l (a p) -> (l a) p", p=P)).then_inc(loaded, 16)
                sp.dma_start(vecs[0:32, :], k.i["norm_g"].rearrange("l (a p) -> (l a) p", p=P)).then_inc(loaded, 16)
                sp.dma_start(vecs[32:48, :], k.i["final_norm_g"].rearrange("(a p) -> a p", p=P)).then_inc(loaded, 16)
                sp.dma_start(vecs[48:96, :], k.i["conv_w"].rearrange("o w (a p) -> (o w a) p", p=P)).then_inc(loaded, 16)
                sp.dma_start(vecs[96:112, :], k.i["conv_b"].rearrange("o (a p) -> (o a) p", p=P)).then_inc(loaded, 16)
                sp.dma_start(xn[:, :, :], k.i["x_prompt"][0].rearrange("(i p) d -> p i d", p=P)).then_inc(loaded, 16)
                for h in range(2 * NH):
                    sp.wait_ge(bias_row, 2 * h + 2)
                    sp.dma_start(bass.AP(k.bias_skew.tensor, h * P * (BREV + 1), [[BREV + 1, P], [1, BREV]]), rows[:, h % 2, :]).then_inc(bias_out[h % 2], 16)

            @block.tensor
            def _(pe):
                pe.sem_inc(k.w_free, 4)
                pe.wait_ge(loaded, 11 * 16)
                for kt in range(KT):
                    if kt >= 4:
                        pe.wait_ge(kept, kt - 3)
                    for i in range(TT):
                        mm = pe.transpose(ps[:, kt % 4, i * P:(i + 1) * P], xn[:, i, kt * P:(kt + 1) * P], k.ident)
                    mm.then_inc(turned, 1)
                for kt in range(KT):
                    mm = pe.transpose(ps[:, 4, kt * NS:(kt + 1) * NS], xs[:, kt * P:(kt + 1) * P], k.ident[0:NS, 0:NS])
                mm.then_inc(turned, 1)
                for kt in range(KT):
                    mm = pe.transpose(ps[:, 5, kt * C9:(kt + 1) * C9], cn[:, kt * P:(kt + 1) * P], k.ident[0:C9, 0:C9])
                mm.then_inc(turned, 1)
                pe.transpose(ps[:, 6, 0:96], ba[:, :], k.ident[0:96, 0:96])
                pe.transpose(ps[:, 6, 96:208], vecs[:, :], k.ident[0:112, 0:112]).then_inc(turned, 1)
                pe.wait_ge(table_in, 32)
                pe.wait_ge(kept, KT + 3)
                for h in range(2 * NH):
                    if h >= 2:
                        pe.wait_ge(bias_row, 2 * h - 2)
                    pe.matmul(ps[:, 6 + h % 2, :], k.table[:, h:h + 1].broadcast_to([32, P]), k.hot[:, O_P:O_P + T], start=True, stop=True).then_inc(bias_mm, 1)

            @block.scalar
            def _(act):
                act.dma_start(k.table[:, :], k.i["rel_bias"]).then_inc(table_in, 16)
                act.dma_start(k.hot[:, :], k.i["hot"]).then_inc(table_in, 16)
                act.wait_ge(turned, KT + 1)
                nc.scalar.activation(k.xT[:, :, T:TC], ps[:, 4, 0:KT * NS].rearrange("p (k s) -> p k s", s=NS), ACT.Copy).then_inc(k.s_vectors_kept, 1)
                act.wait_ge(turned, KT + 2)
                nc.scalar.activation(k.cT[:, :, :], ps[:, 5, 0:KT * C9].rearrange("p (k s) -> p k s", s=C9), ACT.Copy).then_inc(k.s_vectors_kept, 1)
                act.wait_ge(turned, KT + 3)
                nc.scalar.activation(k.vT[:, :], ps[:, 6, 0:208], ACT.Copy).then_inc(k.s_vectors_kept, 1)

            @block.gpsimd
            def _(pool):
                pool.memset(k.onesb[:, :], 1.0).then_inc(k.s_ones, 1)
                pool.wait_ge(k.s_ones, 1)

            @block.vector
            def _(dve):
                dve.memset(rows[:, 0, T:BREV], NEG).then_inc(bias_row, 1)
                dve.memset(rows[:, 1, T:BREV], NEG).then_inc(k.s_tail_set, 1)
                for kt in range(KT):
                    dve.wait_ge(turned, kt + 1)
                    dve.tensor_copy(k.xT[:, kt, 0:T], ps[:, kt % 4, :]).then_inc(kept, 1)
                dve.wait_ge(k.s_vectors_kept, 3)
                dve.wait_ge(k.s_tail_set, 1)
                dve.nop().then_inc(kept, 3)
                for h in range(2 * NH):
                    dve.wait_ge(bias_mm, h + 1)
                    if h >= 2:
                        dve.wait_ge(bias_out[h % 2], 16 * (h // 2))
                    dve.tensor_copy(rows[:, h % 2, 0:T], ps[:, 6 + h % 2, :]).then_inc(bias_row, 1 if h == 0 else 2)
                for b in range(2):
                    dve.wait_ge(bias_out[b], 16 * NH)


class Split:

    def __init__(self, k):
        self.k, self.r = k, k.ring
        self.high, self.used = k.sem("sp_high"), k.sem("sp_used")

    def hi(self, act, s, j4):
        k, n = self.k, self.r + s
        act.wait_ge(k.w_in[n % 4], j4 * 4 + 16 * (n // 4 + 1))
        act.wait_ge(self.used, j4 + (s + 1))
        act.activation(k.wh[:, s % 2, :], k.w[:, n % 4, :], ACT.Copy).then_inc(self.high, 1)

    def lo(self, dve, s, j4):
        k, n = self.k, self.r + s
        dve.wait_ge(self.high, j4 + (s + 1))
        dve.tensor_tensor(k.wl[:, s % 2, :], k.w[:, n % 4, :], k.wh[:, s % 2, :].bitcast(F32), ALU.subtract).then_inc(k.w_free, 1)

    def matmuls(self, pe, s, j4, banks, ready=None):
        k, n = self.k, self.r + s
        pe.wait_ge(k.w_free, j4 + (n + 5))
        wh, wl = (t[:, s % 2, :].rearrange("p (a n) -> p a n", n=P) for t in (k.wh, k.wl))
        for kt in range(KT):
            if ready:
                pe.wait_ge(ready[0], kt + ready[1])
            for m, (w, x) in enumerate(((wh, k.hh), (wh, k.hl), (wl, k.hh))):
                for hf in range(2):
                    mm = pe.matmul(k.psum[:, banks + hf, 0:HC], w[:, kt, :], x[:, kt, hf * HC:(hf + 1) * HC], start=(kt == 0 and m == 0), stop=(kt == KT - 1 and m == 2))
        mm.then_inc(self.used, 1)


def stage_ada(k, layer):
    nc, ps = k.nc, k.psum
    rows_kept, turned, kept, cleared, c_high, c_low = (k.sem(f"ada_{n}") for n in ("rows_kept", "turned", "kept", "cleared", "c_high", "c_low"))
    high, low, used = (k.sem(f"ada_{n}") for n in ("high", "low", "used"))
    r = k.ring
    HW = KT * P // 2
    wh, wl = (t[:, :, :].rearrange("p b (h n) -> p (b h) n", n=HW) for t in (k.wh, k.wl))

    def split_high(act, s, j8):
        n = r + s
        act.wait_ge(k.w_in[n % 4], j8 * 32 + 16 * (n // 4 + 1))
        for hf in range(2):
            act.wait_ge(used, j8 * 16 + (2 * s + hf + 1))
            act.activation(wh[:, (2 * s + hf) % 4, :], k.w[:, n % 4, hf * HW:(hf + 1) * HW], ACT.Copy).then_inc(high, 1)

    def split_low(dve, s, j8):
        n = r + s
        for hf in range(2):
            dve.wait_ge(high, j8 * 16 + (2 * s + hf + 1))
            dve.tensor_tensor(wl[:, (2 * s + hf) % 4, :], k.w[:, n % 4, hf * HW:(hf + 1) * HW], wh[:, (2 * s + hf) % 4, :].bitcast(F32), ALU.subtract).then_inc(k.w_free if hf else low, 1)

    with ExitStack() as ctx:
        rows = k.sb(f"ada_rows{layer}", [C9, 2, 512], ctx=ctx)
        ch, cl = (k.sb(f"ada_{n}{layer}", [P, KT, P], F32R, ctx) for n in ("c_high", "c_low"))
        with nc.Block() as block:

            @block.sync
            def _(sp):
                with sp.Fori(0, 12) as j:
                    for s in range(4):
                        sp.wait_ge(k.w_free, j * 4 + (r + s + 1))
                        src = k.i["w_ada"][layer, s * 512:(s + 1) * 512, bass.ds(j * 512, 512)]
                        sp.dma_start(k.w[:, (r + s) % 4, :].rearrange("p (a n) -> p a n", n=512), src.rearrange("(a p) n -> p a n", p=P)).then_inc(k.w_in[(r + s) % 4], 16)

            @block.tensor
            def _(pe):
                pe.sem_inc(kept, 2)
                pe.sem_inc(used, 4)
                pe.wait_ge(c_low, 1)
                with pe.Fori(0, 6) as j:
                    for c in range(2):
                        for q in range(4):
                            s = c * 4 + q
                            for b in range(2):
                                if b == 0:
                                    pe.wait_ge(low, j * 8 + (s + 1))
                                else:
                                    pe.wait_ge(k.w_free, j * 8 + (r + s + 5))
                                for a in range(2):
                                    for m, (x, w) in enumerate(((ch, wh), (cl, wh), (ch, wl))):
                                        mm = pe.matmul(ps[:, c, :], x[:, q * 4 + b * 2 + a, :], w[:, (2 * s + b) % 4, a * 512:(a + 1) * 512], start=(q + b + a + m == 0), stop=(q + b + a == 5 and m == 2))
                                mm.then_inc(used, 1)
                        pe.wait_ge(rows_kept, j * 2 + (c + 1))
                        pe.wait_ge(kept, j * 2 + (c + 1))
                        settle(k, pe)
                        for f in range(4):
                            mm = pe.transpose(ps[:, 2 + c, f * C9:(f + 1) * C9], rows[:, c, f * P:(f + 1) * P], k.ident[0:C9, 0:C9])
                        mm.then_inc(turned, 1)

            @block.scalar
            def _(act):

                def chunks(j8, last=False):
                    for s in range(8):
                        if not (last and s == 7):
                            split_high(act, s + 1, j8)
                        if s % 4 == 3:
                            act.wait_ge(used, j8 * 16 + (2 * s + 6))
                            nc.scalar.activation(rows[:, s // 4, :], ps[0:C9, s // 4, :], ACT.Copy).then_inc(rows_kept, 1)

                act.wait_ge(cleared, 1)
                nc.scalar.activation(ch[:, :, 0:C9], k.cT[:, :, :], ACT.Copy).then_inc(c_high, 1)
                split_high(act, 0, 0)
                with act.Fori(0, 5) as j:
                    chunks(j)
                chunks(5, last=True)

            @block.vector
            def _(dve):

                def chunks(j8, last=False):
                    for s in range(8):
                        if not (last and s == 7):
                            split_low(dve, s + 1, j8)
                        if s % 4 == 3:
                            c = s // 4
                            dve.wait_ge(turned, j8 * 2 + (c + 1))
                            dve.tensor_tensor(k.adaT[:, bass.ds(j8 * 8 + c * 4, 4), :], ps[:, 2 + c, 0:4 * C9].rearrange("p (f c) -> p f c", c=C9),
                                              k.vT[:, bass.ds(j8 * 8 + (layer * 48 + c * 4), 4)].unsqueeze(2).broadcast_to([P, 4, C9]), ALU.add).then_inc(kept, 1)

                dve.memset(ch[:, :, :].bitcast(F32), 0.0)
                dve.memset(cl[:, :, :].bitcast(F32), 0.0).then_inc(cleared, 1)
                dve.wait_ge(c_high, 1)
                dve.tensor_tensor(cl[:, :, 0:C9], k.cT[:, :, :], ch[:, :, 0:C9].bitcast(F32), ALU.subtract).then_inc(c_low, 1)
                split_low(dve, 0, 0)
                with dve.Fori(0, 5) as j:
                    chunks(j)
                chunks(5, last=True)
                dve.wait_ge(kept, 14)
    k.ring += 48


def load_weights(k, eng, n, cols, slot=None):
    slot = n % 4 if slot is None else slot
    eng.wait_ge(k.w_free, n + 1)
    eng.dma_start(k.w[:, slot, :].rearrange("p (a n) -> p a n", n=P), cols.rearrange("(a p) n -> p a n", p=P)).then_inc(k.w_in[slot], 16)


class Norm:

    def __init__(self, k, layer, ctx, hp=None):
        self.k, self.layer, self.hp = k, layer, hp
        self.sq_done, self.sum_mm, self.step, self.root, self.scaled, self.high, self.fin = (k.sem(f"nm_{n}") for n in ("square", "sum", "step", "root", "scaled", "high", "fin"))
        self.sq = k.sb(f"nm_sq{layer}", [P, 2, TC], ctx=ctx)
        self.v = k.sb(f"nm_v{layer}", [P, TC], ctx=ctx)
        self.t = k.sb(f"nm_t{layer}", [P, TC], ctx=ctx)
        self.rs = k.sb(f"nm_r{layer}", [P, TC], ctx=ctx)
        self.ab = k.sb(f"nm_ab{layer}", [P, KT, C9], ctx=ctx)
        self.hs = k.sb(f"nm_hs{layer}", [P, KT, NS], ctx=ctx)

    def squares(self, act):
        k = self.k
        with act.Fori(0, KT // 2) as j:
            for b in range(2):
                act.wait_ge(self.sum_mm, j * 2 + (b + 1))
                act.activation(self.sq[:, b, :], k.xT[:, bass.ds(j * 2 + b, 1), :].rearrange("p o c -> p (o c)"), ACT.Square).then_inc(self.sq_done, 1)
        act.wait_ge(self.step, 1)
        act.activation(self.rs[:, :], self.v[:, :], ACT.Sqrt).then_inc(self.root, 1)

    def high_parts(self, act):
        k = self.k
        act.wait_ge(self.scaled, 1)
        act.activation(k.hh[:, :, T:TC], self.hs[:, :, :], ACT.Copy).then_inc(self.high, 1)
        for kt in range(KT):
            act.wait_ge(self.scaled, kt + 2)
            act.activation(k.hh[:, kt, 0:T], self.hp[:, kt % 4, 0:T], ACT.Identity, bias=k.adaT[:, kt, 0:1]).then_inc(self.high, 1)

    def sums(self, pe):
        k = self.k
        pe.sem_inc(self.sum_mm, 2)
        for kt in range(KT):
            pe.wait_ge(self.sq_done, kt + 1)
            for hf in range(2):
                mm = pe.matmul(k.psum[:, hf, 0:HC], k.ones, self.sq[:, kt % 2, hf * HC:(hf + 1) * HC], start=(kt == 0), stop=(kt == KT - 1))
            mm.then_inc(self.sum_mm, 1)

    def normalise(self, dve, before_low=None):
        k, layer, step, fin, high, scaled = self.k, self.layer, self.step, self.fin, self.high, self.scaled
        v, t, rs, ab, hs, hp = self.v, self.t, self.rs, self.ab, self.hs, self.hp
        n = 0

        def then(ins):
            nonlocal n
            n += 1
            ins.then_inc(step, 1)
            return n

        dve.wait_ge(self.sum_mm, KT + 2)
        for hf in range(2):
            ins = dve.tensor_scalar(v[:, hf * HC:(hf + 1) * HC], k.psum[:, hf, 0:HC], 1.0 / D, EPS, ALU.mult, ALU.add)
        then(ins)
        if layer < 2:
            dve.scalar_tensor_tensor(out=ab[:, :, :], in0=k.adaT[:, KT:2 * KT, :], scalar=1.0,
                                     in1=k.vT[:, 96 + layer * KT:96 + (layer + 1) * KT].unsqueeze(2).broadcast_to([P, KT, C9]), op0=ALU.add, op1=ALU.mult)
        dve.wait_ge(self.root, 1)
        dve.wait_ge(step, then(dve.reciprocal(t[:, :], rs[:, :])))
        dve.wait_ge(step, then(dve.tensor_tensor(rs[:, :], t[:, :], t[:, :], ALU.mult)))
        dve.wait_ge(step, then(dve.tensor_tensor(rs[:, :], rs[:, :], v[:, :], ALU.mult)))
        dve.wait_ge(step, then(dve.tensor_scalar(rs[:, :], rs[:, :], -0.5, 1.5, ALU.mult, ALU.add)))
        dve.wait_ge(step, then(dve.tensor_tensor(rs[:, :], rs[:, :], t[:, :], ALU.mult)))
        if layer == 2:
            for kt in range(KT):
                dve.scalar_tensor_tensor(out=k.hT[:, kt, :], in0=k.xT[:, kt, :], scalar=k.vT[:, 128 + kt:129 + kt], in1=rs[:, :], op0=ALU.mult, op1=ALU.mult).then_inc(fin, 1)
            dve.wait_ge(fin, KT)
            return
        dve.wait_ge(step, then(dve.tensor_tensor(hs[:, :, :], k.xT[:, :, T:TC], rs[:, T:TC].unsqueeze(1).broadcast_to([P, KT, NS]), ALU.mult)))
        dve.wait_ge(step, then(dve.tensor_tensor(hs[:, :, :], hs[:, :, :], ab[:, :, 1:C9], ALU.mult)))
        dve.tensor_tensor(hs[:, :, :], hs[:, :, :], k.adaT[:, 0:KT, 1:C9], ALU.add).then_inc(scaled, 1)
        before_low(dve)
        for kt in range(KT + 2):
            if kt < KT:
                if kt >= 4:
                    dve.wait_ge(fin, kt - 2)
                dve.scalar_tensor_tensor(out=hp[:, kt % 4, 0:T], in0=k.xT[:, kt, 0:T], scalar=ab[:, kt, 0:1], in1=rs[:, 0:T], op0=ALU.mult, op1=ALU.mult).then_inc(scaled, 1)
            if kt == 0:
                dve.wait_ge(high, 1)
                dve.tensor_tensor(k.hl[:, :, T:TC], hs[:, :, :], k.hh[:, :, T:TC].bitcast(F32), ALU.subtract).then_inc(fin, 1)
            if kt >= 2:
                q = kt - 2
                dve.wait_ge(high, q + 2)
                dve.scalar_tensor_tensor(out=k.hl[:, q, 0:T], in0=hp[:, q % 4, 0:T], scalar=k.adaT[:, q, 0:1], in1=k.hh[:, q, 0:T].bitcast(F32), op0=ALU.add, op1=ALU.subtract).then_inc(fin, 1)


def stage_final_norm(k):
    with ExitStack() as ctx:
        norm = Norm(k, 2, ctx)
        with k.nc.Block() as block:

            @block.scalar
            def _(act):
                norm.squares(act)

            @block.tensor
            def _(pe):
                norm.sums(pe)

            @block.vector
            def _(dve):
                norm.normalise(dve)


def stage_project(k):
    nc, ps = k.nc, k.psum
    kept_a, kept_v = k.sem("pj_kept_a"), k.sem("pj_kept_v")
    stored = k.stored
    gate_w_in, moved = k.sem("pj_gate_w_in"), k.sem("pj_moved")
    r = k.ring
    sp_ = Split(k)
    rounds = NTILES // 4 - 1
    with ExitStack() as ctx:
        out = k.sb("pj_out", [P, 4, TC], ctx=ctx)
        norm = Norm(k, 0, ctx, out)
        with nc.Block() as block:

            @block.sync
            def _(sp):
                w = k.i["w_in_att"]
                for first, col, count in RUNS:
                    with sp.Fori(0, count // 4) as j:
                        for s in range(4):
                            load_weights(k, sp, j * 4 + (r + first + s), w[0, :, bass.ds(j * 512 + (col + s * P), P)], (r + first + s) % 4)
                n = r + NTILES - 2
                load_weights(k, sp, n, w[0, :, RUNS[2][1] + 8 * P:RUNS[2][1] + 9 * P])
                n += 1
                sp.wait_ge(k.w_free, n + 1)
                wg = k.w[:, n % 4, :].rearrange("p (a n) -> p a n", n=P)
                sp.dma_start(wg[:, :, 0:WI_ROW], k.i["w_in_att"][0, :, GA_COL:GA_COL + WI_ROW].rearrange("(a p) n -> p a n", p=P)).then_inc(k.w_in[n % 4], 16)
                sp.dma_start(wg[:, :, WI_ROW:P], k.i["w_in_att"][0, :, WI_COL:WI_COL + NI].rearrange("(a p) n -> p a n", p=P)).then_inc(gate_w_in, 16)

            @block.tensor
            def _(pe):
                pe.sem_inc(kept_a, 4)
                pe.sem_inc(kept_v, 4)
                pe.sem_inc(sp_.used, 2)

                def tile(s, j4, ready=None):
                    pe.wait_ge(kept_a, j4 + (s + 1))
                    pe.wait_ge(kept_v, j4 + (s + 1))
                    sp_.matmuls(pe, s, j4, (s % 4) * 2, ready)

                norm.sums(pe)
                tile(0, 0, (norm.fin, 2))
                for s in range(1, 4):
                    tile(s, 0)
                with pe.Fori(1, rounds) as j:
                    for s in range(4):
                        tile(s, j * 4)
                for s in range(4 * rounds, NTILES):
                    tile(s, 0)

            @block.scalar
            def _(act):

                def step(s, j4, first=False, last=False):
                    if not last:
                        sp_.hi(act, s + 1, j4)
                    act.wait_ge(sp_.used, j4 + (s + 3))
                    if not first:
                        act.wait_ge(stored[s % 4], j4 * 4 + 16 * (s // 4))
                    nc.scalar.activation(out[:, s % 4, 0:HC], ps[:, (s % 4) * 2, 0:HC], ACT.Copy).then_inc(kept_a, 1)

                for name in ("win_k", "win_v"):
                    act.dma_start(k.o[name + "_s"][0, :, 0:WIN - 1], k.i["state_nsa_" + name][0, :, 1:WIN]).then_inc(moved, 16)
                norm.squares(act)
                sp_.hi(act, 0, 0)
                norm.high_parts(act)
                for s in range(4):
                    step(s, 0, first=True)
                with act.Fori(1, rounds) as j:
                    for s in range(4):
                        step(s, j * 4)
                for s in range(4 * rounds, NTILES):
                    if s + 1 == NTILES - 1:
                        act.wait_ge(gate_w_in, 16)
                    step(s, 0, last=(s == NTILES - 1))
                act.wait_ge(moved, 32)

            @block.vector
            def _(dve):

                def step(s, j4, first=False, last=False):
                    if not last:
                        sp_.lo(dve, s + 1, j4)
                    dve.wait_ge(sp_.used, j4 + (s + 3))
                    if not first:
                        dve.wait_ge(stored[s % 4], j4 * 4 + 16 * (s // 4))
                    dve.tensor_copy(out[:, s % 4, HC:TC], ps[:, (s % 4) * 2 + 1, 0:HC]).then_inc(kept_v, 1)

                norm.normalise(dve, lambda dve: sp_.lo(dve, 0, 0))
                for s in range(4):
                    step(s, 0, first=True)
                with dve.Fori(1, rounds) as j:
                    for s in range(4):
                        step(s, j * 4)
                for s in range(4 * rounds, NTILES):
                    step(s, 0, last=(s == NTILES - 1))

            @block.gpsimd
            def _(pool):

                def store(s, j4, tile):
                    pool.wait_ge(kept_a, j4 + (s + 5))
                    pool.wait_ge(kept_v, j4 + (s + 5))
                    pool.dma_start(tile, out[:, s % 4, :]).then_inc(stored[s % 4], 16)

                with pool.Fori(0, rounds) as j:
                    for s in range(4):
                        store(s, j * 4, k.proj[bass.ds(j * 4 + s, 1)].rearrange("o p c -> (o p) c"))
                for s in range(4 * rounds, NTILES):
                    store(s, 0, k.proj[s])
                for s in range(4):
                    pool.wait_ge(stored[s], 16 * len(range(s, NTILES, 4)))
    k.ring += NTILES


def stage_rows(k):
    nc, ps = k.nc, k.psum
    tile_in, turned, rows_kept, rows_out = (k.sem(f"rw_{n}") for n in ("tile_in", "turned", "rows_kept", "rows_out"))
    pairs = [(KC, "cmp_k"), (VC, "cmp_v"), (KS, "slc_k"), (VS, "slc_v"), (KW, "win_k"), (VW, "win_v"), (KB, "dsa_k"), (VB, "dsa_v"), (KI, "idx_k")]
    with ExitStack() as ctx:
        src = k.sb("rw_src", [P, 2, 2, TC], ctx=ctx)
        rows = k.sb("rw_rows", [P, 2, TT, 256], ctx=ctx)
        rows_s = k.sb("rw_rows_s", [NS, 2, 256], ctx=ctx)
        with nc.Block() as block:

            @block.sync
            def _(sp):
                for n, (tile, name) in enumerate(pairs + [(GW, None)]):
                    if n >= 2:
                        sp.wait_ge(turned, n - 1)
                    if name == "idx_k":
                        sp.dma_start(src[:, n % 2, 0, :], k.proj[tile]).then_inc(tile_in, 16)
                    elif name:
                        sp.dma_start(src[:, n % 2, :, :], k.proj[tile:tile + 2].rearrange("g p c -> p g c")).then_inc(tile_in, 16)
                    else:
                        sp.dma_start(src[:, n % 2, 0, :], k.proj[tile]).then_inc(tile_in, 16)
                    sp.wait_ge(tile_in, 16 * (n + 1))

            @block.tensor
            def _(pe):
                for n, (tile, name) in enumerate(pairs + [(GW, None)]):
                    pe.wait_ge(tile_in, 16 * (n + 1))
                    if n >= 2:
                        pe.wait_ge(rows_kept, 2 * (n - 1))
                    width, parts = P, 2 if name and name != "idx_k" else 1
                    for g in range(parts):
                        for i in range(TT):
                            at = i * 256 + g * P
                            pe.transpose(ps[:, 3 * (n % 2) + at // 512, at % 512:at % 512 + width], src[0:width, n % 2, g, i * P:(i + 1) * P], k.ident[0:width, 0:width])
                        mm = pe.transpose(ps[0:NS, 3 * (n % 2) + 2, g * P:g * P + width], src[0:width, n % 2, g, T:TC], k.ident[0:width, 0:width])
                    mm.then_inc(turned, 1)

            @block.vector
            def _(dve):
                for n, (tile, name) in enumerate(pairs + [(GW, None)]):
                    width = 256 if name and name != "idx_k" else P
                    dve.wait_ge(turned, n + 1)
                    if name:
                        if n >= 2:
                            dve.wait_ge(rows_out, 32 * (n - 1))
                        to, to_s = rows[:, n % 2, :, 0:width], rows_s[:, n % 2, 0:width]
                    b = 3 * (n % 2)
                    if not name:
                        for at, row, w in ((0, 0, NGA), (NGA, WI_ROW, NI)):
                            dve.tensor_copy(k.gw[:, :, at:at + w], ps[:, b:b + 2, :].rearrange("p b (i c) -> p (b i) c", c=256)[:, :, row:row + w])
                            dve.tensor_copy(k.gws[:, at:at + w], ps[0:NS, b + 2, row:row + w]).then_inc(rows_kept, 1)
                        continue
                    dve.tensor_copy(to, ps[:, b:b + 2, :].rearrange("p b (i c) -> p (b i) c", c=256)[:, :, 0:width]).then_inc(rows_kept, 1)
                    dve.tensor_copy(to_s, ps[0:NS, b + 2, 0:width]).then_inc(rows_kept, 1)
                dve.wait_ge(rows_kept, 2 * (len(pairs) + 1))

            @block.scalar
            def _(act):
                for n, (tile, name) in enumerate(pairs):
                    width = P if name == "idx_k" else 256
                    act.wait_ge(rows_kept, 2 * (n + 1))
                    flat = "a b (i p) g d -> p (a b i) (g d)" if width == 256 else "a b (i p) d -> p (a b i) d"
                    flat_s = "a b t g d -> (a b t) (g d)" if width == 256 else "a b t d -> (a b t) d"
                    act.dma_start(k.o[name + "_p"].rearrange(flat, p=P), rows[:, n % 2, :, 0:width]).then_inc(rows_out, 16)
                    out_s = k.o[name + "_s"]
                    if name[:3] == "win":
                        out_s = out_s[:, :, WIN - 1:WIN]
                    act.dma_start(out_s.rearrange(flat_s), rows_s[:, n % 2, 0:width]).then_inc(rows_out, 16)
                    act.wait_ge(rows_out, 32 * (n + 1))


def stage_sample_queries(k):
    nc = k.nc
    got, zero, step, out, back = (k.sem(f"sq_{n}") for n in ("got", "zero", "step", "out", "back"))
    with nc.Block() as block:

        @block.sync
        def _(sp):
            sp.dma_start(k.sT[:, :, :], k.proj[0:GW, :, T:TC].rearrange("t p s -> p t s")).then_inc(got, 16)
            sp.wait_ge(step, 2)
            sp.dma_start(k.gate_rows, k.gws[:, :]).then_inc(out, 16)
            sp.wait_ge(out, 16)
            sp.dma_start(k.ga_s[:, :], k.gate_rows[:, 0:NGA].rearrange("s (h b) -> s h b", b=3)).then_inc(back, 16)
            sp.dma_start(k.wi_s[:, :], k.gate_rows[:, NGA:NGW].unsqueeze(2)).then_inc(back, 16)
            sp.wait_ge(back, 32)

        @block.gpsimd
        def _(pool):
            pool.memset(k.qpa[:, :], 0.0)
            pool.memset(k.qpb[:, :], 0.0)
            pool.memset(k.qpi[:, :], 0.0).then_inc(zero, 1)
            pool.memset(k.zeros[:, :], 0.0).then_inc(zero, 1)
            pool.wait_ge(zero, 2)

        @block.vector
        def _(dve):
            dve.wait_ge(k.s_sig, 2)
            dve.tensor_scalar(k.gw[:, :, 0:NGA], k.gw[:, :, 0:NGA], 1.0, None, ALU.add)
            dve.tensor_scalar(k.gws[:, 0:NGA], k.gws[:, 0:NGA], 1.0, None, ALU.add).then_inc(k.s_sig, 1)
            dve.wait_ge(k.s_sig, 3)
            dve.reciprocal(k.gw[:, :, 0:NGA], k.gw[:, :, 0:NGA])
            dve.reciprocal(k.gws[:, 0:NGA], k.gws[:, 0:NGA]).then_inc(step, 1)
            dve.tensor_scalar(k.gw[:, :, NGA:NGW], k.gw[:, :, NGA:NGW], NI ** -0.5, None, ALU.mult)
            dve.tensor_scalar(k.gws[:, NGA:NGW], k.gws[:, NGA:NGW], NI ** -0.5, None, ALU.mult).then_inc(step, 1)
            dve.wait_ge(got, 16)
            dve.wait_ge(zero, 2)
            for pad, tile, scale in ((k.qpa, QA, SCALE), (k.qpb, QB, SCALE)):
                for h in range(NH):
                    at = (h // 4) * 64 + h
                    dve.tensor_scalar(pad[:, at:at + 136 * 7 + 1:136], k.sT[:, tile + h, :], scale, None, ALU.mult).then_inc(step, 1)
            for h in range(NI):
                dve.tensor_scalar(k.qpi[:, h:h + 144 * 7 + 1:144], k.sT[:, QI + h, :], SCALE, None, ALU.mult).then_inc(step, 1)
            dve.wait_ge(step, 2 + 2 * NH + NI)
            dve.wait_ge(back, 32)
            dve.tensor_scalar(k.wsel[:, :], k.const[:, C_BD16:C_BD16 + NS], k.wi_s[:, 0:1], None, ALU.mult).then_inc(step, 1)
            dve.wait_ge(step, 3 + 2 * NH + NI)

        @block.scalar
        def _(act):
            nc.scalar.activation(k.gw[:, :, 0:NGA], k.gw[:, :, 0:NGA], ACT.Exp, scale=-1.0).then_inc(k.s_sig, 1)
            nc.scalar.activation(k.gws[:, 0:NGA], k.gws[:, 0:NGA], ACT.Exp, scale=-1.0).then_inc(k.s_sig, 1)


def settle(k, eng):
    eng.sem_inc(k.settled[eng.engine], 1)


def off(i):
    return P * (i * (i + 1) // 2)


def stage_index_prompt(k):
    nc, ps = k.nc, k.psum
    q_in, mm_done, relu_done, added, step = [k.sem("ip_q_in0"), k.sem("ip_q_in1")], *(k.sem(f"ip_{n}") for n in ("mm", "relu", "added", "step"))
    k_in = k.sem("ip_k_in")
    with ExitStack() as ctx:
        q = k.sb("ip_q", [P, 2, TC], ctx=ctx)
        ki = k.sb("ip_k", [P, TC], ctx=ctx)
        rl = k.sb("ip_relu", [P, 2, off(TT)], ctx=ctx)
        sc = k.mask
        with nc.Block() as block:

            @block.sync
            def _(sp):
                sp.dma_start(ki[:, :], k.proj[KI]).then_inc(k_in, 16)
                with sp.Fori(0, NI // 2) as j:
                    for b in range(2):
                        sp.wait_ge(mm_done, j * 2 + (b + 1))
                        sp.dma_start(q[:, b, :], k.proj[bass.ds(j * 2 + (QI + b), 1)].rearrange("o p c -> (o p) c")).then_inc(q_in[b], 16)
                load_w1(k, sp, "k")

            @block.tensor
            def _(pe):
                pe.sem_inc(mm_done, 2)
                pe.sem_inc(relu_done, 2)
                pe.wait_ge(k_in, 16)
                with pe.Fori(0, NI // 2) as j:
                    for b in range(2):
                        pe.wait_ge(q_in[b], j * 16 + 16)
                        pe.wait_ge(relu_done, j * 2 + (b + 1))
                        for i in range(TT):
                            mm = pe.matmul(ps[:, 4 * b + i, 0:P * (i + 1)], q[:, b, i * P:(i + 1) * P], ki[:, 0:P * (i + 1)], start=True, stop=True)
                        mm.then_inc(mm_done, 1)

            @block.scalar
            def _(act):
                with act.Fori(0, NI // 2) as j:
                    for b in range(2):
                        act.wait_ge(mm_done, j * 2 + (b + 3))
                        act.wait_ge(added, j * 2 + (b + 1))
                        for i in range(TT):
                            ins = nc.scalar.activation(rl[:, b, off(i):off(i + 1)], ps[:, 4 * b + i, 0:P * (i + 1)], ACT.Relu, scale=SCALE)
                        ins.then_inc(relu_done, 1)

            @block.vector
            def _(dve):
                dve.memset(sc[:, :], 0.0).then_inc(added, 2)
                with dve.Fori(0, NI // 2) as j:
                    for b in range(2):
                        dve.wait_ge(relu_done, j * 2 + (b + 3))
                        dve.wait_ge(added, j * 2 + (b + 2))
                        for i in range(TT):
                            ins = dve.scalar_tensor_tensor(out=sc[:, off(i):off(i + 1)], in0=rl[:, b, off(i):off(i + 1)], scalar=k.gw[:, i, bass.ds(j * 2 + (NGA + b), 1)],
                                                           in1=sc[:, off(i):off(i + 1)], op0=ALU.mult, op1=ALU.add)
                        ins.then_inc(added, 1)

            @block.gpsimd
            def _(pool):
                pool.wait_ge(added, NI + 2)
                for i in range(TT):
                    d = sc[:, off(i + 1) - P:off(i + 1)]
                    pool.affine_select(out=d, in_=d, compare_op=ALU.is_ge, fill=NEG, base=0, pattern=[[-1, P]], channel_multiplier=1).then_inc(step, 1)
                pool.wait_ge(step, TT)


def load_pages(k, sp, cache, dst, arrived, s, first, count):
    _, pages = k.nc.values_load_multi_w_load_instructions(k.pages[0:1, bass.ds(s * PG + first, count)], engines=[sp.engine], min_val=0, max_val=NPOOL - 1,
                                                          skip_runtime_bounds_check_because="a page table holds numbers of pages of the pool only")
    for g, page in enumerate(pages):
        src = cache[0, bass.ds(page, 1)]
        src = src.rearrange("o p g d -> (o p) (g d)") if len(src.shape) == 4 else src.rearrange("o p d -> (o p) d")
        sp.dma_start(dst[:, g, :], src).then_inc(arrived, 16)


def load_w1(k, eng, which):
    eng.dma_start(k.w1[which], k.i["cmp_w1_" + which][0].rearrange("(l d) n -> d l n", d=P)).then_inc(k.w1_in[which], 16)


def stage_index_sample(k):
    nc, ps = k.nc, k.psum
    arrived = [k.sem("is_arrived0"), k.sem("is_arrived1")]
    turned, kept, used, qcopy, relu_done, summed, scored, step = (k.sem(f"is_{n}") for n in
        ("turned", "kept", "used", "qcopy", "relu", "summed", "scored", "step"))
    with ExitStack() as ctx:
        pg = k.sb("is_pages", [P, 2, PG, P], ctx=ctx)
        kt = k.sb("is_keys", [P, 2, PAST], ctx=ctx)
        qs = k.sb("is_q", [P, 2, P], ctx=ctx)
        rl = k.sb("is_relu", [P, PAST + 1], ctx=ctx)
        sc = k.mask_s
        with nc.Block() as block:

            @block.sync
            def _(sp):
                with sp.Fori(0, NS // 2) as j:
                    for b in range(2):
                        sp.wait_ge(turned, j * 8 + (4 * b + 4))
                        load_pages(k, sp, k.i["cache_dsa_idx_k"], pg[:, b, 0:8], arrived[b], j * 2 + b, 0, 8)
                load_w1(k, sp, "v")

            @block.tensor
            def _(pe):
                pe.sem_inc(turned, 8)
                pe.sem_inc(used, 2)
                pe.sem_inc(kept, 2)
                for c in range(4):
                    pe.matmul(ps[:, c, :], k.zeros[:, :], k.xT[:, 0, 0:512], start=True, stop=True)
                for s in range(NS):
                    mm = pe.matmul(ps[:, 4, 0:1], k.qpi[:, s * P:(s + 1) * P], k.sT[:, KI, s:s + 1], start=(s == 0), stop=(s == NS - 1))
                mm.then_inc(summed, 1)

                def turn_keys(j2, s):
                    pe.wait_ge(arrived[s % 2], (j2 + s - s % 2) * (8 * PG) + 16 * PG)
                    for c in range(4):
                        pe.wait_ge(kept, j2 * 4 + (4 * s + c + 1))
                        for g in range(4):
                            mm = pe.transpose(ps[:, 5 + c % 2, g * P:(g + 1) * P], pg[:, s % 2, c * 4 + g, :], k.ident)
                        mm.then_inc(turned, 1)

                def add_logits(j2, s):
                    pe.wait_ge(qcopy, j2 + (s + 1))
                    pe.wait_ge(kept, j2 * 4 + (4 * s + 6))
                    for c in range(4):
                        mm = pe.matmul(ps[:, c, :], qs[:, s % 2, :], kt[:, s % 2, c * 512:(c + 1) * 512], start=False, stop=True, skip_group_check=True)
                    mm.then_inc(used, 1)

                turn_keys(0, 0)
                with pe.Fori(0, NS // 2 - 1) as j:
                    for s in range(2):
                        turn_keys(j * 2, s + 1)
                        add_logits(j * 2, s)
                turn_keys(0, NS - 1)
                add_logits(0, NS - 2)
                add_logits(0, NS - 1)
                pe.wait_ge(relu_done, 5)
                for c in range(4):
                    mm = pe.matmul(ps[0:NS, c, :], k.wsel[:, :], rl[:, c * 512:(c + 1) * 512], start=True, stop=True)
                pe.matmul(ps[0:NS, 4, 0:1], k.wsel[:, :], rl[:, PAST:PAST + 1], start=True, stop=True).then_inc(scored, 1)

            @block.scalar
            def _(act):
                with act.Fori(0, NS // 2) as j:
                    for b in range(2):
                        act.wait_ge(turned, j * 8 + (4 * b + 4))
                        load_pages(k, act, k.i["cache_dsa_idx_k"], pg[:, b, 8:16], arrived[b], j * 2 + b, 8, 8)
                act.wait_ge(used, NS + 2)
                act.wait_ge(summed, 1)
                for c in range(4):
                    nc.scalar.activation(rl[:, c * 512:(c + 1) * 512], ps[:, c, :], ACT.Relu).then_inc(relu_done, 1)
                nc.scalar.activation(rl[:, PAST:PAST + 1], ps[:, 4, 0:1], ACT.Relu).then_inc(relu_done, 1)

            @block.vector
            def _(dve):
                with dve.Fori(0, NS // 2) as j:
                    for b in range(2):
                        dve.wait_ge(used, j * 2 + (b + 1))
                        dve.tensor_copy(qs[:, b, :], k.qpi[:, bass.ds(j * 256 + b * P, P)]).then_inc(qcopy, 1)
                        for c in range(4):
                            dve.wait_ge(turned, j * 8 + (8 + 4 * b + c + 1))
                            dve.tensor_copy(kt[:, b, c * 512:(c + 1) * 512], ps[:, 5 + c % 2, :]).then_inc(kept, 1)
                dve.wait_ge(scored, 1)
                dve.tensor_copy(sc[:, 0:PAST], ps[0:NS, 0:4, :].rearrange("p b c -> p (b c)"))
                dve.tensor_copy(sc[:, PAST:PAST + 1], ps[0:NS, 4, 0:1]).then_inc(step, 2)
                dve.wait_ge(step, 2)


def stage_compress(k, which):
    nc, ps = k.nc, k.psum
    names = ("cz_w", "cz_prompt", "cz_zero", "cz_pe", "cz_pe_mm", "cz_pe_kept", "cz_turned", "cz_kept", "cz_picked_p", "cz_picked_s", "cz_hid", "cz_x", "cz_exp",
             "cz_act", "cz_step", "cz_hid_turned", "cz_hid_kept", "cz_out", "cz_done", "cz_arrived0", "cz_arrived1")
    sems = [k.sem(n) for n in names]
    w_got, prompt_in, zeroed, pe_turned, pe_mm, pe_kept, turned, kept, picked_p, picked_s, hid, x_done, exp_done, act_done, step, hid_turned, hid_kept, out_mm, done, arr0, arr1 = sems
    arrived = [arr0, arr1]
    keys = which == "k"
    dst = k.kcmp if keys else k.vcmp
    with ExitStack() as ctx:
        w1 = k.w1[which]
        w2 = k.sb("cz_w2" + which, [P, 2, P], ctx=ctx)
        pe_n = k.sb("cz_pen" + which, [CB, P], ctx=ctx)
        pe_t = k.sb("cz_pet" + which, [P, CB], ctx=ctx)
        pe_b = k.sb("cz_peb" + which, [P, CH], ctx=ctx)
        pg = k.sb("cz_pg" + which, [P, 2, PG // 2, 256], ctx=ctx)
        xt = k.sb("cz_xt" + which, [P, 2, G, PAST], ctx=ctx)
        x = k.sb("cz_x" + which, [P, CH], ctx=ctx)
        e = k.sb("cz_e" + which, [P, CH], ctx=ctx)
        hc = k.sb("cz_hc" + which, [P, CH], ctx=ctx)
        best = k.sb("cz_best" + which, [P, TT, 8], ctx=ctx)
        with nc.Block() as block:

            @block.sync
            def _(sp):
                sp.dma_start(pe_n[:, :], k.i["cmp_pe_" + which][0]).then_inc(w_got, 16)
                sp.dma_start(w2[:, :, :], k.i["cmp_w2_" + which][0].rearrange("(c d) n -> d c n", d=P)).then_inc(w_got, 16)
                sp.wait_ge(zeroed, 1)
                t = KC if keys else VC
                sp.dma_start(xt[:, 1, :, 0:T], k.proj[t:t + 2, :, 0:T].rearrange("g p c -> p g c")).then_inc(prompt_in, 16)
                with sp.Fori(0, NS) as s:
                    for hf in range(2):
                        sp.wait_ge(turned, s * 8 + (4 * hf + 4))
                        load_pages(k, sp, k.i["cache_nsa_cmp_" + which], pg[:, hf], arrived[hf], s, hf * (PG // 2), PG // 2)

            @block.tensor
            def _(pe):
                pe.sem_inc(turned, 8)
                pe.sem_inc(kept, 2)
                pe.wait_ge(w_got, 32)
                pe.wait_ge(k.w1_in[which], 16)
                pe.transpose(ps[:, 6, 0:CB], pe_n[:, :], k.ident[0:CB, 0:CB]).then_inc(pe_turned, 1)
                pe.wait_ge(pe_kept, 1)
                for l in range(CB):
                    mm = pe.matmul(ps[:, 2, 0:CH], pe_t[:, l:l + 1].broadcast_to([P, P]), w1[:, l, :], start=(l == 0), stop=(l == CB - 1))
                mm.then_inc(pe_mm, 1)

                def hidden(b):
                    for l in range(CB):
                        rows = xt[:, b, :, :].rearrange("p g (n l) -> p (g n) l", l=CB)[:, :, l]
                        mm = pe.matmul(ps[:, b, 0:CH], rows, w1[:, l, :], start=(l == 0), stop=(l == CB - 1))
                    mm.then_inc(hid, 1)

                def second(j2, n):
                    pe.wait_ge(act_done, j2 + (n + 1))
                    for c in range(2):
                        mm = pe.transpose(ps[:, 6, c * P:(c + 1) * P], hc[:, c * P:(c + 1) * P], k.ident)
                    mm.then_inc(hid_turned, 1)
                    pe.wait_ge(hid_kept, j2 + (n + 1))
                    for c in range(2):
                        if keys:
                            mm = pe.matmul(ps[:, 7, 0:P], w2[:, c, :], k.hct[:, c * P:(c + 1) * P], start=(c == 0), stop=(c == 1))
                        else:
                            mm = pe.matmul(ps[:, 7, 0:P], k.hct[:, c * P:(c + 1) * P], w2[:, c, :], start=(c == 0), stop=(c == 1))
                    mm.then_inc(out_mm, 1)

                def turn_rows(j2, s):
                    for hf in range(2):
                        pe.wait_ge(arrived[hf], j2 * (8 * 16) + 8 * 16 * (s + 1))
                        for c in range(4):
                            pe.wait_ge(kept, j2 * 8 + (8 * s + 4 * hf + c + 1))
                            for g in range(G):
                                for q in range(2):
                                    mm = pe.transpose(ps[:, 4 + c % 2, g * 256 + q * P:g * 256 + (q + 1) * P], pg[:, hf, 2 * c + q, g * P:(g + 1) * P], k.ident)
                            mm.then_inc(turned, 1)

                def unit(j2, n, last=False):
                    if not last:
                        turn_rows(j2, n)
                    second(j2, n - 1)
                    pe.wait_ge(kept, j2 * 8 + (8 * n + 2))
                    hidden((n - 1) % 2)

                turn_rows(0, 0)
                pe.wait_ge(prompt_in, 16)
                hidden(1)
                with pe.Fori(0, NS // 2 - 1) as j:
                    for n in (1, 2):
                        unit(j * 2, n)
                unit(0, NS - 1)
                unit(0, NS, last=True)
                second(0, NS)

            @block.scalar
            def _(act):
                def copy(o, i):
                    return nc.scalar.activation(o, i, ACT.Copy)

                def keep_rows(j2, s, banks):
                    for c in banks:
                        act.wait_ge(turned, j2 * 8 + (8 * s + c + 9))
                        copy(xt[:, s % 2, :, c * 256:(c + 1) * 256], ps[:, 4 + c % 2, :].rearrange("p (g q) -> p g q", g=G)).then_inc(kept, 1)

                def exp(j2, n):
                    act.wait_ge(x_done, j2 + (n + 1))
                    nc.scalar.activation(e[:, :], x[:, :], ACT.Exp, scale=-1.0).then_inc(exp_done, 1)

                def keep_hidden(j2, n):
                    act.wait_ge(hid_turned, j2 + (n + 1))
                    copy(k.hct[:, :], ps[:, 6, 0:CH]).then_inc(hid_kept, 1)

                def unit(j2, n):
                    act.wait_ge(hid, j2 + n)
                    keep_rows(j2, n, range(2))
                    exp(j2, n - 1)
                    keep_rows(j2, n, range(2, 8))
                    keep_hidden(j2, n - 1)

                act.wait_ge(pe_turned, 1)
                copy(pe_t[:, :], ps[:, 6, 0:CB]).then_inc(pe_kept, 1)
                keep_rows(0, 0, range(8))
                with act.Fori(0, NS // 2 - 1) as j:
                    for n in (1, 2):
                        unit(j * 2, n)
                unit(0, NS - 1)
                for n in (NS - 1, NS):
                    exp(0, n)
                    keep_hidden(0, n)

            @block.vector
            def _(dve):
                def silu(j2, n):
                    base = j2 * 2 + (2 * n + 1)
                    dve.wait_ge(hid, j2 + (n + 1))
                    dve.tensor_tensor(x[:, :], ps[:, (n - 1) % 2, 0:CH], pe_b[:, :], ALU.add).then_inc(x_done, 1)
                    dve.wait_ge(exp_done, j2 + (n + 1))
                    dve.tensor_scalar(e[:, :], e[:, :], 1.0, None, ALU.add).then_inc(step, 1)
                    dve.wait_ge(step, base + 1)
                    dve.reciprocal(e[:, :], e[:, :]).then_inc(step, 1)
                    dve.wait_ge(step, base + 2)
                    dve.tensor_tensor(hc[:, :], x[:, :], e[:, :], ALU.mult).then_inc(act_done, 1)

                def keep_out(j2, n):
                    dve.wait_ge(out_mm, j2 + (n + 1))
                    dve.tensor_copy(dst[:, bass.ds(j2 + n, 1), :].rearrange("p o c -> p (o c)"), ps[:, 7, 0:P]).then_inc(done, 1)

                def pick(j2, n, scores, rounds, picked):
                    W = len(scores)
                    for q in range(rounds):
                        at = j2 * (2 * W * rounds) + 2 * W * (rounds * n + q)
                        for i, (sc, b) in enumerate(scores):
                            dve.wait_ge(picked, at + (i + 1))
                            settle(k, dve)
                            dve.max(b, sc).then_inc(picked, 1)
                        for i, (sc, b) in enumerate(scores):
                            dve.wait_ge(picked, at + (W + i + 1))
                            settle(k, dve)
                            dve.match_replace(sc, b, sc, TAKEN).then_inc(picked, 1)

                ROUNDS_S = TOPK_S // 8 // NS
                sample = [(k.mask_s[:, :], best[0:NS, TT - 1, :])]
                prompt = [(k.mask[:, off(i):off(i + 1)], best[:, i - 1, :]) for i in range(1, TT)]
                if keys:
                    picks = [(sample, ROUNDS_S - 1, picked_s)]
                else:
                    picks = [(prompt, TOPK_P // 8 // NS, picked_p), (sample, 1, picked_s)]
                for scores, _, picked in picks:
                    dve.sem_inc(picked, len(scores))
                dve.memset(xt[:, 1, :, :], 0.0).then_inc(zeroed, 1)
                dve.wait_ge(pe_mm, 1)
                dve.tensor_copy(pe_b[:, :], ps[:, 2, 0:CH]).then_inc(step, 1)
                dve.wait_ge(step, 1)
                with dve.Fori(0, NS // 2) as j:
                    for n in range(2):
                        silu(j * 2, n)
                        for what in picks:
                            pick(j * 2, n, *what)
                        keep_out(j * 2, n)
                silu(0, NS)
                keep_out(0, NS)
                for scores, rounds, picked in picks:
                    dve.wait_ge(picked, len(scores) * (2 * rounds * NS + 1))
                if not keys:
                    dve.tensor_scalar(k.mask_s[:, :], k.mask_s[:, :], TAKEN, NEG, ALU.not_equal, ALU.mult).then_inc(done, 1)
                    dve.memset(k.mask[:, off(0):off(1)], 0.0)
                    dve.tensor_scalar(k.mask[:, off(1):off(TT)], k.mask[:, off(1):off(TT)], TAKEN, NEG, ALU.not_equal, ALU.mult).then_inc(done, 1)
                dve.wait_ge(done, NS + 1 if keys else NS + 3)


def stage_compressed_sample(k):
    nc, ps = k.nc, k.psum
    mm_done, step, exp_done, grouped, out_mm, ct_kept = (k.sem(f"cs_{n}") for n in ("mm", "step", "exp", "grouped", "out", "ct_kept"))
    R = NS * NH
    with ExitStack() as ctx:
        p = k.sb("cs_p", [R, 2, NCB], ctx=ctx)
        pt = k.sb("cs_pt", [P, R], ctx=ctx)
        st = k.sb("cs_stat", [R, 4], ctx=ctx)
        best = k.sb("cs_best", [NS * G, 8], ctx=ctx)
        with nc.Block() as block:

            @block.tensor
            def _(pe):
                pe.wait_ge(step, 1)
                pe.matmul(ps[0:R, 0, 0:NCB], k.tabs[:, 0, :], k.hot[:, O_C:O_C + NCB], start=True, stop=False)
                for n in range(NS * G):
                    mm = pe.matmul(ps[0:R, 0, 0:NCB], k.qpa[:, n * R:(n + 1) * R], k.kcmp[:, n // G + 1, (n % G) * NCB:(n % G + 1) * NCB], start=False, stop=(n == NS * G - 1))
                mm.then_inc(mm_done, 1)
                pe.wait_ge(step, 5)
                pe.matmul(ps[0:NS * G, 1, 0:NCB], k.const[0:R, C_R16:C_R16 + NS * G], p[:, 0, :], start=True, stop=True).then_inc(grouped, 1)
                pe.wait_ge(step, 8)
                pe.transpose(ps[:, 2, 0:R], p[:, :, :].rearrange("r a n -> r (a n)"), k.ident[0:R, 0:R]).then_inc(out_mm, 1)
                pe.wait_ge(ct_kept, 1)
                for n in range(NS * G):
                    s, g = n // G, n % G
                    at = s * NH + g * 4
                    mm = pe.matmul(ps[:, 3 + g, at:at + 4], k.vcmp[g * NCB:(g + 1) * NCB, s + 1, :], pt[g * NCB:(g + 1) * NCB, at:at + 4], start=(s == 0), stop=True, skip_group_check=True)
                mm.then_inc(out_mm, 1)

            @block.scalar
            def _(act):
                act.wait_ge(step, 3)
                nc.scalar.activation(p[:, 0, :], ps[0:R, 0, 0:NCB], ACT.Exp, bias=st[:, 1:2], accum_out=st[:, 2:3]).then_inc(exp_done, 1)
                act.wait_ge(out_mm, 1)
                nc.scalar.activation(pt[:, :], ps[:, 2, 0:R], ACT.Copy).then_inc(ct_kept, 1)

            @block.vector
            def _(dve):
                for m in range(2):
                    ins = dve.tensor_copy(k.tabs[:, m, :].rearrange("p (s h) -> p s h", h=NH), k.table[:, m * NH:(m + 1) * NH].unsqueeze(1).broadcast_to([32, NS, NH]))
                ins.then_inc(step, 1)
                dve.wait_ge(mm_done, 1)
                dve.reduce_max(st[:, 0:1], ps[0:R, 0, 0:NCB], AX).then_inc(step, 1)
                dve.wait_ge(step, 2)
                dve.tensor_scalar(st[:, 1:2], st[:, 0:1], -1.0, None, ALU.mult).then_inc(step, 1)
                dve.wait_ge(exp_done, 1)
                dve.reciprocal(st[:, 3:4], st[:, 2:3]).then_inc(step, 1)
                dve.wait_ge(step, 4)
                dve.tensor_scalar(p[:, 0, :], p[:, 0, :], st[:, 3:4], None, ALU.mult).then_inc(step, 1)
                dve.memset(k.msel[:, :], 0.0).then_inc(step, 1)
                dve.wait_ge(grouped, 1)
                dve.wait_ge(step, 6)
                dve.tensor_reduce(k.msel[:, 0:NCB // 2], ps[0:NS * G, 1, 0:NCB].rearrange("p (n r) -> p n r", r=2), AX, ALU.add).then_inc(step, 1)
                dve.wait_ge(step, 7)
                dve.tensor_scalar(p[:, 0, :], p[:, 0, :], k.ga_s[:, 0:1], None, ALU.mult).then_inc(k.s_gated, 1)
                dve.wait_ge(k.s_gated, 1)
                dve.tensor_copy(p[:, 1, :], p[:, 0, :]).then_inc(step, 1)
                n = 8
                for c in (slice(0, 1), slice(31, 33)):
                    dve.tensor_scalar(k.msel[:, c], k.msel[:, c], 1e4, None, ALU.add).then_inc(step, 1)
                    n += 1
                for r in range(2):
                    dve.wait_ge(step, n)
                    settle(k, dve)
                    dve.max(best[:, :], k.msel[:, :]).then_inc(step, 1)
                    dve.wait_ge(step, n + 1)
                    settle(k, dve)
                    dve.match_replace(k.msel[:, :], best[:, :], k.msel[:, :], TAKEN).then_inc(step, 1)
                    n += 2
                dve.wait_ge(step, n)
                dve.tensor_scalar(k.msel[:, :], k.msel[:, :], TAKEN, NEG, ALU.not_equal, ALU.mult)
                dve.wait_ge(out_mm, 2)
                for g in range(G):
                    def cols(t):
                        return t.rearrange("p (s h) -> p s h", h=NH)[:, :, g * 4:(g + 1) * 4]
                    dve.tensor_copy(cols(k.oS[:, 0, :]), cols(ps[:, 3 + g, 0:R])).then_inc(step, 1)
                dve.wait_ge(step, n + 2)


def stage_attend_sample(k, kind):
    nc, ps = k.nc, k.psum
    mixer, npg, kname, vname, ktile, nkname, gate = {
        "slc": (0, PG, "cache_nsa_slc_k", "cache_nsa_slc_v", KS, "slc_v_s", 1),
        "win": (0, WIN // P, "state_nsa_win_k", "state_nsa_win_v", KW, "win_v_s", 2),
        "dsa": (1, PG, "cache_dsa_k", "cache_dsa_v", KB, "dsa_v_s", None)}[kind]
    names = ("arr0", "arr1", "varr00", "varr01", "varr10", "varr11", "vnew", "turned", "kept_a", "kept_v", "used", "qcopy", "mm", "step", "exp", "pt", "pt_kept_a", "pt_kept_v", "slot", "vused", "o_kept", "o_turned", "out")
    sems = [k.sem("at_" + n) for n in names]
    arr0, arr1, varr00, varr01, varr10, varr11, vnew_in, turned, kept_a, kept_v, used, qcopy, mm_done, step, exp_done, pt_mm, pt_kept_a, pt_kept_v, slot, vused, o_kept, o_turned, out_mm = sems
    arrived, v_arrived = [arr0, arr1], [[varr00, varr01], [varr10, varr11]]
    R = NS * NH
    qp = (k.qpa, k.qpb)[mixer]
    NK = npg * P
    hp = npg // 2
    tb = hp // 2
    kb = NK // 512
    hot0 = O_S + PAST - NK
    with ExitStack() as ctx:
        pg = k.sb("at_pg" + kind, [P, 2, hp, 256], ctx=ctx)
        kt = k.sb("at_kt" + kind, [P, 2, G, NK], ctx=ctx)
        qs = k.sb("at_q" + kind, [P, 2, G * R], ctx=ctx)
        p = k.sb("at_p" + kind, [R, NK + 1], ctx=ctx)
        pt = k.sb("at_pt" + kind, [P, npg, R], ctx=ctx)
        st = k.sb("at_st" + kind, [R, 8], ctx=ctx)
        pd = k.sb("at_pd" + kind, [R, NS], ctx=ctx)
        pn = k.sb("at_pn" + kind, [NS, R], ctx=ctx)
        vnew = k.sb("at_vn" + kind, [NS, 256], ctx=ctx)
        pts = k.sb("at_pts" + kind, [P, 2, npg, NH], ctx=ctx)
        pns = k.sb("at_pns" + kind, [NS, 2, NH], ctx=ctx)
        o = k.sb("at_o" + kind, [NH, NS, 256], ctx=ctx)

        values = [kt[:, b].rearrange("p g n -> p (g n)").rearrange("p (h a d) -> p h a d", h=2, d=256) for b in range(2)]

        def load_half(eng, to, s, hf, name, sem):
            if kind == "win":
                eng.dma_start(to[:, hf, :, :], k.i[name][0, bass.ds(s, 1), hf * hp * P:(hf + 1) * hp * P].rearrange("o (n p) g d -> p (o n) (g d)", p=P)).then_inc(sem, 16)
            else:
                load_pages(k, eng, k.i[name], to[:, hf], sem, s, hf * hp, hp)

        with nc.Block() as block:

            @block.sync
            def _(sp):
                if kind == "win":
                    sp.dma_start(vnew[:, :], k.o[nkname][0, :, WIN - 1].rearrange("s g d -> s (g d)")).then_inc(vnew_in, 16)
                else:
                    sp.dma_start(vnew[:, :], k.o[nkname][0, :, 0].rearrange("s g d -> s (g d)")).then_inc(vnew_in, 16)

                with sp.Fori(0, NS) as s:
                    for hf in range(2):
                        sp.wait_ge(turned, s * (2 * tb) + (hf * tb + tb))
                        load_half(sp, pg, s, hf, kname, arrived[hf])
                for s in range(2):
                    sp.wait_ge(used, NS + s + 1)
                    for hf in range(2):
                        load_half(sp, values[s], s, hf, vname, v_arrived[s][hf])
                with sp.Fori(1, NS // 2) as j:
                    for b in range(2):
                        sp.wait_ge(vused, j * 4 + 2 * b)
                        load_half(sp, values[b], j * 2 + b, 0, vname, v_arrived[b][0])

            per = 16 * (1 if kind == "win" else hp)

            @block.tensor
            def _(pe):
                pe.sem_inc(turned, 2 * tb)
                pe.sem_inc(used, 2)
                pe.sem_inc(kept_a, 1)
                pe.sem_inc(kept_v, 1)
                pe.sem_inc(vused, 2)
                pe.sem_inc(o_kept, 2)
                for c in range(kb + 1):
                    logits = ps[0:R, c, :] if c < kb else ps[0:R, 4, 0:1]
                    hot = k.hot[:, hot0 + c * 512:hot0 + (c + 1) * 512] if c < kb else k.hot[:, O_S + PAST:O_S + PAST + 1]
                    pe.matmul(logits, k.tabs[:, mixer, :], hot, start=True, stop=True)
                    if kind == "slc":
                        sel = k.msel[:, c * 8:(c + 1) * 8].unsqueeze(2).broadcast_to([NS * G, 8, 64]) if c < kb else k.msel[:, 32:33]
                        pe.matmul(logits, k.const[0:NS * G, C_RT:C_RT + R], sel, start=False, stop=True, skip_group_check=True)
                    if kind == "dsa":
                        sel = k.mask_s[:, c * 512:(c + 1) * 512] if c < kb else k.mask_s[:, PAST:PAST + 1]
                        pe.matmul(logits, k.const[0:NS, C_E8:C_E8 + R], sel, start=False, stop=True, skip_group_check=True)
                for n in range(NS * G):
                    pe.matmul(ps[0:R, 4, 0:1], qp[:, n * R:(n + 1) * R], k.sT[:, ktile + n % G, n // G:n // G + 1], start=False, stop=True, skip_group_check=True)

                def turn_keys(j2, s):
                    for hf in range(2):
                        pe.wait_ge(arrived[hf], j2 * per + per * (s + 1))
                        for c in range(tb):
                            q = hf * tb + c
                            pe.wait_ge(kept_v if q % 2 else kept_a, j2 * tb + (tb * s + q // 2 + 1))
                            for g in range(G):
                                for a in range(2):
                                    mm = pe.transpose(ps[:, 5 + q % 2, g * 256 + a * P:g * 256 + (a + 1) * P], pg[:, hf, 2 * c + a, g * P:(g + 1) * P], k.ident)
                            mm.then_inc(turned, 1)

                def add_logits(j2, s):
                    pe.wait_ge(qcopy, j2 + (s + 1))
                    pe.wait_ge(kept_a, j2 * tb + (tb * s + tb + 1))
                    pe.wait_ge(kept_v, j2 * tb + (tb * s + tb + 1))
                    for c in range(kb):
                        for g in range(G):
                            mm = pe.matmul(ps[0:R, c, :], qs[:, s % 2, g * R:(g + 1) * R], kt[:, s % 2, g, c * 512:(c + 1) * 512], start=False, stop=True, skip_group_check=True)
                    mm.then_inc(used, 1)

                turn_keys(0, 0)
                with pe.Fori(0, NS // 2 - 1) as j:
                    for s in range(2):
                        turn_keys(j * 2, s + 1)
                        add_logits(j * 2, s)
                turn_keys(0, NS - 1)
                add_logits(0, NS - 2)
                add_logits(0, NS - 1)
                pe.wait_ge(step, 7)
                for a in range(npg):
                    mm = pe.transpose(ps[:, 5 + a // 8, (a % 8) * R:(a % 8 + 1) * R], p[:, a * P:(a + 1) * P], k.ident[0:R, 0:R])
                pe.transpose(ps[0:NS, 7, 0:R], pd[:, :], k.ident[0:R, 0:R]).then_inc(pt_mm, 1)
                pe.wait_ge(pt_kept_a, 2)
                pe.wait_ge(pt_kept_v, 1)
                pe.wait_ge(vnew_in, 16)
                with pe.Fori(0, NS // 2) as j:
                    for b in range(2):
                        pe.wait_ge(slot, j * 4 + (2 * b + 2))
                        pe.wait_ge(o_kept, j * 2 + (b + 1))
                        settle(k, pe)
                        pe.matmul(ps[0:NH, b, 0:256], pns[:, b, :], vnew[:, :], start=True, stop=False)
                        for hf in range(2):
                            pe.wait_ge(v_arrived[b][hf], j * per + per)
                            for a in range(hp):
                                mm = pe.matmul(ps[0:NH, b, 0:256], pts[:, b, hf * hp + a, :], values[b][:, hf, a, :], start=False, stop=(hf == 1 and a == hp - 1))
                            mm.then_inc(vused, 1)
                pe.wait_ge(o_kept, NS + 2)
                for g in range(G):
                    for s in range(NS):
                        mm = pe.transpose(ps[:, 2, (g * NS + s) * NH:(g * NS + s + 1) * NH], o[:, s, g * P:(g + 1) * P], k.ident[0:NH, 0:NH])
                mm.then_inc(o_turned, 1)

            def turned_keys(eng, copy, j, b, par, kept):
                for q in range(par, 2 * tb, 2):
                    eng.wait_ge(turned, j * (4 * tb) + (2 * tb * b + q + 2 * tb + 1))
                    copy(kt[:, b, :, q * 256:(q + 1) * 256], ps[:, 5 + par, :].rearrange("p (g q) -> p g q", g=G)).then_inc(kept, 1)

            @block.scalar
            def _(act):
                def copy(o, i):
                    return nc.scalar.activation(o, i, ACT.Copy)

                with act.Fori(0, NS // 2) as j:
                    for b in range(2):
                        act.wait_ge(used, j * 2 + (b + 1))
                        copy(qs[:, b, :], qp[:, bass.ds(j * (4 * R) + b * 2 * R, 2 * R)]).then_inc(qcopy, 1)
                        turned_keys(act, copy, j, b, 0, kept_a)
                act.wait_ge(step, 3)
                nc.scalar.activation(p[:, 0:NK].rearrange("r (b c) -> r b c", c=512), ps[0:R, 0:kb, :], ACT.Exp, bias=st[:, 6:7], accum_out=st[:, 7:8]).then_inc(exp_done, 1)
                nc.scalar.activation(p[:, NK:NK + 1], ps[0:R, 4, 0:1], ACT.Exp, bias=st[:, 6:7]).then_inc(exp_done, 1)
                act.wait_ge(pt_mm, 1)
                copy(pt[:, 0:min(npg, 8), :], ps[:, 5, 0:min(npg, 8) * R].rearrange("p (a r) -> p a r", r=R)).then_inc(pt_kept_a, 1)
                copy(pn[:, :], ps[0:NS, 7, 0:R]).then_inc(pt_kept_a, 1)
                act.wait_ge(pt_kept_a, 2)
                act.wait_ge(pt_kept_v, 1)

                def fill_slot(j2, s):
                    act.wait_ge(vused, j2 * 2 + 2 * s)
                    copy(pts[:, s % 2, :, :], pt[:, :, bass.ds(j2 * NH + s * NH, NH)]).then_inc(slot, 1)
                    copy(pns[:, s % 2, :], pn[:, bass.ds(j2 * NH + s * NH, NH)]).then_inc(slot, 1)

                for s in range(2):
                    fill_slot(0, s)
                with act.Fori(1, NS // 2) as j:
                    for b in range(2):
                        fill_slot(j * 2, b)
                        load_half(act, values[b], j * 2 + b, 1, vname, v_arrived[b][1])

            @block.vector
            def _(dve):
                with dve.Fori(0, NS // 2) as j:
                    for b in range(2):
                        dve.wait_ge(used, j * 2 + (b + 1))
                        turned_keys(dve, dve.tensor_copy, j, b, 1, kept_v)
                dve.wait_ge(used, NS + 2)
                dve.tensor_reduce(st[:, 5:6], ps[0:R, 0:kb, :], mybir.AxisListType.XY, ALU.max).then_inc(step, 1)
                dve.wait_ge(step, 1)
                dve.tensor_tensor(st[:, 4:5], st[:, 5:6], ps[0:R, 4, 0:1], ALU.max).then_inc(step, 1)
                dve.wait_ge(step, 2)
                dve.tensor_scalar(st[:, 6:7], st[:, 4:5], -1.0, None, ALU.mult).then_inc(step, 1)
                dve.wait_ge(exp_done, 2)
                dve.tensor_tensor(st[:, 5:6], st[:, 7:8], p[:, NK:NK + 1], ALU.add).then_inc(step, 1)
                dve.wait_ge(step, 4)
                dve.reciprocal(st[:, 4:5], st[:, 5:6]).then_inc(step, 1)
                dve.wait_ge(step, 5)
                if gate is None:
                    dve.tensor_scalar(p[:, :], p[:, :], st[:, 4:5], None, ALU.mult).then_inc(step, 1)
                else:
                    dve.tensor_scalar(p[:, :], p[:, :], st[:, 4:5], k.ga_s[:, gate:gate + 1], ALU.mult, ALU.mult).then_inc(step, 1)
                dve.wait_ge(step, 6)
                dve.tensor_scalar(pd[:, :], k.const[0:R, C_BD8:C_BD8 + NS], p[:, NK:NK + 1], None, ALU.mult).then_inc(step, 1)
                dve.wait_ge(pt_mm, 1)
                if npg > 8:
                    dve.tensor_copy(pt[:, 8:16, :], ps[:, 6, :].rearrange("p (a r) -> p a r", r=R)).then_inc(pt_kept_v, 1)
                else:
                    dve.nop().then_inc(pt_kept_v, 1)
                with dve.Fori(0, NS // 2) as j:
                    for b in range(2):
                        dve.wait_ge(vused, j * 4 + (2 * b + 4))
                        dve.tensor_copy(o[:, bass.ds(j * 2 + b, 1), :].rearrange("p o c -> p (o c)"), ps[0:NH, b, 0:256]).then_inc(o_kept, 1)
                dve.wait_ge(o_turned, 1)
                for g in range(G):

                    def heads(t):
                        return t.rearrange("p (s h) -> p s h", h=NH)[:, :, g * 4:(g + 1) * 4]

                    own, to = heads(ps[:, 2, g * R:(g + 1) * R]), heads(k.oS[:, mixer, :])
                    if kind == "dsa":
                        dve.tensor_copy(to, own).then_inc(out_mm, 1)
                    else:
                        dve.tensor_tensor(to, own, to, ALU.add).then_inc(out_mm, 1)
                dve.wait_ge(out_mm, 2)


def stage_attend_prompt(k, mixer):
    nc, ps = k.nc, k.psum
    A = mixer == 0
    branches = [(KS, "slc_v_p"), (KW, "win_v_p")] if A else [(KB, "dsa_v_p")]
    NB = len(branches)
    HG = NH // G
    units = [(r, i, br) for r in range(HG) for i in range(TT) for br in range(NB)]
    U = len(units)
    UH = U // HG
    SL = 2 if A else 4
    names = ("in0", "in1", "in2", "in3", "scaled", "qk", "added", "neg", "exp", "recip", "prob", "turned", "kept", "pv", "head", "fin", "ez", "zstep",
             "cqk", "cstep", "csub", "cexp", "cprob", "cturned", "ckept", "cmask", "vc", "zrecip")
    sems = [k.sem("pa_" + n) for n in names]
    in0, in1, in2, in3, scaled, qk, added, neg, exped, recip, prob, turned, kept, pv, head, fin, ez, zstep, cqk, cstep, csub, cexp, cprob, cturned, ckept, cmask_set, vc_out, zrecip = sems
    arrived = [in0, in1, in2, in3]
    loads = 8 if A else 5
    tile0, ztile, ytile = (QA, ZA, 0) if A else (QB, ZB, NH)
    tag = "AB"[mixer]
    DP, DT, DV, ring = 1, 2, 3, 4
    ZP = 4 if A else 2
    with ExitStack() as ctx:
        hq = k.sb("pa_q" + tag, [P, SL, T], ctx=ctx)
        hz = k.sb("pa_z" + tag, [P, SL, TC], ctx=ctx)
        hk = k.sb("pa_k" + tag, [P, SL, NB, T], ctx=ctx)
        hv = k.sb("pa_v" + tag, [P, SL, NB, TT, P], ctx=ctx)
        ht = k.sb("pa_t" + tag, [P, SL, T], ctx=ctx)
        hvc = k.sb("pa_vc" + tag, [NCB // 4, 2, P], ctx=ctx)
        e = k.sb("pa_e" + tag, [P, SL, TC], ctx=ctx)
        sc = k.sb("pa_s" + tag, [P, ring, T], ctx=ctx)
        pt = k.sb("pa_pt" + tag, [P, ring, T], ctx=ctx)
        st = k.sb("pa_st" + tag, [P, ring, 4], ctx=ctx)
        lc = k.sb("pa_lc" + tag, [P, TT, 16], ctx=ctx)
        cm = k.sb("pa_cm" + tag, [P, TT, 16], ctx=ctx)
        cs = k.sb("pa_cs" + tag, [P, 4, TT], ctx=ctx)
        pc = k.sb("pa_pc" + tag, [16, T], ctx=ctx)
        yo = k.sb("pa_yo" + tag, [P, 2, TC], ctx=ctx)
        with nc.Block() as block:

            @block.sync
            def _(sp):
                if A:
                    for g in range(G):
                        sp.dma_start(k.vcmp_rows[g], k.vcmp[g * NCB:g * NCB + 16, 0, :]).then_inc(vc_out, 16)
                    sp.wait_ge(vc_out, 32)
                with sp.Fori(0, G) as g:
                    for r in range(HG):
                        b = r % SL
                        sp.wait_ge(fin, g * HG + (r + 1))

                        def load(dst, src):
                            sp.dma_start(dst, src).then_inc(arrived[b], 16)

                        load(hq[:, b, :], k.proj[bass.ds(g * HG + (tile0 + r), 1), :, 0:T].rearrange("o p c -> (o p) c"))
                        load(hz[:, b, :], k.proj[bass.ds(g * HG + (ztile + r), 1)].rearrange("o p c -> (o p) c"))
                        load(ht[:, b, :], bass.AP(k.bias_skew.tensor, g * (HG * P * (BREV + 1)) + ((mixer * NH + r) * P * (BREV + 1) + P - 1), [[BREV, P], [1, T]]))
                        for br, (kt, v) in enumerate(branches):
                            load(hk[:, b, br, :], k.proj[bass.ds(g + kt, 1), :, 0:T].rearrange("o p c -> (o p) c"))
                            load(hv[:, b, br], k.o[v][0, 0, :, bass.ds(g, 1)].rearrange("(i p) o d -> p i (o d)", p=P))
                        if A:
                            load(hvc[:, b, :], k.vcmp_rows[bass.ds(g, 1)].rearrange("o n d -> (o n) d"))

            @block.tensor
            def _(pe):
                pe.sem_inc(added, 2)
                pe.sem_inc(kept, 2)
                pe.sem_inc(fin, SL)
                if A:
                    pe.sem_inc(csub, 1)
                    pe.sem_inc(ckept, 1)
                with pe.Fori(0, G) as g:
                    for t in range(U + DV):
                        if t < U:
                            r, i, br = units[t]
                            if t % UH == 0:
                                pe.wait_ge(scaled, g * HG + (r + 1))
                                if A:
                                    pe.wait_ge(csub, g * HG + (r + 1))
                                    for ii in range(TT):
                                        mm = pe.matmul(ps[:, 6, ii * 16:(ii + 1) * 16], hq[:, r % SL, ii * P:(ii + 1) * P], k.kcmp[:, 0, bass.ds(g * NCB, 16)], start=True, stop=True)
                                    mm.then_inc(cqk, 1)
                            pe.wait_ge(added, g * U + (t + 1))
                            pe.matmul(ps[:, t % 2, 0:P * (i + 1)], hq[:, r % SL, i * P:(i + 1) * P], hk[:, r % SL, br, 0:P * (i + 1)], start=True, stop=True).then_inc(qk, 1)
                        if DT <= t < U + DT:
                            v = t - DT
                            r, i, br = units[v]
                            if A and v % UH == 0:
                                pe.wait_ge(cprob, g * HG + (r + 1))
                                pe.wait_ge(ckept, g * HG + (r + 1))
                                for ii in range(TT):
                                    mm = pe.transpose(ps[0:16, 7, ii * P:(ii + 1) * P], lc[:, ii, :], k.ident)
                                mm.then_inc(cturned, 1)
                            pe.wait_ge(prob, g * U + (v + 1))
                            pe.wait_ge(kept, g * U + (v + 1))
                            for c in range(i + 1):
                                mm = pe.transpose(ps[:, 2 + v % 2, c * P:(c + 1) * P], sc[:, v % ring, c * P:(c + 1) * P], k.ident)
                            mm.then_inc(turned, 1)
                        if t >= DV:
                            v = t - DV
                            r, i, br = units[v]
                            o = 4 + r % 2
                            if v % UH == 0:
                                pe.wait_ge(fin, g * HG + (r + SL - 1))
                                if A:
                                    pe.wait_ge(ckept, g * HG + (r + 2))
                                    pe.matmul(ps[:, o, :], hvc[:, r % SL, :], pc[:, :], start=True, stop=True)
                            pe.wait_ge(kept, g * U + (v + 3))
                            for c in range(i + 1):
                                mm = pe.matmul(ps[:, o, i * P:(i + 1) * P], hv[:, r % SL, br, c, :], pt[:, v % ring, c * P:(c + 1) * P],
                                               start=(not A and v % UH == 0 and c == 0), stop=True, skip_group_check=True)
                            mm.then_inc(pv, 1)

            @block.scalar
            def _(act):

                def scale_q(g, r):
                    act.wait_ge(arrived[r % SL], g * (HG // SL * 16 * loads) + 16 * loads * (r // SL + 1))
                    nc.scalar.activation(hq[:, r % SL, :], hq[:, r % SL, :], ACT.Copy, scale=SCALE).then_inc(scaled, 1)

                def exp_z(r):
                    nc.scalar.activation(e[:, r % SL, :], hz[:, r % SL, :], ACT.Exp, scale=-1.0).then_inc(ez, 1)

                with act.Fori(0, G) as g:
                    scale_q(g, 0)
                    exp_z(0)
                    for t in range(U + DT):
                        if t < U:
                            r, i, br = units[t]
                            if t % UH == UH - 2 and r + 1 < HG:
                                act.wait_ge(fin, g * HG + (r + 2))
                                scale_q(g, r + 1)
                            if t % UH == (UH - 1 if A else UH - 2) and r + 1 < HG:
                                exp_z(r + 1)
                            act.wait_ge(neg, g * U + (t + 1))
                            n = P * (i + 1)
                            nc.scalar.activation(sc[:, t % ring, 0:n], sc[:, t % ring, 0:n], ACT.Exp, bias=st[:, t % ring, 1:2], accum_out=st[:, t % ring, 2:3]).then_inc(exped, 1)
                            if A and t % UH == 0:
                                act.wait_ge(csub, g * HG + (r + 2))
                                nc.scalar.activation(lc[:, :, :], lc[:, :, :], ACT.Exp).then_inc(cexp, 1)
                        if t >= DT:
                            v = t - DT
                            r, i, br = units[v]
                            if A and v % UH == 0:
                                act.wait_ge(cturned, g * HG + (r + 1))
                                nc.scalar.activation(pc[:, :], ps[0:16, 7, :], ACT.Copy).then_inc(ckept, 1)
                            act.wait_ge(turned, g * U + (v + 1))
                            if v >= ring:
                                act.wait_ge(pv, g * U + (v - ring + 1))
                            nc.scalar.activation(pt[:, v % ring, 0:P * (i + 1)], ps[:, 2 + v % 2, 0:P * (i + 1)], ACT.Copy).then_inc(kept, 1)

            @block.vector
            def _(dve):

                def logits(g, t):
                    r, i, br = units[t]
                    n = P * (i + 1)
                    s = sc[:, t % ring, 0:n]
                    dve.wait_ge(qk, g * U + (t + 1))
                    if t >= ring:
                        dve.wait_ge(turned, g * U + (t - ring + 1))
                    bias = ht[:, r % SL, T - n:T]
                    if A:
                        settle(k, dve)
                        dve.tensor_tensor_reduce(s, ps[:, t % 2, 0:n], bias, 1.0, TAKEN, ALU.add, ALU.max, st[:, t % ring, 0:1]).then_inc(added, 1)
                        dve.wait_ge(added, g * U + (t + 3))
                    else:
                        dve.tensor_tensor(s, ps[:, t % 2, 0:n], bias, ALU.add).then_inc(added, 1)
                        dve.wait_ge(added, g * U + (t + 3))
                        settle(k, dve)
                        dve.tensor_tensor_reduce(s, s, k.mask[:, off(i):off(i + 1)], 1.0, TAKEN, ALU.add, ALU.max, st[:, t % ring, 0:1]).then_inc(cstep, 1)
                        dve.wait_ge(cstep, g * U + (t + 1))
                    dve.tensor_scalar(st[:, t % ring, 1:2], st[:, t % ring, 0:1], -1.0, None, ALU.mult).then_inc(neg, 1)

                def probabilities(g, t):
                    r, i, br = units[t]
                    s = sc[:, t % ring, 0:P * (i + 1)]
                    dve.wait_ge(exped, g * U + (t + 1))
                    dve.reciprocal(st[:, t % ring, 3:4], st[:, t % ring, 2:3]).then_inc(recip, 1)
                    dve.wait_ge(recip, g * U + (t + 1))
                    if A:
                        gate = k.gw[:, i, bass.ds(g * (3 * HG) + (3 * r + 1 + br), 1)]
                        dve.tensor_scalar(s, s, st[:, t % ring, 3:4], gate, ALU.mult, ALU.mult).then_inc(prob, 1)
                    else:
                        dve.tensor_scalar(s, s, st[:, t % ring, 3:4], None, ALU.mult).then_inc(prob, 1)

                def recip_z(g, r, q):
                    if q == 0:
                        dve.wait_ge(zstep, g * (2 * HG) + (2 * r + 1))
                    part = e[:, r % SL, q * (TC // ZP):(q + 1) * (TC // ZP)]
                    dve.reciprocal(part, part).then_inc(zrecip, 1)

                CS = 11

                def compressed_logits(g, r):
                    at = g * (HG * CS) + r * CS
                    dve.wait_ge(cqk, g * HG + (r + 1))
                    dve.wait_ge(cstep, at + 1)
                    dve.memset(lc[:, :, :], NEG).then_inc(cstep, 1)
                    dve.wait_ge(cstep, at + 2)
                    for i in range(TT):
                        n = 4 * (i + 1)
                        u0 = T - P * (i + 1) + CB - 1
                        dve.tensor_tensor(lc[:, i, 0:n], ps[:, 6, i * 16:i * 16 + n], ht[:, r % SL, u0:u0 + CB * (n - 1) + 1:CB], ALU.add).then_inc(cstep, 1)
                    dve.wait_ge(cstep, at + 6)
                    dve.reduce_max(cs[:, 0, :], lc[:, :, :], AX).then_inc(cstep, 1)
                    dve.wait_ge(cstep, at + 7)
                    dve.tensor_tensor(lc[:, :, :], lc[:, :, :], cs[:, 0, :].unsqueeze(2).broadcast_to([P, TT, 16]), ALU.subtract).then_inc(csub, 1)

                def compressed_probabilities(g, r):
                    at = g * (HG * CS) + r * CS
                    dve.wait_ge(cexp, g * HG + (r + 1))
                    dve.tensor_tensor(lc[:, :, :], lc[:, :, :], cm[:, :, :], ALU.mult).then_inc(cstep, 1)
                    dve.wait_ge(cstep, at + 8)
                    dve.tensor_reduce(cs[:, 1, :], lc[:, :, :], AX, ALU.add).then_inc(cstep, 1)
                    dve.wait_ge(cstep, at + 9)
                    dve.tensor_scalar(cs[:, 2, :], cs[:, 1, :], 1e-30, None, ALU.max).then_inc(cstep, 1)
                    dve.wait_ge(cstep, at + 10)
                    dve.reciprocal(cs[:, 1, :], cs[:, 2, :]).then_inc(cstep, 1)
                    dve.wait_ge(cstep, at + 11)
                    dve.tensor_tensor(cs[:, 3, :], cs[:, 1, :], k.gw[:, :, bass.ds(g * (3 * HG) + 3 * r, 1)].rearrange("p i o -> p (i o)"), ALU.mult).then_inc(cstep, 1)
                    dve.wait_ge(cstep, at + 12)
                    dve.tensor_tensor(lc[:, :, :], lc[:, :, :], cs[:, 3, :].unsqueeze(2).broadcast_to([P, TT, 16]), ALU.mult).then_inc(cprob, 1)

                def finish(g, r):
                    h = g * HG + r
                    dve.wait_ge(pv, g * U + UH * (r + 1))
                    dve.wait_ge(zstep, g * (2 * HG) + (2 * r + 2))
                    dve.wait_ge(k.y_out[r % 2], g * (16 * HG // 2) + 16 * (ytile // 2 + r // 2))
                    y = yo[:, r % 2, :]
                    dve.tensor_tensor(y[:, 0:T], ps[:, 4 + r % 2, :], e[:, r % SL, 0:T], ALU.mult)
                    o = k.oS[:, mixer, :].rearrange("p (s h) -> p h s", h=NH)[:, bass.ds(h, 1), :].rearrange("p o s -> p (o s)")
                    dve.tensor_tensor(y[:, T:TC], o, e[:, r % SL, T:TC], ALU.mult).then_inc(fin, 1)

                if A:
                    dve.wait_ge(cmask_set, 2)
                    dve.nop().then_inc(cstep, 1)
                with dve.Fori(0, G) as g:
                    for t in range(U + DV + 1):
                        if t < U:
                            r = units[t][0]
                            logits(g, t)
                            if t % UH == 0:
                                if A:
                                    if r:
                                        dve.wait_ge(cturned, g * HG + r)
                                    compressed_logits(g, r)
                        if DP <= t < U + DP:
                            v = t - DP
                            if A and v % UH == 0:
                                compressed_probabilities(g, units[v][0])
                            probabilities(g, v)
                        v = t - (2 if A else 1)
                        if 0 <= v < U and v % UH < ZP:
                            recip_z(g, units[v][0], v % UH)
                        if t >= UH + DV and (t - DV) % UH == 0:
                            finish(g, (t - DV) // UH - 1)
                dve.wait_ge(fin, NH + SL)

            @block.gpsimd
            def _(pool):
                if A:
                    pool.memset(cm[:, :, :], 1.0).then_inc(cmask_set, 1)
                    pool.wait_ge(cmask_set, 1)
                    pool.affine_select(out=cm[:, :, :], in_=cm[:, :, :], compare_op=ALU.is_ge, fill=0.0, base=-(CB - 1), pattern=[[P, TT], [-CB, 16]], channel_multiplier=1).then_inc(cmask_set, 1)
                def store(g, r):
                    pool.wait_ge(fin, g * HG + (r + 1 + SL))
                    pool.dma_start(k.y_rows[bass.ds(g * HG + (ytile + r), 1)].rearrange("o p c -> (o p) c"), yo[:, r % 2, :]).then_inc(k.y_out[r % 2], 16)

                with pool.Fori(0, G) as g:
                    for r in range(HG):
                        z = e[:, r % SL, :]
                        pool.wait_ge(ez, g * HG + (r + 1))
                        settle(k, pool)
                        pool.tensor_scalar(z, z, 1.0, None, ALU.add).then_inc(zstep, 1)
                        pool.wait_ge(zrecip, g * (ZP * HG) + ZP * (r + 1))
                        pool.tensor_tensor(z, hz[:, r % SL, :], z, ALU.mult).then_inc(zstep, 1)
                        if r:
                            store(g, r - 1)
                    store(g, HG - 1)
                for b in range(2):
                    pool.wait_ge(k.y_out[b], 16 * (ytile + NH) // 2)


def stage_out(k, layer):
    nc, ps = k.nc, k.psum
    w_out = k.i["w_out_att" if layer == 0 else "w_out_conv"]
    freed, step, fin, y_high, y_low = (k.sem("ou_" + n) for n in ("freed", "step", "fin", "y_high", "y_low"))
    Y = 8
    y_in = [k.sem(f"ou_y_in{b}") for b in range(Y)]
    r = k.ring
    sp_ = Split(k)
    with ExitStack() as ctx:
        t = k.sb(f"ou_t{layer}", [P, 2, NS], ctx=ctx)
        y = k.sb(f"ou_y{layer}", [P, Y, TC], ctx=ctx)
        with nc.Block() as block:

            @block.sync
            def _(sp):

                load_weights(k, sp, r, w_out[0, :, 0:P])
                for kt in range(KT):
                    if kt >= Y:
                        sp.wait_ge(y_low, kt - Y + 1)
                    sp.dma_start(y[:, kt % Y, :], k.y_rows[kt]).then_inc(y_in[kt % Y], 16)
                for s in range(1, 4):
                    load_weights(k, sp, r + s, w_out[0, :, s * P:(s + 1) * P])
                with sp.Fori(1, 4) as j:
                    for s in range(4):
                        load_weights(k, sp, j * 4 + (r + s), w_out[0, :, bass.ds(j * 512 + s * P, P)], (r + s) % 4)

            @block.tensor
            def _(pe):
                pe.sem_inc(freed, 4)
                pe.sem_inc(sp_.used, 2)

                def tile(s, j4, ready=None):
                    pe.wait_ge(freed, j4 + (s + 1))
                    sp_.matmuls(pe, s, j4, 2 * (s % 4), ready)

                tile(0, 0, (y_low, 1))
                for s in range(1, 4):
                    tile(s, 0)
                with pe.Fori(1, 4) as j:
                    for s in range(4):
                        tile(s, j * 4)

            @block.scalar
            def _(act):
                sp_.hi(act, 0, 0)
                for kt in range(KT):
                    act.wait_ge(y_in[kt % Y], 16 * (kt // Y + 1))
                    nc.scalar.activation(k.hh[:, kt, :], y[:, kt % Y, :], ACT.Copy).then_inc(y_high, 1)
                with act.Fori(0, 3) as j:
                    for s in range(4):
                        sp_.hi(act, s + 1, j * 4)
                for s in range(12, 15):
                    sp_.hi(act, s + 1, 0)

            @block.vector
            def _(dve):
                sp_.lo(dve, 0, 0)
                for kt in range(KT):
                    dve.wait_ge(y_high, kt + 1)
                    dve.tensor_tensor(k.hl[:, kt, :], y[:, kt % Y, :], k.hh[:, kt, :].bitcast(F32), ALU.subtract).then_inc(y_low, 1)

                def tile(s, j4, last=False):
                    if not last:
                        sp_.lo(dve, s + 1, j4)
                    dve.wait_ge(sp_.used, j4 + (s + 3))
                    f = j4 + s
                    x = k.xT[:, bass.ds(f, 1), :].rearrange("p o c -> p (o c)")
                    ada = k.adaT[:, bass.ds(f + 2 * KT, 1), :].rearrange("p o c -> p (o c)")
                    b = 2 * (s % 4)
                    dve.tensor_tensor(t[:, s % 2, :], ps[:, b + 1, T - HC:HC], ada[:, 1:C9], ALU.mult).then_inc(step, 1)
                    dve.scalar_tensor_tensor(out=x[:, 0:HC], in0=ps[:, b, 0:HC], scalar=ada[:, 0:1], in1=x[:, 0:HC], op0=ALU.mult, op1=ALU.add)
                    dve.scalar_tensor_tensor(out=x[:, HC:T], in0=ps[:, b + 1, 0:T - HC], scalar=ada[:, 0:1], in1=x[:, HC:T], op0=ALU.mult, op1=ALU.add).then_inc(freed, 1)
                    dve.wait_ge(step, j4 + (s + 1))
                    dve.tensor_tensor(x[:, T:TC], t[:, s % 2, :], x[:, T:TC], ALU.add).then_inc(fin, 1)

                with dve.Fori(0, 3) as j:
                    for s in range(4):
                        tile(s, j * 4)
                for s in range(12, 16):
                    tile(s, 0, last=(s == 15))
                dve.wait_ge(fin, KT)
                dve.wait_ge(freed, KT + 4)
    k.ring += 16


def stage_conv(k):
    nc, ps = k.nc, k.psum
    state_in, turned, st_kept, zeroed, cu_turned, cu_kept, out = (k.sem("cv_" + n) for n in ("state_in", "turned", "st_kept", "zeroed", "cu_turned", "cu_kept", "out"))
    freed = [k.sem(f"cv_freed{s}") for s in range(4)]
    step, ydone, zstep = k.sem("cv_step"), k.sem("cv_y"), k.sem("cv_zstep")
    zrecip = k.sem("cv_zrecip")
    r = k.ring
    sp_ = Split(k)
    CW = 96 + 48
    CBI = 96 + 96
    with ExitStack() as ctx:
        sn = k.sb("cv_sn", [2 * NS, D], ctx=ctx)
        stT = k.sb("cv_st", [P, KT, 2 * NS], ctx=ctx)
        parts = k.sb("cv_parts", [P, 4, TC], ctx=ctx)
        hh, bg, z, e = (parts[:, b, :] for b in range(4))
        norm = Norm(k, 1, ctx, parts)
        u = k.sb("cv_u", [P, 2 + TC], ctx=ctx)
        y = k.sb("cv_yb", [P, TC], ctx=ctx)
        yo = k.sb("cv_yo", [P, TC], ctx=ctx)
        cu = k.sb("cv_cu", [P, KT, 2 + NS], ctx=ctx)
        rows = sn[0:2 + NS, :]
        with nc.Block() as block:

            @block.sync
            def _(sp):
                with sp.Fori(0, KT) as j:
                    for s in range(4):
                        load_weights(k, sp, j * 4 + (r + s), k.i["w_in_conv"][0, :, bass.ds(j * P + s * D, P)], (r + s) % 4)
                sp.wait_ge(cu_kept, 1)
                sp.dma_start(k.o["conv_p"][0, 0], rows[0:2, :]).then_inc(out, 16)
                sp.dma_start(k.o["conv_s"][0, :, 1], rows[2:2 + NS, :]).then_inc(out, 16)
                sp.wait_ge(out, 48)

            @block.gpsimd
            def _(pool):
                pool.memset(u[:, 0:2], 0.0).then_inc(zeroed, 1)
                pool.wait_ge(zeroed, 1)
                with pool.Fori(0, KT) as j:
                    pool.wait_ge(ydone, j + 2)
                    pool.dma_start(k.y_rows[bass.ds(j, 1)].rearrange("o p c -> (o p) c"), yo[:, :]).then_inc(k.y_out[0], 16)
                pool.wait_ge(k.y_out[0], 16 * (NH + KT))

            @block.tensor
            def _(pe):
                for s in range(4):
                    pe.sem_inc(freed[s], 1)
                pe.sem_inc(sp_.used, 2)
                norm.sums(pe)
                pe.wait_ge(state_in, 16)
                for kt in range(KT):
                    mm = pe.transpose(ps[:, 4, kt * 16:(kt + 1) * 16], sn[:, kt * P:(kt + 1) * P], k.ident[0:16, 0:16])
                mm.then_inc(turned, 1)
                pe.wait_ge(st_kept, 1)
                for s in range(4):
                    pe.wait_ge(freed[s], 1)
                    sp_.matmuls(pe, s, 0, 2 * s, (norm.fin, 2) if s == 0 else None)
                with pe.Fori(1, KT) as j:
                    for s in range(4):
                        pe.wait_ge(freed[s], j + 1)
                        sp_.matmuls(pe, s, j * 4, 2 * s)
                pe.wait_ge(ydone, KT + 1)
                for s in range(4):
                    pe.wait_ge(freed[s], KT + 1)
                for kt in range(KT):
                    mm = pe.transpose(ps[0:2 + NS, kt // 4, (kt % 4) * P:(kt % 4 + 1) * P], cu[:, kt, :], k.ident)
                mm.then_inc(cu_turned, 1)

            def halves(s):
                return ps[:, 2 * s:2 * s + 2, 0:HC]

            def two(t):
                return t.rearrange("p (a c) -> p a c", c=HC)

            @block.scalar
            def _(act):
                act.dma_start(sn[:, :], k.i["state_conv"][0].rearrange("s w d -> (s w) d")).then_inc(state_in, 16)
                act.dma_start(k.o["conv_s"][0, :, 0], k.i["state_conv"][0, :, 1]).then_inc(out, 16)
                norm.squares(act)
                act.wait_ge(turned, 1)
                nc.scalar.activation(stT[:, :, :], ps[:, 4, 0:KT * 16].rearrange("p (k w) -> p k w", w=16), ACT.Copy).then_inc(st_kept, 1)
                def channels(j, last=False):
                    sp_.hi(act, 1, j * 4)
                    act.wait_ge(ydone, j + 1)
                    act.wait_ge(sp_.used, j * 4 + 3)
                    nc.scalar.activation(two(hh[:, :]), halves(0), ACT.Copy).then_inc(freed[0], 1)
                    sp_.hi(act, 2, j * 4)
                    act.wait_ge(sp_.used, j * 4 + 4)
                    nc.scalar.activation(two(bg[:, :]), halves(1), ACT.Copy).then_inc(freed[1], 1)
                    sp_.hi(act, 3, j * 4)
                    if not last:
                        sp_.hi(act, 4, j * 4)
                    act.wait_ge(sp_.used, j * 4 + 6)
                    nc.scalar.activation(two(z[:, :]), halves(3), ACT.Copy)
                    nc.scalar.activation(two(e[:, :]), halves(3), ACT.Exp, scale=-1.0).then_inc(freed[3], 1)
                    act.wait_ge(freed[3], j + 2)
                    nc.scalar.activation(e[:, :], e[:, :], ACT.Copy, bias=1.0).then_inc(zstep, 1)

                sp_.hi(act, 0, 0)
                norm.high_parts(act)
                with act.Fori(0, KT - 1) as j:
                    channels(j)
                channels(KT - 1, True)

            @block.vector
            def _(dve):
                N = 8

                def channels(j, last=False, first=False):

                    def vec(col, base=0):
                        return k.vT[:, bass.ds(j + base + col, 1)]

                    def tap(w):
                        return vec(CW + w * KT)

                    for s in range(1, 4):
                        sp_.lo(dve, s, j * 4)
                    if not last:
                        sp_.lo(dve, 4, j * 4)
                    us = u[:, 2 + T:2 + TC]
                    st0 = stT[:, bass.ds(j, 1), :].rearrange("p o (s w) -> p (o s) w", w=2)
                    dve.wait_ge(freed[0], j + 2)
                    dve.wait_ge(sp_.used, j * 4 + 5)
                    dve.tensor_tensor(two(u[:, 2:2 + TC]), halves(2), two(hh[:, :]), ALU.mult).then_inc(freed[2], 1)
                    dve.wait_ge(freed[2], j + 2)
                    dve.tensor_copy(cu[:, bass.ds(j, 1), 0:2].rearrange("p o c -> p (o c)"), u[:, T:T + 2]).then_inc(step, 1)
                    dve.tensor_copy(cu[:, bass.ds(j, 1), 2:2 + NS].rearrange("p o c -> p (o c)"), us).then_inc(step, 1)
                    dve.tensor_scalar(y[:, 0:T], u[:, 0:T], tap(0), vec(CBI), ALU.mult, ALU.add).then_inc(step, 1)
                    dve.tensor_scalar(y[:, T:TC], st0[:, :, 0], tap(0), vec(CBI), ALU.mult, ALU.add).then_inc(step, 1)
                    dve.wait_ge(step, j * N + 4)
                    dve.scalar_tensor_tensor(out=y[:, 0:T], in0=u[:, 1:1 + T], scalar=tap(1), in1=y[:, 0:T], op0=ALU.mult, op1=ALU.add).then_inc(step, 1)
                    dve.scalar_tensor_tensor(out=y[:, T:TC], in0=st0[:, :, 1], scalar=tap(1), in1=y[:, T:TC], op0=ALU.mult, op1=ALU.add).then_inc(step, 1)
                    dve.wait_ge(step, j * N + 6)
                    dve.scalar_tensor_tensor(out=y[:, :], in0=u[:, 2:2 + TC], scalar=tap(2), in1=y[:, :], op0=ALU.mult, op1=ALU.add).then_inc(step, 1)
                    dve.wait_ge(step, j * N + 7)
                    dve.wait_ge(freed[1], j + 2)
                    dve.tensor_tensor(y[:, :], y[:, :], bg[:, :], ALU.mult).then_inc(step, 1)
                    dve.wait_ge(zstep, j + 1)
                    dve.reciprocal(e[:, :], e[:, :]).then_inc(zrecip, 1)
                    dve.wait_ge(zrecip, j * 2 + 1)
                    dve.tensor_tensor(e[:, :], z[:, :], e[:, :], ALU.mult).then_inc(zrecip, 1)
                    dve.wait_ge(zrecip, j * 2 + 2)
                    dve.wait_ge(step, j * N + 8)
                    if not first:
                        dve.wait_ge(k.y_out[0], j * 16 + 16 * NH)
                    dve.tensor_tensor(yo[:, :], e[:, :], y[:, :], ALU.mult).then_inc(ydone, 1)
                norm.normalise(dve, lambda dve: sp_.lo(dve, 0, 0))
                dve.wait_ge(zeroed, 1)
                dve.wait_ge(st_kept, 1)
                dve.wait_ge(norm.fin, KT + 1)
                dve.nop().then_inc(ydone, 1)
                channels(0, first=True)
                with dve.Fori(1, KT - 1) as j:
                    channels(j)
                channels(KT - 1, last=True)
                dve.wait_ge(cu_turned, 1)
                dve.tensor_copy(rows[:, :], ps[0:2 + NS, 0:4, :].rearrange("p b c -> p (b c)")).then_inc(cu_kept, 1)
    k.ring += 64


def stage_final(k):
    nc, ps = k.nc, k.psum
    turned, kept_a, kept_v, out = (k.sem("fi_" + n) for n in ("turned", "kept_a", "kept_v", "out"))
    with ExitStack() as ctx:
        rows = k.sb("fi_rows", [P, TT + 1, D], ctx=ctx)
        with nc.Block() as block:

            @block.tensor
            def _(pe):
                for i in range(TT + 1):
                    w = P if i < TT else NS
                    if i >= 2:
                        pe.wait_ge(kept_a, i - 1)
                        pe.wait_ge(kept_v, i - 1)
                    for kt in range(KT):
                        mm = pe.transpose(ps[0:w, 4 * (i % 2) + kt // 4, (kt % 4) * P:(kt % 4 + 1) * P], k.hT[:, kt, i * P:i * P + w], k.ident)
                    mm.then_inc(turned, 1)

            @block.scalar
            def _(act):
                for i in range(TT + 1):
                    w = P if i < TT else NS
                    act.wait_ge(turned, i + 1)
                    nc.scalar.activation(rows[0:w, i, 0:1024].rearrange("p (b c) -> p b c", c=512), ps[0:w, 4 * (i % 2):4 * (i % 2) + 2, :], ACT.Copy).then_inc(kept_a, 1)

            @block.vector
            def _(dve):
                for i in range(TT + 1):
                    w = P if i < TT else NS
                    dve.wait_ge(turned, i + 1)
                    dve.tensor_copy(rows[0:w, i, 1024:2048].rearrange("p (b c) -> p b c", c=512), ps[0:w, 4 * (i % 2) + 2:4 * (i % 2) + 4, :]).then_inc(kept_v, 1)

            @block.sync
            def _(sp):
                for i in range(TT + 1):
                    sp.wait_ge(kept_a, i + 1)
                    sp.wait_ge(kept_v, i + 1)
                    if i < TT:
                        sp.dma_start(k.o["y_p"][0, i * P:(i + 1) * P, :], rows[:, i, :]).then_inc(out, 16)
                    else:
                        sp.dma_start(k.o["y_s"][:, 0, :], rows[0:NS, i, :]).then_inc(out, 16)
                sp.wait_ge(out, 16 * (TT + 1))


def build(nc, ins, outs):
    with ExitStack() as ctx:
        k = Kernel(nc, ctx, ins, outs)
        k.const = k.sb("const", [P, C_ALL])
        k.ident = k.const[:, C_ID:C_ID + P]
        k.onesb = k.sb("ones", [P, P])
        k.ones = k.onesb[:, :]
        k.xT = k.sb("xT", [P, KT, TC])
        k.cT = k.sb("cT", [P, KT, C9])
        k.vT = k.sb("vT", [P, 208])
        k.adaT = k.sb("adaT", [P, 48, C9])
        k.w = k.sb("w", [P, 4, 2048])
        k.bias_skew = k.dram("bias_skew", [2 * NH * P * (BREV + 1)])
        k.vcmp_rows = k.dram("vcmp_rows", [G, 16, P])
        k.proj = k.dram("proj", [NTILES, P, TC])
        k.y_rows = k.dram("y_rows", [KT, P, TC])
        k.gate_rows = k.dram("gate_rows", [NS, NGW])
        k.w_free = k.sem("w_free")
        k.y_out = [k.sem(f"y_out{b}") for b in range(2)]
        k.w_in = [k.sem(f"w_in{s}") for s in range(4)]
        k.w1_in = {which: k.sem("w1_in_" + which) for which in "kv"}
        k.stored = [k.sem(f"pj_stored{s}") for s in range(4)]
        k.s_vectors_kept, k.s_tail_set, k.s_gated, k.s_ones, k.s_sig = (k.sem(n) for n in ("vectors_kept", "tail_set", "gated", "ones_set", "sigmoid"))
        k.settled = {e.engine: k.sem(f"settled_{n}") for n, e in (("pe", nc.tensor), ("dve", nc.vector), ("pool", nc.gpsimd))}
        k.ring = 0
        with ExitStack() as layer0:
            k.pages = k.sb("pages", [1, P], I32, ctx=layer0)
            k.table = k.sb("table", [32, 2 * NH], ctx=layer0)
            k.hot = k.sb("hot", [32, O_ALL], ctx=layer0)
            k.gw = k.sb("gw", [P, TT, NGW], ctx=layer0)
            k.gws = k.sb("gws", [NS, NGW], ctx=layer0)
            with k.stage():
                stage_load(k)
            with ExitStack() as projecting:
                k.split_buffers("0", projecting)
                with k.stage():
                    stage_ada(k, 0)
                with k.stage():
                    stage_project(k)
            with k.stage():
                stage_rows(k)
            k.sT = k.sb("sT", [P, GW, NS], ctx=layer0)
            k.qpa, k.qpb = k.sb("qpa", [P, NS * G * 64], ctx=layer0), k.sb("qpb", [P, NS * G * 64], ctx=layer0)
            k.ga_s, k.wi_s = k.sb("ga_s", [NS * NH, 3], ctx=layer0), k.sb("wi_s", [P, 1], ctx=layer0)
            k.wsel = k.sb("wsel", [P, NS], ctx=layer0)
            k.mask = k.sb("mask", [P, off(TT)], ctx=layer0)
            k.oS = k.sb("oS", [P, 2, NS * NH], ctx=layer0)
            k.kcmp, k.vcmp = k.sb("kcmp", [P, NS + 1, P], ctx=layer0), k.sb("vcmp", [P, NS + 1, P], ctx=layer0)
            with ExitStack() as sample:
                k.mask_s = k.sb("mask_s", [NS, PAST + 1], ctx=sample)
                k.hct = k.sb("hct", [P, CH], ctx=sample)
                k.msel = k.sb("msel", [NS * G, 33], ctx=sample)
                k.tabs = k.sb("tabs", [32, 2, NS * NH], ctx=sample)
                with ExitStack() as compressing:
                    k.w1 = {"k": k.w[:, :, :].rearrange("p s (l n) -> p (s l) n", n=CH), "v": k.sb("w1_v", [P, CB, CH], ctx=compressing)[:, :, :]}
                    with ExitStack() as indexing:
                        k.qpi = k.sb("qpi", [P, NS * P], ctx=indexing)
                        k.zeros = k.sb("zeros", [P, P], ctx=indexing)
                        with k.stage():
                            stage_sample_queries(k)
                        with k.stage():
                            stage_index_prompt(k)
                        with k.stage():
                            stage_index_sample(k)
                    with k.stage():
                        stage_compress(k, "k")
                    with k.stage():
                        stage_compress(k, "v")
                with k.stage():
                    stage_compressed_sample(k)
                with k.stage():
                    stage_attend_sample(k, "slc")
                with k.stage():
                    stage_attend_sample(k, "win")
                with k.stage():
                    stage_attend_sample(k, "dsa")
            with k.stage():
                stage_attend_prompt(k, 0)
            with k.stage():
                stage_attend_prompt(k, 1)
        with ExitStack() as closing:
            k.split_buffers("1", closing)
            with k.stage():
                stage_out(k, 0)
            with k.stage():
                stage_ada(k, 1)
            with k.stage():
                stage_conv(k)
            with k.stage():
                stage_out(k, 1)
        k.hT = k.sb("hT", [P, KT, TC])
        with k.stage():
            stage_final_norm(k)
        with k.stage():
            stage_final(k)


OUTS = [("y_p", (1, T, D)), ("y_s", (NS, 1, D))]
for _n in ("cmp_k", "cmp_v", "slc_k", "slc_v", "win_k", "win_v", "dsa_k", "dsa_v"):
    OUTS += [(_n + "_p", (1, 1, T, G, P)), (_n + "_s", (1, NS, WIN if _n[:3] == "win" else 1, G, P))]
OUTS += [("idx_k_p", (1, 1, T, P)), ("idx_k_s", (1, NS, 1, P)), ("conv_p", (1, 1, 2, D)), ("conv_s", (1, NS, 2, D))]


def shape_constants():
    import numpy as np
    c = np.zeros((P, C_ALL), np.float32)
    c[:, C_ID:C_ID + P] = np.eye(P)
    for row in range(NS * NH):
        c[row, C_BD8 + row // NH] = 1
        c[row, C_R16 + row // 4] = 1
        c[row // 4, C_RT + row] = 1
        c[row // NH, C_E8 + row] = 1
    for row in range(P):
        c[row, C_BD16 + row // NI] = 1

    def bucket(n):
        far = 16 + (np.log(np.maximum(n, 16).astype(np.float32) / np.float32(16)) / np.float32(4.1588830833596715) * np.float32(16)).astype(np.int32)
        return np.where(n < 16, n, np.minimum(far, 31))

    hot = np.zeros((32, O_ALL), np.float32)
    hot[bucket(T - 1 - np.arange(T)), O_P + np.arange(T)] = 1
    hot[bucket(PAST - np.arange(PAST + 1)), O_S + np.arange(PAST + 1)] = 1
    hot[bucket(PAST - (CB * np.arange(NCB) + CB - 1)), O_C + np.arange(NCB)] = 1
    return {"const": c, "hot": hot}


def kernel(**inputs):
    import numpy as _np
    import concourse.bacc as _bacc
    from concourse.bass_utils import run_bass_kernel_spmd as _run

    nc = _bacc.Bacc("TRN2", target_bir_lowering=False, num_devices=1)
    arrays, ins, outs = {}, {}, {}
    for name, a in list(inputs.items()) + list(shape_constants().items()):
        a = _np.ascontiguousarray(a)
        arrays[f"in_{name}"] = a
        ins[name] = nc.dram_tensor(f"in_{name}", a.shape, mybir.dt.from_np(a.dtype), kind="ExternalInput").ap()
    for name, shape in OUTS:
        outs[name] = nc.dram_tensor(f"out_{name}", shape, F32, kind="ExternalOutput").ap()
    build(nc, ins, outs)
    r = _run(nc, [arrays], core_ids=[0])
    return tuple(r.results[0][f"out_{name}"] for name, _ in OUTS)
```
